# Optimizing a Trainium2 kernel written in Bass

```python
import math
import jax
import jax.numpy as jnp
from jax import lax
import numpy as np

D_MODEL = 1024
BATCH = 1
SEQ = 256
DEPTH = 2

HEAD_DIM = 64
BLOCK = 128
EPS = 1e-6

DIL_PAIRS = ((128, 1), (512, 4), (2048, 16))
DIL_SLOTS = 6
A_HEADS = 18
A_WIDTH = A_HEADS * HEAD_DIM
A_OUT = DIL_SLOTS * HEAD_DIM

SSD_INNER = 2 * D_MODEL
SSD_HEADDIM = 64
SSD_HEADS = SSD_INNER // SSD_HEADDIM
SSD_GROUPS = 8
SSD_HPG = SSD_HEADS // SSD_GROUPS
SSD_STATE = 128
SSD_CONV = 4
SSD_CHUNK = 128
SSD_CONV_DIM = SSD_INNER + 2 * SSD_GROUPS * SSD_STATE

SB_HEADS = 18
SB_WIDTH = SB_HEADS * HEAD_DIM

N_BRANCHES = 3
IN_SPLITS = (A_WIDTH, A_WIDTH, A_WIDTH, SB_WIDTH, SB_WIDTH, SB_WIDTH,
             SSD_INNER, SSD_CONV_DIM, SSD_HEADS, N_BRANCHES * D_MODEL)
IN_WIDTH = 3 * A_WIDTH + 3 * SB_WIDTH + SSD_INNER + SSD_CONV_DIM + SSD_HEADS + N_BRANCHES * D_MODEL

PEER_HEADS = 8
PEER_NKEYS = 128
PEER_EXPERTS = PEER_NKEYS * PEER_NKEYS
PEER_DKEY = 128
PEER_TOPK = 16
PEER_TOKEN_BLOCK = 128

kernel_name = 'hybrid_dilated_ssd_stickbreak_peer'

def rmsnorm(x, g):
    xf = x.astype(jnp.float32)
    var = jnp.mean(xf * xf, axis=-1, keepdims=True)
    return (xf * lax.rsqrt(var + EPS)).astype(x.dtype) * g

def alibi_slopes(n):
    return jnp.exp2(-8.0 * jnp.arange(1, n + 1, dtype=jnp.float32) / n)

def dilated_window_attention(q, k, v, dilation, steps, slopes):
    b, s, h, dh = q.shape
    length = s // dilation
    nb = -(-length // BLOCK)
    pad_len = nb * BLOCK - length

    def to_blocks(t):
        t = t.reshape(b, length, dilation, h, dh).transpose(0, 2, 1, 3, 4)
        t = t.reshape(b * dilation, length, h, dh)
        t = jnp.pad(t, ((0, 0), (0, pad_len), (0, 0), (0, 0)))
        return t.reshape(b * dilation, nb, BLOCK, h, dh)

    qb, kb, vb = to_blocks(q), to_blocks(k), to_blocks(v)

    def with_previous(t):
        prev = jnp.pad(t[:, :-1], ((0, 0), (1, 0), (0, 0), (0, 0), (0, 0)))
        return jnp.concatenate([prev, t], axis=2)

    kb, vb = with_previous(kb), with_previous(vb)
    scores = jnp.einsum('znqhd,znkhd->znhqk', qb, kb).astype(jnp.float32) * (dh ** -0.5)
    qpos = BLOCK + jnp.arange(BLOCK)
    kpos = jnp.arange(2 * BLOCK)
    dist = qpos[:, None] - kpos[None, :]
    local = (dist >= 0) & (dist <= steps)
    first = (jnp.arange(nb) == 0)[:, None, None] & (kpos < BLOCK)[None, None, :]
    valid = local[None] & ~first
    bias = -slopes[:, None, None] * (dist * dilation).astype(jnp.float32)[None]
    scores = jnp.where(valid[None, :, None], scores + bias[None, None], -jnp.inf)
    m = jnp.max(scores, axis=-1, keepdims=True)
    p = jnp.exp(scores - m)
    den = jnp.sum(p, axis=-1, keepdims=True)
    out = jnp.einsum('znhqk,znkhd->znqhd', (p / den).astype(v.dtype), vb)
    lse = (m + jnp.log(den))[..., 0]
    out = out.reshape(b * dilation, nb * BLOCK, h, dh)[:, :length]
    lse = lse.transpose(0, 1, 3, 2).reshape(b * dilation, nb * BLOCK, h)[:, :length]
    out = out.reshape(b, dilation, length, h, dh).transpose(0, 2, 1, 3, 4).reshape(b, s, h, dh)
    lse = lse.reshape(b, dilation, length, h).transpose(0, 2, 1, 3).reshape(b, s, h)
    return out, lse

def dilated_mixer(q, k, v, slopes):
    b, s = q.shape[:2]
    outs, lses = [], []
    for g, (window, dilation) in enumerate(DIL_PAIRS):
        sl = slice(g * DIL_SLOTS, (g + 1) * DIL_SLOTS)
        o, l = dilated_window_attention(q[:, :, sl], k[:, :, sl], v[:, :, sl],
                                        dilation, window // dilation, slopes[sl])
        outs.append(o)
        lses.append(l)
    alpha = jax.nn.softmax(jnp.stack(lses, axis=0), axis=0)
    y = jnp.sum(alpha[..., None] * jnp.stack(outs, axis=0).astype(jnp.float32), axis=0)
    return y.astype(q.dtype).reshape(b, s, A_OUT)

def causal_depthwise_conv(x, w, bias):
    y = lax.conv_general_dilated(x, w[:, None, :], window_strides=(1,),
                                 padding=((SSD_CONV - 1, 0),),
                                 dimension_numbers=('NWC', 'WIO', 'NWC'),
                                 feature_group_count=x.shape[-1])
    return y + bias

def ssd_chunked(x, dt, a, bm, cm):
    b, s, g, hh, p = x.shape
    n = bm.shape[-1]
    c = s // SSD_CHUNK
    x = x.astype(jnp.float32).reshape(b, c, SSD_CHUNK, g, hh, p)
    dt = dt.reshape(b, c, SSD_CHUNK, g, hh)
    bm = bm.astype(jnp.float32).reshape(b, c, SSD_CHUNK, g, n)
    cm = cm.astype(jnp.float32).reshape(b, c, SSD_CHUNK, g, n)
    cum = jnp.cumsum(dt * a, axis=2)
    xdt = x * dt[..., None]
    cum_t = cum.transpose(0, 1, 3, 4, 2)
    seg = cum_t[..., :, None] - cum_t[..., None, :]
    tril = jnp.tril(jnp.ones((SSD_CHUNK, SSD_CHUNK), dtype=bool))
    decay = jnp.exp(jnp.where(tril, seg, -jnp.inf))
    cb = jnp.einsum('bctgn,bcsgn->bcgts', cm, bm)
    y_diag = jnp.einsum('bcghts,bcsghp->bctghp', cb[:, :, :, None] * decay, xdt)
    decay_states = jnp.exp(cum[:, :, -1:] - cum)
    states = jnp.einsum('bclgn,bclgh,bclghp->bcghpn', bm, decay_states, xdt)
    chunk_decay = jnp.exp(cum[:, :, -1])

    def step(h_state, inp):
        st, dec = inp
        return h_state * dec[..., None, None] + st, h_state

    h0 = jnp.zeros((b, g, hh, p, n), jnp.float32)
    _, prev = lax.scan(step, h0, (states.transpose(1, 0, 2, 3, 4, 5),
                                  chunk_decay.transpose(1, 0, 2, 3)))
    prev = prev.transpose(1, 0, 2, 3, 4, 5)
    y_off = jnp.einsum('bctgn,bcghpn,bctgh->bctghp', cm, prev, jnp.exp(cum))
    return (y_diag + y_off).reshape(b, s, g, hh, p)

def ssd_mixer(z, xbc, dt_raw, conv_w, conv_b, dt_bias, a_log, d_skip, norm_g):
    b, s = z.shape[:2]
    xbc = jax.nn.silu(causal_depthwise_conv(xbc, conv_w, conv_b))
    xs = xbc[..., :SSD_INNER].reshape(b, s, SSD_GROUPS, SSD_HPG, SSD_HEADDIM)
    bm = xbc[..., SSD_INNER:SSD_INNER + SSD_GROUPS * SSD_STATE].reshape(b, s, SSD_GROUPS, SSD_STATE)
    cm = xbc[..., SSD_INNER + SSD_GROUPS * SSD_STATE:].reshape(b, s, SSD_GROUPS, SSD_STATE)
    dt = jax.nn.softplus(dt_raw.astype(jnp.float32) + dt_bias.astype(jnp.float32))
    dt = dt.reshape(b, s, SSD_GROUPS, SSD_HPG)
    a = -jnp.exp(a_log.astype(jnp.float32)).reshape(SSD_GROUPS, SSD_HPG)
    y = ssd_chunked(xs, dt, a, bm, cm)
    y = y + d_skip.astype(jnp.float32).reshape(SSD_GROUPS, SSD_HPG)[:, :, None] * xs.astype(jnp.float32)
    y = y.astype(z.dtype).reshape(b, s, SSD_INNER)
    return rmsnorm(y * jax.nn.silu(z), norm_g)

def stick_breaking_attention(q, k, v):
    b, s, h, dh = q.shape
    scale = dh ** -0.5
    outs = []
    for i in range(s // BLOCK):
        kv_len = (i + 1) * BLOCK
        z = jnp.einsum('bqhd,bkhd->bhqk', q[:, i * BLOCK:kv_len], k[:, :kv_len]).astype(jnp.float32) * scale
        tpos = i * BLOCK + jnp.arange(BLOCK)
        causal = jnp.arange(kv_len)[None, :] < tpos[:, None]
        log_beta = jax.nn.log_sigmoid(z)
        log_keep = jnp.where(causal, jax.nn.log_sigmoid(-z), 0.0)
        between = lax.cumsum(log_keep, axis=3, reverse=True) - log_keep
        w = jnp.where(causal, jnp.exp(log_beta + between), 0.0)
        outs.append(jnp.einsum('bhqk,bkhd->bqhd', w.astype(v.dtype), v[:, :kv_len]))
    return jnp.concatenate(outs, axis=1)

def peer_ffn(h, w_query, sub_keys, expert_down, expert_up):
    b, s, d = h.shape
    t = b * s
    hf = h.reshape(t, d)
    q = (hf @ w_query).reshape(t, PEER_HEADS, 2, PEER_DKEY)
    scores = jnp.einsum('thcd,hckd->thck', q, sub_keys).astype(jnp.float32)
    top_s, top_i = lax.top_k(scores, PEER_TOPK)
    cand_s = (top_s[:, :, 0, :, None] + top_s[:, :, 1, None, :]).reshape(t, PEER_HEADS, PEER_TOPK * PEER_TOPK)
    cand_i = (top_i[:, :, 0, :, None] * PEER_NKEYS + top_i[:, :, 1, None, :]).reshape(t, PEER_HEADS, PEER_TOPK * PEER_TOPK)
    best_s, best_pos = lax.top_k(cand_s, PEER_TOPK)
    expert_idx = jnp.take_along_axis(cand_i, best_pos, axis=-1)
    gates = jax.nn.softmax(best_s, axis=-1).astype(h.dtype)
    nblk = t // PEER_TOKEN_BLOCK

    def block_fn(args):
        hb, idx, g = args
        act = jnp.einsum('td,thkd->thk', hb, expert_down[idx])
        return jnp.einsum('thk,thkd->td', g * jax.nn.gelu(act, approximate=False), expert_up[idx])

    y = lax.map(block_fn, (hf.reshape(nblk, PEER_TOKEN_BLOCK, d),
                           expert_idx.reshape(nblk, PEER_TOKEN_BLOCK, PEER_HEADS, PEER_TOPK),
                           gates.reshape(nblk, PEER_TOKEN_BLOCK, PEER_HEADS, PEER_TOPK)))
    return y.reshape(b, s, d)

def setup_inputs(seed: int = 0) -> dict:
    key = jax.random.key(seed)
    ks = jax.random.split(key, 20)

    def nrm(k, shape, scale):
        return jax.random.normal(k, shape, jnp.float32) * scale

    dt0 = jnp.exp(jax.random.uniform(ks[5], (DEPTH, SSD_HEADS), jnp.float32)
                  * (math.log(0.1) - math.log(0.001)) + math.log(0.001))
    return {
        'x': nrm(ks[0], (BATCH, SEQ, D_MODEL), 1.0),
        'norm_mix_g': 1.0 + nrm(ks[1], (DEPTH, D_MODEL), 0.02),
        'w_in': nrm(ks[2], (DEPTH, D_MODEL, IN_WIDTH), D_MODEL ** -0.5),
        'conv_w': nrm(ks[3], (DEPTH, SSD_CONV, SSD_CONV_DIM), SSD_CONV ** -0.5),
        'conv_b': nrm(ks[4], (DEPTH, SSD_CONV_DIM), 0.02),
        'dt_bias': dt0 + jnp.log(-jnp.expm1(-dt0)),
        'a_log': jnp.log(jax.random.uniform(ks[6], (DEPTH, SSD_HEADS), jnp.float32, 1.0, 16.0)),
        'd_skip': 1.0 + nrm(ks[7], (DEPTH, SSD_HEADS), 0.02),
        'ssd_norm_g': 1.0 + nrm(ks[8], (DEPTH, SSD_INNER), 0.02),
        'w_branch_a': nrm(ks[9], (DEPTH, A_OUT, D_MODEL), A_OUT ** -0.5),
        'w_branch_b': nrm(ks[10], (DEPTH, SSD_INNER, D_MODEL), SSD_INNER ** -0.5),
        'w_branch_c': nrm(ks[11], (DEPTH, SB_WIDTH, D_MODEL), SB_WIDTH ** -0.5),
        'w_out': nrm(ks[12], (DEPTH, D_MODEL, D_MODEL), D_MODEL ** -0.5),
        'norm_ffn_g': 1.0 + nrm(ks[13], (DEPTH, D_MODEL), 0.02),
        'peer_w_query': nrm(ks[14], (DEPTH, D_MODEL, PEER_HEADS * 2 * PEER_DKEY), D_MODEL ** -0.5),
        'peer_sub_keys': nrm(ks[15], (DEPTH, PEER_HEADS, 2, PEER_NKEYS, PEER_DKEY), PEER_DKEY ** -0.5),
        'peer_down': nrm(ks[16], (DEPTH, PEER_EXPERTS, D_MODEL), D_MODEL ** -0.5),
        'peer_up': nrm(ks[17], (DEPTH, PEER_EXPERTS, D_MODEL), PEER_HEADS ** -0.5),
        'final_norm_g': 1.0 + nrm(ks[18], (D_MODEL,), 0.02),
    }

def reference(x, norm_mix_g, w_in, conv_w, conv_b, dt_bias, a_log, d_skip, ssd_norm_g,
              w_branch_a, w_branch_b, w_branch_c, w_out, norm_ffn_g,
              peer_w_query, peer_sub_keys, peer_down, peer_up, final_norm_g):
    b, s, d = x.shape
    slopes = alibi_slopes(A_HEADS)
    offsets = []
    acc = 0
    for w in IN_SPLITS[:-1]:
        acc += w
        offsets.append(acc)
    for l in range(DEPTH):
        h = rmsnorm(x, norm_mix_g[l])
        proj = h @ w_in[l]
        qa, ka, va, qc, kc, vc, z, xbc, dt_raw, gate_logits = jnp.split(proj, offsets, axis=-1)
        heads_a = lambda t: t.reshape(b, s, A_HEADS, HEAD_DIM)
        heads_c = lambda t: t.reshape(b, s, SB_HEADS, HEAD_DIM)
        y_a = dilated_mixer(heads_a(qa), heads_a(ka), heads_a(va), slopes)
        y_b = ssd_mixer(z, xbc, dt_raw, conv_w[l], conv_b[l], dt_bias[l], a_log[l],
                        d_skip[l], ssd_norm_g[l])
        y_c = stick_breaking_attention(heads_c(qc), heads_c(kc), heads_c(vc)).reshape(b, s, SB_WIDTH)
        gates = jax.nn.sigmoid(gate_logits.astype(jnp.float32)).astype(x.dtype).reshape(b, s, N_BRANCHES, d)
        merged = (gates[:, :, 0] * (y_a @ w_branch_a[l])
                  + gates[:, :, 1] * (y_b @ w_branch_b[l])
                  + gates[:, :, 2] * (y_c @ w_branch_c[l]))
        x = x + merged @ w_out[l]
        h = rmsnorm(x, norm_ffn_g[l])
        x = x + peer_ffn(h, peer_w_query[l], peer_sub_keys[l], peer_down[l], peer_up[l])
    return rmsnorm(x, final_norm_g)


_drawn_inputs = setup_inputs


def setup_inputs(seed=0):
    import zlib

    import numpy as np

    out = dict(_drawn_inputs(seed))
    spreads = {}
    factors = {}
    for name, (base, spread) in spreads.items():
        noise = np.random.default_rng([zlib.crc32(name.encode()), seed]).standard_normal(out[name].shape)
        drawn = base * np.exp(spread * noise) if base else spread * noise
        out[name] = jnp.asarray(drawn.astype(out[name].dtype))
    for name, factor in factors.items():
        out[name] = (out[name] * factor).astype(out[name].dtype)
    return out
```

```python
from contextlib import ExitStack

import numpy as np
import concourse.bass as bass
from concourse import mybir

F32 = mybir.dt.float32
F32R = mybir.dt.float32r
BF16 = mybir.dt.bfloat16
U32 = mybir.dt.uint32
ALU = mybir.AluOpType
ACT = mybir.ActivationFunctionType
AX = mybir.AxisListType

P = 128
LAYERS, SEQ, D = 2, 256, 1024
TT = SEQ // P
KD = D // P
HD = 64
A_HEADS, A_SLOTS, A_GROUPS = 18, 6, 3
DILATION = (1, 4, 16)
A_W, C_W, A_OUT = A_HEADS * HD, 18 * HD, A_SLOTS * HD
C_HEADS = 18
SSD_IN, GROUPS, HPG, NSTATE = 2048, 8, 4, 128
SSD_H = GROUPS * HPG
CONV = SSD_IN + 2 * GROUPS * NSTATE
KEYS, TOPK, RH = 128, 16, 8
EPS = 1e-6
NEG = -3.0e38

RING = 4
CW = 512
V_CH, QK_CH, X_CH, Z_CH, G_CH = 5, 9, 8, 4, 6
C_V, C_QK = 0, V_CH
C_X = C_QK + QK_CH
C_Z = C_X + X_CH
C_G = C_Z + Z_CH
CHUNKS = C_G + G_CH
U_C = 4 * CHUNKS
U_A = U_C + C_W // P
U_B = U_A + A_OUT // P
U_O = U_B + SSD_IN // P
U_Q = U_O + KD
U_K = U_Q + 16
U_E = U_K + 2
UNITS = U_E + 2 * KEYS
V_COLS = 2 * A_W + SSD_H


def chunk_of_stream(c):
    return 4 * c if c < CHUNKS else U_Q + 4 * (c - CHUNKS)


def slot_units(slot):
    return len(range(slot, UNITS, RING))


def make_order():
    order = {u: [] for u in range(UNITS)}
    for c in range(CHUNKS + 4):
        order[chunk_of_stream(c) + 3].append(("evacuate", c))
    order[23].append(("dt", 0))
    a0 = 4 * (C_QK + 5) + 1
    for j in range(A_SLOTS):
        order[a0 + 2 + 4 * j].append(("a_turn", j))
        order[a0 + 4 + 4 * j].append(("a_mix", j))
    for j in range(A_SLOTS):
        order[a0 + 4 * j].append(("a_score", j))
    c0 = a0 + 4 * A_SLOTS + 1
    for p in range(C_HEADS // 2):
        order[c0 + 2 + 4 * p].append(("c_sum", p))
        order[c0 + 4 + 4 * p].append(("c_mix", p))
    for p in range(C_HEADS // 2):
        order[c0 + 4 * p].append(("c_score", p))
    s0 = 4 * C_G
    assert c0 + 4 * (C_HEADS // 2) < s0
    for n in range(2 * GROUPS):
        order[s0 + 2 * n].append(("ssd", n))
    order[s0 + 4 * GROUPS].append(("ssd", 2 * GROUPS))
    for i in range(3):
        order[s0 + 1 + 2 * i].append(("split_y", i))
    order[U_A - 1].append(("merge", 0))
    order[U_B - 1].append(("merge", 1))
    order[U_A].append(("ssd_norm", 0))
    for k in range(16):
        order[U_A + 1 + k].append(("turn_b", k))
    order[U_O - 1].append(("merge", 2))
    order[U_O - 1].append(("turn_merged", 0))
    order[U_Q - 1].append(("add_x", 0))
    order[U_Q - 1].append(("norm", 1))
    order[U_K].append(("key_scores", 0))
    order[U_K + 1].append(("key_scores", 1))
    return order


ORDER = make_order()


def build_trunk(nc, x_in, stream, fm_params, row_params, mix_f32, mix_bf16, ident_in, iota_in, final_g, out):
    with ExitStack() as ctx:
        base = 16512

        def at(name, shape, offset, dtype=F32):
            return nc.alloc_sbuf_tensor_at(name, [P, *shape], dtype, offset=base + 4 * offset)

        fence = ctx.enter_context(nc.sbuf_tensor("fence", [P, 53200], F32))
        x = at("x", [TT, D], 0)
        h_hi = at("h_hi", [KD, SEQ], 2048, F32R)
        h_lo = at("h_lo", [KD, SEQ], 4096, F32R)
        raw = at("raw", [RING, 1024], 6144)
        w_hi = at("w_hi", [RING, 1024], 10240, F32R)
        w_lo = at("w_lo", [RING, 1024], 14336, F32R)
        ident = at("ident", [P], 18432)
        iota = at("iota", [P], 18560)
        fmp = at("fmp", [LAYERS, 192], 18688)
        stat = at("stat", [64], 19072)
        ar = 19136
        qk = at("qk", [36, SEQ], ar)
        gates = at("gates", [TT, 3 * D], ar)
        yt_hi = at("yt_hi", [12, SEQ], ar + 6144, F32R)
        v = at("v", [TT, V_COLS], ar + 9216)
        xt = at("xt", [32, SEQ], ar + 13888)
        z = at("z", [TT, SSD_IN], ar + 22080)
        yt = at("yt", [12, SEQ], ar + 26176)
        yt_lo = at("yt_lo", [12, SEQ], ar + 26176, F32R)
        ws = ar + 29248
        a_p = at("a_p", [A_GROUPS, 384], ws)
        a_pt = at("a_pt", [A_GROUPS, 384], ws + 1152)
        c_sp = at("c_sp", [2, 384], ws)
        c_w = at("c_w", [2, 384], ws + 768)
        merged = at("merged", [TT, D], ws)
        dts = ar + 31552
        dt = at("dt", [TT, SSD_H], dts)
        da = at("da", [TT, SSD_H], dts + 64)
        ed = at("ed", [2, SSD_H], dts + 128)
        dtd = at("dtd", [SSD_H], dts + 192)
        dtt = at("dtt", [TT, SSD_H], dts + 224)
        ea = at("ea", [SSD_H], dts + 288)
        mixc = ar + 31872
        mixf = at("mixf", [1664], mixc)
        upper = mixf[:, 0:128]
        lower = mixf[:, 128:256]
        neg_ge = mixf[:, 256:384]
        neg_one = mixf[:, 384:512]
        dist = mixf[:, 512:1664].rearrange("p (g n) -> p g n", g=A_GROUPS)
        mixb = at("mixb", [2, P], mixc + 1664, BF16)
        rows = at("rows", [96], mixc + 1792)
        sv = ar + 9216
        s_r = at("s_r", [HPG, P], sv)
        s_e = at("s_e", [2, HPG, P], sv + 512)
        s_cb = at("s_cb", [P], sv + 1536)
        s_xdt = at("s_xdt", [2, HPG, HD], sv + 1664)
        s_xdd = at("s_xdd", [HPG, HD], sv + 2176)
        s_state = at("s_state", [HPG, HD], sv + 2432)
        s_bt = at("s_bt", [P], sv + 2688)
        s_y = at("s_y", [2, HPG, HD], sv + 2816)
        mtmp = at("mtmp", [2, CW], sv + 3392)
        junk = at("junk", [SSD_IN], sv)
        m_hi = at("m_hi", [KD, SEQ], sv, F32R)
        m_lo = at("m_lo", [KD, SEQ], sv + 2048, F32R)
        yb_hi = at("yb_hi", [16, SEQ], ar + 13888, F32R)
        yb_lo = at("yb_lo", [16, SEQ], ar + 13888 + 4096, F32R)
        xn = at("xn", [TT, D], ar + 22080)
        njunk = at("njunk", [TT, D], ar + 22080 + 2048)
        q_hi = at("q_hi", [16, SEQ], ar + 13888, F32R)
        q_lo = at("q_lo", [16, SEQ], ar + 13888 + 4096, F32R)
        sc = at("sc", [TT, 16, KEYS], ar)
        tk = ar + 13888
        t_val = at("t_val", [TT, RH, 2, TOPK], tk)
        t_idx = at("t_idx", [TT, RH, 2, TOPK], tk + 512, U32)
        t_idf = at("t_idf", [TT, RH, 2, TOPK], tk + 1024)
        cand = at("cand", [RH, TOPK, TOPK], tk + 1536)
        b_val = at("b_val", [TT, RH, TOPK], tk + 3840)
        b_pos = at("b_pos", [TT, RH, TOPK], tk + 4096, U32)
        b_row = at("b_row", [2, TT, RH, TOPK], tk + 4352, U32)
        b_rof = at("b_rof", [2, TT, RH, TOPK], tk + 4864)
        eq = at("eq", [RH, TOPK, TOPK], tk + 5376)
        pick = at("pick", [3, TT, RH, TOPK], tk + 7424)
        tkt = at("tkt", [2, 256], ar + 9216)
        route = at("route", [KEYS, SEQ], ar)
        tail = ar + 32768
        pick_t = at("pick_t", [3, SEQ], tail)
        hot = at("hot", [2, 2, KEYS], tail + 768)
        g_hi = at("g_hi", [2, SEQ], tail, F32R)
        g_act = at("g_act", [2, SEQ], tail + 512)
        g_lo = at("g_lo", [2, SEQ], tail + 512, F32R)
        fing = at("fing", [D], ar + 9216)

        pp = ctx.enter_context(nc.psum_tensor("pp", [P, 4, 512], F32))
        pm = ctx.enter_context(nc.psum_tensor("pm", [P, 4, 512], F32))

        class Signal:

            def __init__(self, name, per_layer, start=0):
                self.sem = ctx.enter_context(nc.semaphore(name))
                self.per, self.start = per_layer, start

            def at(self, l, n):
                return l * self.per + (n + self.start)

        sg_raw = [Signal(f"raw_landed{s}", 16 * slot_units(s)) for s in range(RING)]
        sg_hi = Signal("high_ready", UNITS, 1)
        sg_lo = Signal("low_ready", UNITS, 1)
        sg_used = Signal("unit_used", UNITS, 1)
        sg_sq, sg_root, sg_rstd, sg_xn = (Signal(n, 2) for n in ("squares", "roots", "rstd_ready", "xn_ready"))
        sg_turn, sg_hh, sg_hl = Signal("xn_turned", 8), Signal("h_high", 16), Signal("h_low", 16)
        sg_ev, sg_cv, sg_xs, sg_ql = Signal("chunk_out", 28), Signal("conv_step", 128), Signal("conv_silu", 4), Signal("query_low", 4)
        sg_dt, sg_dta, sg_dtp = Signal("dt_vector", 4), Signal("dt_scalar", 5), Signal("dt_sums", 1)
        sg_as, sg_ab, sg_am, sg_ae, sg_ar = Signal("a_scores", 18), Signal("a_biased", 18), Signal("a_max", 6), Signal("a_exp", 6), Signal("a_scaled", 12)
        sg_at, sg_ap, sg_apv, sg_ay = Signal("a_turned", 18), Signal("a_turned_out", 18), Signal("a_mixed", 6), Signal("a_out", 6)
        sg_cz, sg_cl, sg_csp, sg_cc = Signal("c_scores", 18), Signal("c_log", 54), Signal("c_softplus", 18), Signal("c_summed", 18)
        sg_cw, sg_cpv, sg_cy = Signal("c_weights", 18), Signal("c_mixed", 9), Signal("c_out", 9)
        sg_sr, sg_s1, sg_sgm, sg_se, sg_sb = Signal("s_steps", 16), Signal("s_turned", 16), Signal("s_segments", 16), Signal("s_decay", 16), Signal("s_bt_out", 8)
        sg_sc, sg_sx, sg_sm, sg_s2, sg_st, sg_sd = Signal("s_cb_out", 16), Signal("s_inputs", 16), Signal("s_masked", 16), Signal("s_products", 16), Signal("s_state_out", 8), Signal("s_sum", 48)
        sg_yh, sg_yl = Signal("y_high", 3), Signal("y_low", 3)
        sg_bq, sg_br, sg_bt, sg_bh, sg_bl = Signal("b_squares", 3), Signal("b_rstd", 1), Signal("b_turned", 16), Signal("b_high", 16), Signal("b_low", 16)
        sg_mg, sg_mt = Signal("merged_c", 4), Signal("merge_step", 16)
        sg_mtt, sg_mh, sg_ml, sg_xa = Signal("merged_turned", 8), Signal("merged_high", 8), Signal("merged_low", 8), Signal("x_added", 2, 1)
        sg_kv = Signal("key_scores_out", 4)
        n_tk = 5 * 32 + 1 + 2 * (1 + 5 * 8) + 3 + 12 + 4
        sg_tk, sg_gx, sg_ix, sg_ixe = Signal("retrieval_step", n_tk), Signal("gate_exp", 1), Signal("picks_turned", 1), Signal("picks_out", 3)
        sg_hot, sg_rt, sg_free = Signal("one_hots", SEQ), Signal("routes", SEQ, 1), Signal("route_banks_free", SEQ // 4, 4)
        sg_ge, sg_gl = Signal("gelu", KEYS), Signal("weighted", 3 * KEYS)
        s_init = ctx.enter_context(nc.semaphore("init_landed"))
        s_apart = ctx.enter_context(nc.semaphore("apart"))
        INIT = 5 * 16
        sg_mix = Signal("mix_constants", 48)
        s_fin = ctx.enter_context(nc.semaphore("final_step"))
        s_fina = ctx.enter_context(nc.semaphore("final_scalar"))
        s_out = ctx.enter_context(nc.semaphore("out_stored"))
        s_fg = ctx.enter_context(nc.semaphore("final_g_landed"))

        def final_of(n):
            return 6 * (n // 2) + (2 if n % 2 == 0 else 6)

        def a_head(j, g):
            h = g * A_SLOTS + j
            return h // 2, HD * (h % 2), HD * h

        def down_v(j):
            return 0 if j == 0 else 2 * j - 1

        def up_v(j):
            return 2 * j + 2 if j < KEYS - 1 else 2 * KEYS - 1

        block = ctx.enter_context(nc.Block())

        @block.sync
        def _(sp):
            sp.dma_start(x[:], x_in.rearrange("(a p) d -> p a d", p=P)).then_inc(s_init, 16)
            sp.dma_start(ident[:], ident_in).then_inc(s_init, 16)
            sp.dma_start(iota[:], iota_in).then_inc(s_init, 16)
            sp.dma_start(fmp[:], fm_params.rearrange("l p n -> p l n")).then_inc(s_init, 16)
            with sp.Fori(0, LAYERS) as l:
                for s in range(RING):
                    sp.wait_ge(sg_hi.sem, sg_hi.at(l, 0))
                    sp.wait_ge(sg_lo.sem, sg_lo.at(l, 0))
                    sp.dma_start(raw[:, s, :], stream[bass.ds(l * UNITS + s, 1)].rearrange("o p n -> p (o n)")).then_inc(sg_raw[s].sem, 16)
                with sp.Fori(1, UNITS // RING) as i:
                    for s in range(RING):
                        sp.wait_ge(sg_hi.sem, sg_hi.at(l, RING * i + (s - RING + 1)))
                        sp.wait_ge(sg_lo.sem, sg_lo.at(l, RING * i + (s - RING + 1)))
                        sp.dma_start(raw[:, s, :], stream[bass.ds(l * UNITS + RING * i + s, 1)].rearrange("o p n -> p (o n)")).then_inc(sg_raw[s].sem, 16)
                for u in range(UNITS // RING * RING, UNITS):
                    sp.wait_ge(sg_hi.sem, sg_hi.at(l, u - RING + 1))
                    sp.wait_ge(sg_lo.sem, sg_lo.at(l, u - RING + 1))
                    sp.dma_start(raw[:, u % RING, :], stream[bass.ds(l * UNITS + u, 1)].rearrange("o p n -> p (o n)")).then_inc(sg_raw[u % RING].sem, 16)
            sp.wait_ge(s_fin, 4)
            sp.dma_start(out.rearrange("(a p) d -> p a d", p=P), xn[:]).then_inc(s_out, 16)
            sp.wait_ge(s_out, 16)

        @block.gpsimd
        def _(pool):
            with pool.Fori(0, LAYERS) as l:
                pool.wait_ge(sg_xa.sem, sg_xa.at(l, 0))
                pool.sem_inc(s_apart)
                pool.dma_start(mixf[:], mix_f32).then_inc(sg_mix.sem, 16)
                pool.dma_start(mixb[:], mix_bf16.rearrange("p (a n) -> p a n", a=2)).then_inc(sg_mix.sem, 16)
                pool.dma_start(rows[:], row_params[bass.ds(l, 1)].rearrange("o p n -> p (o n)")).then_inc(sg_mix.sem, 16)
            pool.wait_ge(sg_xa.sem, sg_xa.at(LAYERS, 0))
            pool.dma_start(fing[:], final_g).then_inc(s_fg, 16)

        @block.tensor
        def _(pe):
            pe.sem_inc(sg_used.sem, sg_used.start)
            pe.sem_inc(sg_rt.sem, sg_rt.start)
            pe.wait_ge(s_init, INIT)
            with pe.Fori(0, LAYERS) as l:

                def wait(sig, n):
                    pe.wait_ge(sig.sem, sig.at(l, n))

                def transpose(dst, src):
                    return pe.transpose(dst, src, ident[0:src.shape[0], 0:src.shape[0]])

                def unit_ready(u):
                    wait(sg_lo, u + 1)

                def chunk_unit_fm(c, q, rhs_hi, rhs_lo):
                    u = chunk_of_stream(c) + q
                    unit_ready(u)
                    pair = c % 2
                    for s in range(2):
                        for m in range(4):
                            dst = pp[:, 2 * pair + m // 2, SEQ * (m % 2):SEQ * (m % 2 + 1)]
                            col = slice(CW * s + P * m, CW * s + P * (m + 1))
                            wh, wl = w_hi[:, u % RING, col], w_lo[:, u % RING, col]
                            k = 2 * q + s
                            pe.matmul(dst, wh, rhs_hi[:, k, :], start=(k == 0 and m % 2 == 0), stop=False, skip_group_check=True)
                            pe.matmul(dst, wh, rhs_lo[:, k, :], start=False, stop=False, skip_group_check=True)
                            last = pe.matmul(dst, wl, rhs_hi[:, k, :], start=False, stop=(k == KD - 1), skip_group_check=True)
                    last.then_inc(sg_used.sem, 1)

                def chunk_unit_tm(c, q):
                    u = chunk_of_stream(c) + q
                    unit_ready(u)
                    pair = c % 2
                    for s in range(2):
                        k = 2 * q + s
                        col = slice(CW * s, CW * (s + 1))
                        for t in range(TT):
                            tok = slice(P * t, P * (t + 1))
                            dst = pp[:, 2 * pair + t, :]
                            pe.matmul(dst, h_hi[:, k, tok], w_hi[:, u % RING, col], start=(k == 0), stop=False)
                            pe.matmul(dst, h_hi[:, k, tok], w_lo[:, u % RING, col], start=False, stop=False)
                            last = pe.matmul(dst, h_lo[:, k, tok], w_hi[:, u % RING, col], start=False, stop=(k == KD - 1))
                    last.then_inc(sg_used.sem, 1)

                def pair_free(c):
                    if c in (0, 1):
                        return
                    if c in (CHUNKS, CHUNKS + 1):
                        return
                    b = c - 2
                    if C_X <= b < C_Z:
                        wait(sg_cv, 16 * (b - C_X + 1))
                    elif b < C_X:
                        wait(sg_ev, b + 1)
                    elif b < CHUNKS:
                        wait(sg_ev, b + 1 - X_CH)
                    else:
                        wait(sg_ql, b - CHUNKS + 1)

                def slab_unit(u, k, lhs_hi, lhs_lo, start, stop):
                    unit_ready(u)
                    for t in range(TT):
                        tok = slice(P * t, P * (t + 1))
                        for half in range(2):
                            col = slice(CW * half, CW * (half + 1))
                            dst = pp[:, 2 * t + half, :]
                            pe.matmul(dst, lhs_hi[:, k, tok], w_hi[:, u % RING, col], start=start, stop=False)
                            pe.matmul(dst, lhs_hi[:, k, tok], w_lo[:, u % RING, col], start=False, stop=False)
                            last = pe.matmul(dst, lhs_lo[:, k, tok], w_hi[:, u % RING, col], start=False, stop=stop)
                    last.then_inc(sg_used.sem, 1)

                def norm(n):
                    wait(sg_xn, n + 1)
                    for b in range(4):
                        for k in (2 * b, 2 * b + 1):
                            for t in range(TT):
                                last = transpose(pm[:, b, SEQ * (k % 2) + P * t:SEQ * (k % 2) + P * (t + 1)], xn[:, t, P * k:P * (k + 1)])
                        last.then_inc(sg_turn.sem, 1)

                def dt_sums(_n):
                    wait(sg_mix, 48)
                    wait(sg_dt, 3)
                    pe.matmul(pm[:, 3, 0:SSD_H], lower, da[:, 1, :], start=True, stop=True)
                    pe.matmul(pm[:, 3, SSD_H:2 * SSD_H], upper, da[:, 0, :], start=True, stop=True).then_inc(sg_dtp.sem, 1)

                def a_score(j):
                    wait(sg_ev, C_QK + 5)
                    for g in range(A_GROUPS):
                        if j == 0:
                            wait(sg_hl, 8)
                        else:
                            wait(sg_ap, 3 * (j - 1) + g + 1)
                        tile, part, _ = a_head(j, g)
                        row = slice(part, part + HD)
                        q, k = qk[row, tile, :], qk[row, 9 + tile, :]
                        pe.matmul(pm[:, g, 0:P], q[:, 0:P], k[:, 0:P], start=True, stop=True)
                        pe.matmul(pm[:, g, P:3 * P], q[:, P:SEQ], k[:, 0:SEQ], start=True, stop=True).then_inc(sg_as.sem, 1)

                def a_turn(j):
                    wait(sg_ar, 2 * j + 2)
                    for g in range(A_GROUPS):
                        for b in range(3):
                            last = transpose(pm[:, g, P * b:P * (b + 1)], a_p[:, g, P * b:P * (b + 1)])
                        last.then_inc(sg_at.sem, 1)

                def a_mix(j):
                    wait(sg_ap, 3 * j + 3)
                    if j == 0:
                        wait(sg_dta, 5)
                    else:
                        wait(sg_ay, j)
                    part = HD * (j % 2)
                    dst = pm[part:part + HD, 3, :]
                    for g in range(A_GROUPS):
                        _, _, col = a_head(j, g)
                        pe.matmul(dst[:, 0:SEQ], v[:, 0, col:col + HD], a_pt[:, g, 0:SEQ], start=(g == 0), stop=False)
                        last = pe.matmul(dst[:, P:SEQ], v[:, 1, col:col + HD], a_pt[:, g, SEQ:3 * P], start=False, stop=(g == A_GROUPS - 1))
                    last.then_inc(sg_apv.sem, 1)

                def c_score(p):
                    wait(sg_ev, C_X)
                    for i in range(2):
                        h = 2 * p + i
                        if p == 0:
                            wait(sg_ap, 18)
                        else:
                            wait(sg_cw, h - 1)
                        row = slice(HD * i, HD * i + HD)
                        q, k = qk[row, 18 + p, :], qk[row, 27 + p, :]
                        pe.matmul(pm[:, i, 0:SEQ], k[:, 0:P], q, start=True, stop=False, skip_group_check=True)
                        pe.matmul(pm[:, i, SEQ:3 * P], k[:, P:SEQ], q[:, P:SEQ], start=False, stop=False, skip_group_check=True)
                        pe.matmul(pm[:, i, 0:P], mixb[:, 1, :], mixb[:, 0, :], start=False, stop=False, skip_group_check=True)
                        pe.matmul(pm[:, i, SEQ:3 * P], mixb[:, 1, :], mixb[:, 0, :], start=False, stop=False, skip_group_check=True).then_inc(sg_cz.sem, 1)

                def c_sum(p):
                    for i in range(2):
                        wait(sg_csp, 2 * p + i + 1)
                        pe.matmul(pm[:, i, 0:3 * P], neg_ge, c_sp[:, i, :], start=False, stop=False, skip_group_check=True)
                        pe.matmul(pm[:, i, P:SEQ], neg_one, c_sp[:, i, SEQ:3 * P], start=False, stop=True, skip_group_check=True).then_inc(sg_cc.sem, 1)

                def c_mix(p):
                    wait(sg_cw, 2 * p + 2)
                    if p >= 1:
                        wait(sg_cy, p)
                    for i in range(2):
                        dst = pm[HD * i:HD * (i + 1), 2, :]
                        col = A_W + HD * (2 * p + i)
                        pe.matmul(dst[:, 0:SEQ], v[:, 0, col:col + HD], c_w[:, i, 0:SEQ], start=True, stop=False)
                        last = pe.matmul(dst[:, P:SEQ], v[:, 1, col:col + HD], c_w[:, i, SEQ:3 * P], start=False, stop=True)
                    last.then_inc(sg_cpv.sem, 1)

                def ssd(n):
                    if n < 2 * GROUPS:
                        g, t = n // 2, n % 2
                        tok = slice(P * t, P * (t + 1))
                        wait(sg_xs, 4)
                        if n < 2:
                            wait(sg_cw, 18)
                        else:
                            wait(sg_sx, n - 1)
                        if n >= 2 and t == 0:
                            wait(sg_sb, g)
                        b = pm[:, t, :]
                        transpose(b[:, 0:P], xt[:, 2 * g, tok])
                        transpose(b[:, P:2 * P], xt[:, 2 * g + 1, tok])
                        bm, cm = xt[:, 16 + g, tok], xt[:, 24 + g, tok]
                        last = pe.matmul(b[:, 2 * P:3 * P], bm, cm, start=True, stop=True)
                        if t == 0:
                            last = transpose(b[:, 3 * P:4 * P], bm)
                        last.then_inc(sg_s1.sem, 1)
                        wait(sg_sr, n + 1)
                        if n == 0:
                            wait(sg_cy, 9)
                        else:
                            wait(sg_se, n)
                        pe.matmul(pm[:, 2, :], upper, s_r[:].rearrange("p h t -> p (h t)"), start=True, stop=True).then_inc(sg_sgm.sem, 1)
                    if n >= 1:
                        m = n - 1
                        g, t = m // 2, m % 2
                        wait(sg_sm, m + 1)
                        wait(sg_sx, m + 1)
                        if m == 0:
                            wait(sg_ay, 6)
                        else:
                            wait(sg_sd, final_of(m - 1))
                        if g + t:
                            wait(sg_st, g + t)
                        if t == 0:
                            wait(sg_sb, g + 1)
                        for h in range(HPG):
                            pe.matmul(pm[:, 3, HD * h:HD * (h + 1)], s_e[:, t, h, :], s_xdt[:, t, h, :], start=True, stop=True)
                        if t == 0:
                            last = pe.matmul(pm[:, 3, 256:512], s_bt[:], s_xdd[:].rearrange("p h d -> p (h d)"), start=True, stop=True)
                        else:
                            last = pe.matmul(pm[:, 3, 256:512], xt[:, 24 + g, P:SEQ], s_state[:].rearrange("p h d -> p (h d)"), start=True, stop=True)
                        last.then_inc(sg_s2.sem, 1)

                def turn_b(k):
                    wait(sg_sd, 48)
                    if k >= 4:
                        wait(sg_bl, k - 3)
                    for t in range(TT):
                        last = transpose(pm[:, k % 4, P * t:P * (t + 1)], z[:, t, P * k:P * (k + 1)])
                    last.then_inc(sg_bt.sem, 1)

                def turn_merged(_n):
                    wait(sg_mt, 16)
                    wait(sg_bl, 16)
                    for k in range(KD):
                        for t in range(TT):
                            last = transpose(pm[:, k // 2, SEQ * (k % 2) + P * t:SEQ * (k % 2) + P * (t + 1)], merged[:, t, P * k:P * (k + 1)])
                        last.then_inc(sg_mtt.sem, 1)

                steps = {"norm": norm, "dt": dt_sums, "a_score": a_score, "a_turn": a_turn, "a_mix": a_mix,
                         "c_score": c_score, "c_sum": c_sum, "c_mix": c_mix, "ssd": ssd, "turn_b": turn_b,
                         "turn_merged": turn_merged}

                def between(u):
                    for name, arg in ORDER[u]:
                        if name in steps:
                            steps[name](arg)

                norm(0)
                wait(sg_hl, 8)
                for c in range(CHUNKS):
                    pair_free(c)
                    for q in range(4):
                        if C_QK <= c < C_Z:
                            chunk_unit_fm(c, q, h_hi, h_lo)
                        else:
                            chunk_unit_tm(c, q)
                        between(4 * c + q)
                wait(sg_ev, 24)
                wait(sg_yl, 3)
                for u in range(U_C, U_A):
                    k = u - U_C
                    slab_unit(u, 3 + k, yt_hi, yt_lo, k == 0, u == U_A - 1)
                    between(u)
                wait(sg_mg, 4)
                for u in range(U_A, U_B):
                    k = u - U_A
                    slab_unit(u, k, yt_hi, yt_lo, k == 0, u == U_B - 1)
                    between(u)
                wait(sg_mt, 8)
                for u in range(U_B, U_O):
                    k = u - U_B
                    wait(sg_bl, k + 1)
                    slab_unit(u, k, yb_hi, yb_lo, k == 0, u == U_O - 1)
                    between(u)
                for u in range(U_O, U_Q):
                    k = u - U_O
                    wait(sg_ml, k + 1)
                    slab_unit(u, k, m_hi, m_lo, k == 0, u == U_Q - 1)
                    between(u)
                wait(sg_hl, 16)
                for c in range(CHUNKS, CHUNKS + 4):
                    pair_free(c)
                    for q in range(4):
                        chunk_unit_fm(c, q, h_hi, h_lo)
                        between(chunk_of_stream(c) + q)
                wait(sg_ql, 4)
                for b, banks in ((0, pm), (1, pp)):
                    u = U_K + b
                    unit_ready(u)
                    for t in range(TT):
                        tok = slice(P * t, P * (t + 1))
                        for i in range(8):
                            hc = 8 * b + i
                            col = slice(P * i, P * (i + 1))
                            dst = banks[:, 2 * t + i // 4, P * (i % 4):P * (i % 4 + 1)]
                            pe.matmul(dst, q_hi[:, hc, tok], w_hi[:, u % RING, col], start=True, stop=False)
                            pe.matmul(dst, q_hi[:, hc, tok], w_lo[:, u % RING, col], start=False, stop=False)
                            last = pe.matmul(dst, q_lo[:, hc, tok], w_hi[:, u % RING, col], start=False, stop=True)
                    last.then_inc(sg_used.sem, 1)
                wait(sg_kv, 4)
                wait(sg_tk, n_tk)
                for i in range(3):
                    for t in range(TT):
                        last = transpose(pm[:, i, P * t:P * (t + 1)], pick[:, i, t].rearrange("p h k -> p (h k)"))
                last.then_inc(sg_ix.sem, 1)
                wait(sg_ixe, 3)
                pe.sem_inc(s_apart)
                with pe.Fori(0, SEQ // 16) as i:
                    for r in range(16):
                        pe.wait_ge(sg_hot.sem, sg_hot.at(l, 16 * i + (r + 1)))
                        if r % 4 == 0:
                            pe.wait_ge(sg_free.sem, sg_free.at(l, 4 * i + (r // 4 - 3)))
                        pe.matmul(pm[:, r // 4, P * (r % 4):P * (r % 4 + 1)], hot[:, r % 2, 0, :], hot[:, r % 2, 1, :], start=True, stop=True).then_inc(sg_rt.sem, 1)

                def down(slot, vpos, bank):
                    pe.wait_ge(sg_lo.sem, sg_lo.at(l, vpos + (U_E + 1)))
                    for k in range(KD):
                        col = slice(P * k, P * (k + 1))
                        wh, wl = w_hi[:, slot, col], w_lo[:, slot, col]
                        dst = pm[:, bank, 0:SEQ]
                        pe.matmul(dst, wh, h_hi[:, k, :], start=(k == 0), stop=False)
                        pe.matmul(dst, wh, h_lo[:, k, :], start=False, stop=False)
                        last = pe.matmul(dst, wl, h_hi[:, k, :], start=False, stop=(k == KD - 1))
                    last.then_inc(sg_used.sem, 1)

                def up(slot, vpos, j, buf, start, stop):
                    pe.wait_ge(sg_lo.sem, sg_lo.at(l, vpos + (U_E + 1)))
                    pe.wait_ge(sg_gl.sem, sg_gl.at(l, 3 * j + 3))
                    for t in range(TT):
                        tok = slice(P * t, P * (t + 1))
                        for half in range(2):
                            col = slice(CW * half, CW * (half + 1))
                            dst = pp[:, 2 * t + half, :]
                            pe.matmul(dst, g_hi[:, buf, tok], w_hi[:, slot, col], start=start, stop=False, skip_group_check=True)
                            pe.matmul(dst, g_hi[:, buf, tok], w_lo[:, slot, col], start=False, stop=False, skip_group_check=True)
                            last = pe.matmul(dst, g_lo[:, buf, tok], w_hi[:, slot, col], start=False, stop=stop, skip_group_check=True)
                    last.then_inc(sg_used.sem, 1)

                pe.wait_ge(sg_free.sem, sg_free.at(l, SEQ // 4))
                down(U_E % RING, 0, 0)
                for j in range(2):
                    if j == 1:
                        wait(sg_ge, 1)
                    down((U_E + 2 * j + 1) % RING, 2 * j + 1, (j + 1) % 2)
                    up((U_E + 2 * j + 2) % RING, 2 * j + 2, j, j, j == 0, False)
                with pe.Fori(1, KEYS // 2 - 1) as i:
                    for r in range(2):
                        pe.wait_ge(sg_ge.sem, sg_ge.at(l, 2 * i + r))
                        down((U_E + 2 * r + 1) % RING, 4 * i + (2 * r + 1), (r + 1) % 2)
                        up((U_E + 2 * r + 2) % RING, 4 * i + (2 * r + 2), 2 * i + r, r, False, False)
                j = KEYS - 2
                wait(sg_ge, j)
                down((U_E + down_v(j + 1)) % RING, down_v(j + 1), 1)
                up((U_E + up_v(j)) % RING, up_v(j), j, 0, False, False)
                up((U_E + up_v(j + 1)) % RING, up_v(j + 1), j + 1, 1, False, True)

        @block.scalar
        def _(act):
            act.sem_inc(sg_free.sem, sg_free.start)
            act.sem_inc(sg_hi.sem, sg_hi.start)
            act.wait_ge(s_init, INIT)
            with act.Fori(0, LAYERS) as l:

                def wait(sig, n):
                    act.wait_ge(sig.sem, sig.at(l, n))

                def high(u):
                    act.wait_ge(sg_raw[u % RING].sem, sg_raw[u % RING].at(l, 16 * (u // RING + 1)))
                    wait(sg_used, max(u - RING + 1, 0))
                    act.activation(w_hi[:, u % RING, :], raw[:, u % RING, :], ACT.Copy).then_inc(sg_hi.sem, 1)

                def norm(n):
                    for t in range(TT):
                        last = act.activation(njunk[:, t, :], x[:, t, :], ACT.Square, accum_out=stat[:, t:t + 1])
                    last.then_inc(sg_sq.sem, 1)
                    wait(sg_sq, n + 1)
                    act.activation(stat[:, 2:4], stat[:, 0:2], ACT.Sqrt, scale=1.0 / D, bias=stat[:, 60:61]).then_inc(sg_root.sem, 1)
                    for k in range(KD):
                        if k % 2 == 0:
                            wait(sg_turn, 4 * n + k // 2 + 1)
                        act.activation(h_hi[:, k, :], pm[:, k // 2, SEQ * (k % 2):SEQ * (k % 2 + 1)], ACT.Copy,
                                       scale=fmp[:, bass.ds(l, 1), 8 * n + k]).then_inc(sg_hh.sem, 1)

                def evacuate(c):
                    if C_X <= c < C_Z:
                        return
                    wait(sg_used, chunk_of_stream(c) + 4)
                    pair = 2 * (c % 2)
                    for b in range(2):
                        src = pp[:, pair + b, :]
                        if c < C_QK:
                            w = min(CW, V_COLS - CW * c)
                            last = act.activation(v[:, b, CW * c:CW * c + w], src[:, 0:w], ACT.Copy)
                        elif c < C_X:
                            first = 4 * (c - C_QK) + 2 * b
                            for m in (0, 1):
                                is_q = (first + m) // 9 % 2 == 0
                                last = act.activation(qk[:, first + m, :], src[:, SEQ * m:SEQ * (m + 1)], ACT.Copy,
                                                      scale=HD ** -0.5 if is_q else 1.0)
                        elif c < C_G:
                            last = act.activation(z[:, b, CW * (c - C_Z):CW * (c - C_Z + 1)], src, ACT.Silu)
                        elif c < CHUNKS:
                            last = act.activation(gates[:, b, CW * (c - C_G):CW * (c - C_G + 1)], src, ACT.Sigmoid)
                        else:
                            tile = 4 * (c - CHUNKS) + 2 * b
                            last = act.activation(q_hi[:, tile:tile + 2, :].rearrange("p a t -> p (a t)"), src, ACT.Copy)
                    last.then_inc(sg_ev.sem, 1)
                    if C_Z <= c < C_G:
                        i = c - C_Z
                        wait(sg_cv, 128)
                        q = xt[:, 8 * i:8 * i + 8, :]
                        act.activation(q, q, ACT.Silu).then_inc(sg_xs.sem, 1)

                def dt_scalar(_n):
                    wait(sg_mix, 48)
                    act.activation(ea[:], rows[:, 32:64], ACT.Exp).then_inc(sg_dta.sem, 1)
                    wait(sg_dt, 1)
                    act.activation(dtt[:], dt[:], ACT.Abs).then_inc(sg_dta.sem, 1)
                    wait(sg_dta, 2)
                    act.activation(dtt[:], dtt[:], ACT.Exp, scale=-1.0).then_inc(sg_dta.sem, 1)
                    wait(sg_dta, 3)
                    act.activation(dtt[:], dtt[:], ACT.Ln, bias=1.0).then_inc(sg_dta.sem, 1)
                    wait(sg_dtp, 1)
                    act.activation(ed[:].rearrange("p a h -> p (a h)"), pm[:, 3, 0:64], ACT.Exp).then_inc(sg_dta.sem, 1)

                def a_score(j):
                    wait(sg_am, j + 1)
                    act.activation(a_p[:, :, 0:P], a_p[:, :, 0:P], ACT.Exp, bias=stat[:, 4:5], accum_out=stat[:, 6:7])
                    act.activation(a_p[:, :, P:3 * P], a_p[:, :, P:3 * P], ACT.Exp, bias=stat[:, 5:6], accum_out=stat[:, 7:8]).then_inc(sg_ae.sem, 1)

                def a_turn(j):
                    if j >= 1:
                        wait(sg_apv, j)
                    for g in range(A_GROUPS):
                        wait(sg_at, 3 * j + g + 1)
                        act.activation(a_pt[:, g, :], pm[:, g, 0:384], ACT.Copy).then_inc(sg_ap.sem, 1)

                def a_mix(j):
                    wait(sg_apv, j + 1)
                    row = slice(HD * (j % 2), HD * (j % 2) + HD)
                    act.activation(yt[row, j // 2, :], pm[row, 3, 0:SEQ], ACT.Copy).then_inc(sg_ay.sem, 1)

                def c_score(p):
                    for i in range(2):
                        h = 2 * p + i
                        wait(sg_cz, h + 1)
                        if p == 0:
                            wait(sg_apv, 6)
                        else:
                            wait(sg_cc, h - 1)
                        act.activation(c_sp[:, i, :], pm[:, i, 0:384], ACT.Abs).then_inc(sg_cl.sem, 1)
                    for i in range(2):
                        wait(sg_cl, 6 * p + i + 1)
                        act.activation(c_sp[:, i, :], c_sp[:, i, :], ACT.Exp, scale=-1.0).then_inc(sg_cl.sem, 1)
                    for i in range(2):
                        wait(sg_cl, 6 * p + i + 3)
                        act.activation(c_sp[:, i, :], c_sp[:, i, :], ACT.Ln, bias=1.0).then_inc(sg_cl.sem, 1)

                def c_sum(p):
                    if p >= 1:
                        wait(sg_cpv, p)
                    for i in range(2):
                        wait(sg_cc, 2 * p + i + 1)
                        act.activation(c_w[:, i, :], pm[:, i, 0:384], ACT.Exp).then_inc(sg_cw.sem, 1)

                def ssd(n):
                    if n < 2 * GROUPS:
                        t = n % 2
                        if t == 0:
                            wait(sg_s1, n + 1)
                            if n >= 2:
                                wait(sg_s2, n - 1)
                            act.activation(s_bt[:], pm[:, 0, 384:512], ACT.Copy).then_inc(sg_sb.sem, 1)
                        wait(sg_sgm, n + 1)
                        if n >= 2:
                            wait(sg_s2, n - 1)
                        act.activation(s_e[:, t].rearrange("p h t -> p (h t)"), pm[:, 2, :], ACT.Exp).then_inc(sg_se.sem, 1)
                    if n >= 1 and (n - 1) % 2 == 0:
                        wait(sg_s2, n)
                        act.activation(s_state[:].rearrange("p h d -> p (h d)"), pm[:, 3, 256:512], ACT.Copy).then_inc(sg_st.sem, 1)

                def split_y(i):
                    if i == 0:
                        wait(sg_cy, 9)
                        wait(sg_ay, 6)
                        wait(sg_cz, 18)
                    act.activation(yt_hi[:, 4 * i:4 * i + 4, :], yt[:, 4 * i:4 * i + 4, :], ACT.Copy).then_inc(sg_yh.sem, 1)

                def ssd_norm(_n):
                    wait(sg_sd, 48)
                    for t in range(TT):
                        act.activation(junk[:], z[:, t, :], ACT.Square, accum_out=stat[:, 8 + t:9 + t]).then_inc(sg_bq.sem, 1)
                        wait(sg_bq, t + 1)
                    act.activation(stat[:, 10:12], stat[:, 8:10], ACT.Sqrt, scale=1.0 / SSD_IN, bias=stat[:, 60:61]).then_inc(sg_bq.sem, 1)

                def turn_b(k):
                    wait(sg_bt, k + 1)
                    act.activation(yb_hi[:, k, :], pm[:, k % 4, 0:SEQ], ACT.Copy,
                                   scale=fmp[:, bass.ds(l, 1), 176 + k]).then_inc(sg_bh.sem, 1)

                def turn_merged(_n):
                    for k in range(KD):
                        wait(sg_mtt, k // 2 * 2 + 2)
                        act.activation(m_hi[:, k, :], pm[:, k // 2, SEQ * (k % 2):SEQ * (k % 2 + 1)], ACT.Copy).then_inc(sg_mh.sem, 1)

                def norm1(n):
                    wait(sg_xa, 1)
                    norm(n)

                def key_scores(b):
                    banks = pm if b == 0 else pp
                    wait(sg_used, U_K + b + 1)
                    for t in range(TT):
                        act.activation(sc[:, t, 8 * b:8 * b + 8, :].rearrange("p a n -> p (a n)"),
                                       banks[:, 2 * t:2 * t + 2, :].rearrange("p a n -> p (a n)"), ACT.Copy).then_inc(sg_kv.sem, 1)

                steps = {"evacuate": evacuate, "dt": dt_scalar, "a_score": a_score, "a_turn": a_turn, "a_mix": a_mix,
                         "c_score": c_score, "c_sum": c_sum, "ssd": ssd, "split_y": split_y, "ssd_norm": ssd_norm,
                         "turn_b": turn_b, "turn_merged": turn_merged, "norm": norm1, "key_scores": key_scores}

                wait(sg_xa, 0)
                for u in range(RING):
                    high(u)
                norm(0)
                for u in range(U_E):
                    if u + RING < U_E + RING:
                        high(u + RING)
                    for name, arg in ORDER[u]:
                        if name in steps:
                            steps[name](arg)
                wait(sg_tk, n_tk - 12 - 4)
                act.activation(pick[:, 2], pick[:, 2], ACT.Exp).then_inc(sg_gx.sem, 1)
                wait(sg_ix, 1)
                with act.Fori(0, SEQ // 16) as i:
                    for b in range(4):
                        act.wait_ge(sg_rt.sem, sg_rt.at(l, 16 * i + 4 * (b + 1)))
                        act.activation(route[:, :, bass.ds(16 * i + 4 * b, 4)], pm[:, b, :].rearrange("p (t j) -> p j t", t=4), ACT.Copy).then_inc(sg_free.sem, 1)

                def expert_high(slot, vpos, turn):
                    act.wait_ge(sg_raw[slot].sem, sg_raw[slot].at(l, turn * 16))
                    act.wait_ge(sg_used.sem, sg_used.at(l, vpos + (U_E - RING + 1)))
                    act.activation(w_hi[:, slot, :], raw[:, slot, :], ACT.Copy).then_inc(sg_hi.sem, 1)

                def gelu(j, vpos, buf):
                    act.wait_ge(sg_used.sem, sg_used.at(l, vpos + (U_E + 1)))
                    act.activation(g_act[:, buf, :], pm[:, buf, 0:SEQ], ACT.Gelu).then_inc(sg_ge.sem, 1)

                def static_high(vp):
                    u = U_E + vp
                    expert_high(u % RING, vp, u // RING + 1)

                gelu(0, 0, 0)
                static_high(4)
                gelu(1, 1, 1)
                static_high(5)
                static_high(6)
                with act.Fori(1, KEYS // 2 - 1) as i:
                    for r in range(2):
                        gelu(2 * i + r, 4 * i + (2 * r - 1), r)
                        for e in (3, 4):
                            u = U_E + 2 * r + e
                            expert_high(u % RING, 4 * i + (2 * r + e), i + (u // RING + 1))
                gelu(KEYS - 2, down_v(KEYS - 2), 0)
                static_high(2 * KEYS - 1)
                gelu(KEYS - 1, down_v(KEYS - 1), 1)
            act.wait_ge(sg_xa.sem, sg_xa.at(LAYERS, 0))
            for t in range(TT):
                last = act.activation(njunk[:, t, :], x[:, t, :], ACT.Square, accum_out=stat[:, t:t + 1])
            last.then_inc(s_fina, 1)
            act.wait_ge(s_fina, 1)
            act.activation(stat[:, 2:4], stat[:, 0:2], ACT.Sqrt, scale=1.0 / D, bias=stat[:, 60:61]).then_inc(s_fina, 1)

        @block.vector
        def _(dve):
            dve.sem_inc(sg_lo.sem, sg_lo.start)
            dve.sem_inc(sg_xa.sem, sg_xa.start)
            dve.memset(stat[:], EPS).then_inc(s_init, 16)
            slopes = [2.0 ** (-8.0 * (h + 1) / A_HEADS) for h in range(A_HEADS)]
            dve.wait_ge(s_init, INIT)
            with dve.Fori(0, LAYERS) as l:

                def wait(sig, n):
                    dve.wait_ge(sig.sem, sig.at(l, n))

                def low(u):
                    wait(sg_hi, u + 1)
                    dve.tensor_tensor(w_lo[:, u % RING, :], raw[:, u % RING, :], w_hi[:, u % RING, :].bitcast(F32), ALU.subtract).then_inc(sg_lo.sem, 1)

                def norm(n):
                    wait(sg_root, n + 1)
                    dve.reciprocal(stat[:, 12:14], stat[:, 2:4]).then_inc(sg_rstd.sem, 1)
                    wait(sg_rstd, n + 1)
                    for t in range(TT):
                        last = dve.tensor_scalar(xn[:, t, :], x[:, t, :], stat[:, 12 + t:13 + t], None, ALU.mult)
                    last.then_inc(sg_xn.sem, 1)
                    for k in range(KD):
                        wait(sg_hh, 8 * n + k // 2 * 2 + 2)
                        dve.scalar_tensor_tensor(h_lo[:, k, :], pm[:, k // 2, SEQ * (k % 2):SEQ * (k % 2 + 1)],
                                                 fmp[:, bass.ds(l, 1), 8 * n + k], h_hi[:, k, :].bitcast(F32), ALU.mult, ALU.subtract).then_inc(sg_hl.sem, 1)

                def evacuate(c):
                    if c >= CHUNKS:
                        wait(sg_ev, c - X_CH + 1)
                        for b in range(2):
                            tile = 4 * (c - CHUNKS) + 2 * b
                            last = dve.tensor_tensor(q_lo[:, tile:tile + 2, :].rearrange("p a t -> p (a t)"), pp[:, 2 * (c % 2) + b, :],
                                                     q_hi[:, tile:tile + 2, :].rearrange("p a t -> p (a t)").bitcast(F32), ALU.subtract)
                        last.then_inc(sg_ql.sem, 1)
                    if not C_X <= c < C_Z:
                        return
                    wait(sg_used, 4 * c + 4)
                    for tap in range(4):
                        for m in range(4):
                            ch = 4 * (c - C_X) + m
                            src = pp[:, 2 * (c % 2) + m // 2, SEQ * (m % 2):SEQ * (m % 2 + 1)]
                            wk = fmp[:, bass.ds(l, 1), 16 + 4 * ch + 3 - tap]
                            if tap == 0:
                                ins = dve.tensor_scalar(xt[:, ch, :], src, wk, fmp[:, bass.ds(l, 1), 144 + ch], ALU.mult, ALU.add)
                            else:
                                wait(sg_cv, 16 * (c - C_X) + 4 * (tap - 1) + m + 1)
                                ins = dve.scalar_tensor_tensor(xt[:, ch, tap:SEQ], src[:, 0:SEQ - tap], wk, xt[:, ch, tap:SEQ], ALU.mult, ALU.add)
                            ins.then_inc(sg_cv.sem, 1)

                def dt_vector(_n):
                    wait(sg_ev, V_CH)
                    wait(sg_mix, 48)
                    dve.tensor_tensor(dt[:], v[:, :, 2 * A_W:V_COLS], rows[:, 0:32].unsqueeze(1).broadcast_to([P, TT, SSD_H]), ALU.add).then_inc(sg_dt.sem, 1)
                    wait(sg_dta, 4)
                    dve.scalar_tensor_tensor(dt[:], dt[:], 0.0, dtt[:], ALU.max, ALU.add).then_inc(sg_dt.sem, 1)
                    wait(sg_dt, 2)
                    dve.scalar_tensor_tensor(da[:], dt[:], -1.0, ea[:].unsqueeze(1).broadcast_to([P, TT, SSD_H]), ALU.mult, ALU.mult).then_inc(sg_dt.sem, 1)
                    wait(sg_dta, 5)
                    dve.tensor_tensor(dtd[:], dt[:, 0, :], ed[:, 1, :], ALU.mult).then_inc(sg_dt.sem, 1)

                def a_score(j):
                    for g in range(A_GROUPS):
                        wait(sg_as, 3 * j + g + 1)
                        if j >= 1 and g == 0:
                            wait(sg_at, 3 * j)
                        dve.scalar_tensor_tensor(a_p[:, g, :], dist[:, g, :], slopes[g * A_SLOTS + j], pm[:, g, 0:384], ALU.mult, ALU.add).then_inc(sg_ab.sem, 1)
                    wait(sg_ab, 3 * j + 3)
                    dve.tensor_reduce(stat[:, 4:5], a_p[:, :, 0:P], AX.XY, ALU.max, negate=True)
                    dve.tensor_reduce(stat[:, 5:6], a_p[:, :, P:3 * P], AX.XY, ALU.max, negate=True).then_inc(sg_am.sem, 1)
                    wait(sg_ae, j + 1)
                    dve.reciprocal(stat[:, 14:16], stat[:, 6:8]).then_inc(sg_ar.sem, 1)
                    wait(sg_ar, 2 * j + 1)
                    dve.tensor_scalar(a_p[:, :, 0:P], a_p[:, :, 0:P], stat[:, 14:15], None, ALU.mult)
                    dve.tensor_scalar(a_p[:, :, P:3 * P], a_p[:, :, P:3 * P], stat[:, 15:16], None, ALU.mult).then_inc(sg_ar.sem, 1)

                def c_score(p):
                    for i in range(2):
                        wait(sg_cl, 6 * p + i + 5)
                        dve.scalar_tensor_tensor(c_sp[:, i, :], pm[:, i, 0:384], 0.0, c_sp[:, i, :], ALU.max, ALU.add).then_inc(sg_csp.sem, 1)

                def c_mix(p):
                    wait(sg_cpv, p + 1)
                    dve.tensor_copy(yt[:, 3 + p, :], pm[:, 2, 0:SEQ]).then_inc(sg_cy.sem, 1)

                def scan_steps(n):
                    g, t = n // 2, n % 2
                    if n == 0:
                        wait(sg_cy, 9)
                    else:
                        wait(sg_sgm, n)
                    dve.tensor_tensor(s_r[:], da[:, t, HPG * g:HPG * (g + 1)].unsqueeze(2).broadcast_to([P, HPG, P]),
                                      lower.unsqueeze(1).broadcast_to([P, HPG, P]), ALU.mult).then_inc(sg_sr.sem, 1)

                def per_head(row):
                    return row.unsqueeze(2).broadcast_to([P, HPG, HD])

                def ssd(n):
                    if n == 0:
                        scan_steps(0)
                    if n < 2 * GROUPS:
                        g, t = n // 2, n % 2
                        hs = slice(HPG * g, HPG * (g + 1))
                        xs = pm[:, t, 0:256].rearrange("p (h d) -> p h d", h=HPG)
                        wait(sg_s1, n + 1)
                        if t == 0:
                            wait(sg_sb, g + 1)
                        if n:
                            wait(sg_sm, n)
                        dve.tensor_tensor(s_cb[:], pm[:, t, 256:384], lower, ALU.mult).then_inc(sg_sc.sem, 1)
                        if n >= 2:
                            wait(sg_s2, n - 1)
                            wait(sg_sd, final_of(n - 2))
                        dve.tensor_tensor(s_xdt[:, t], xs, per_head(dt[:, t, hs]), ALU.mult)
                        if t == 0:
                            dve.tensor_tensor(s_xdd[:], xs, per_head(dtd[:, hs]), ALU.mult)
                        dve.tensor_tensor(s_y[:, t], xs, per_head(rows[:, 64 + HPG * g:64 + HPG * (g + 1)]), ALU.mult).then_inc(sg_sx.sem, 1)
                        wait(sg_sc, n + 1)
                        wait(sg_se, n + 1)
                        dve.tensor_tensor(s_e[:, t], s_e[:, t], s_cb[:].unsqueeze(1).broadcast_to([P, HPG, P]), ALU.mult).then_inc(sg_sm.sem, 1)
                    if n >= 1:
                        m = n - 1
                        g, t = m // 2, m % 2
                        done = final_of(m - 1) if m else 0
                        heads = slice(HPG * HD * g, HPG * HD * (g + 1))
                        wait(sg_s2, m + 1)
                        wait(sg_st, g + 1)
                        y = s_y[:, t]
                        dve.tensor_tensor(y, y, pm[:, 3, 0:256].rearrange("p (h d) -> p h d", h=HPG), ALU.add).then_inc(sg_sd.sem, 1)
                        if t == 1:
                            off = s_xdt[:, 1]
                            dve.tensor_tensor(off, pm[:, 3, 256:512].rearrange("p (h d) -> p h d", h=HPG),
                                              per_head(ed[:, 0, HPG * g:HPG * (g + 1)]), ALU.mult).then_inc(sg_sd.sem, 1)
                            wait(sg_sd, done + 2)
                            dve.tensor_tensor(y, y, off, ALU.add).then_inc(sg_sd.sem, 1)
                        wait(sg_sd, final_of(m) - 1)
                        zg = z[:, t, heads]
                        dve.tensor_tensor(zg, zg, y.rearrange("p h d -> p (h d)"), ALU.mult).then_inc(sg_sd.sem, 1)
                    if n + 1 < 2 * GROUPS:
                        scan_steps(n + 1)

                def split_y(i):
                    wait(sg_yh, i + 1)
                    dve.tensor_tensor(yt_lo[:, 4 * i:4 * i + 4, :], yt[:, 4 * i:4 * i + 4, :], yt_hi[:, 4 * i:4 * i + 4, :].bitcast(F32), ALU.subtract).then_inc(sg_yl.sem, 1)

                def gate(branch, i):
                    t, half = i // 2, i % 2
                    return gates[:, t, D * branch + CW * half:D * branch + CW * (half + 1)]

                def merged_part(i):
                    return merged[:, i // 2, CW * (i % 2):CW * (i % 2 + 1)]

                def merge(n):
                    if n == 0:
                        wait(sg_used, U_A)
                        for i in range(4):
                            dve.tensor_tensor(merged_part(i), pp[:, i, :], gate(2, i), ALU.mult).then_inc(sg_mg.sem, 1)
                        return
                    wait(sg_used, U_B if n == 1 else U_O)
                    if n == 1:
                        wait(sg_mg, 4)
                    else:
                        wait(sg_br, 1)
                    done = 8 * (n - 1)
                    for i in range(6):
                        if i >= 2:
                            wait(sg_mt, done + (i - 1 if i < 4 else 2 * i - 4 + (i == 4)))
                            dve.tensor_tensor(merged_part(i - 2), merged_part(i - 2), mtmp[:, i % 2, :], ALU.add).then_inc(sg_mt.sem, 1)
                        if i < 4:
                            if i >= 2:
                                wait(sg_mt, done + (3 if i == 2 else 5))
                            if n == 1:
                                dve.tensor_tensor(mtmp[:, i % 2, :], pp[:, i, :], gate(0, i), ALU.mult).then_inc(sg_mt.sem, 1)
                            else:
                                dve.scalar_tensor_tensor(mtmp[:, i % 2, :], pp[:, i, :], stat[:, 16 + i // 2:17 + i // 2], gate(1, i), ALU.mult, ALU.mult).then_inc(sg_mt.sem, 1)

                def ssd_norm(_n):
                    wait(sg_bq, 3)
                    dve.reciprocal(stat[:, 16:18], stat[:, 10:12]).then_inc(sg_br.sem, 1)

                def turn_b(k):
                    wait(sg_bh, k + 1)
                    dve.scalar_tensor_tensor(yb_lo[:, k, :], pm[:, k % 4, 0:SEQ],
                                             fmp[:, bass.ds(l, 1), 176 + k], yb_hi[:, k, :].bitcast(F32), ALU.mult, ALU.subtract).then_inc(sg_bl.sem, 1)

                def turn_merged(_n):
                    for k in range(KD):
                        wait(sg_mh, k // 2 * 2 + 2)
                        dve.tensor_tensor(m_lo[:, k, :], pm[:, k // 2, SEQ * (k % 2):SEQ * (k % 2 + 1)], m_hi[:, k, :].bitcast(F32), ALU.subtract).then_inc(sg_ml.sem, 1)

                def add_x(n):
                    wait(sg_used, U_Q if n == 0 else UNITS)
                    for t in range(TT):
                        last = dve.tensor_tensor(x[:, t, :], x[:, t, :], pp[:, 2 * t:2 * t + 2, :].rearrange("p a n -> p (a n)"), ALU.add)
                    last.then_inc(sg_xa.sem, 1)

                steps = {"evacuate": evacuate, "dt": dt_vector, "a_score": a_score, "c_score": c_score, "c_mix": c_mix,
                         "ssd": ssd, "split_y": split_y, "merge": merge, "ssd_norm": ssd_norm, "turn_b": turn_b,
                         "turn_merged": turn_merged, "add_x": add_x, "norm": norm}

                for u in range(RING):
                    low(u)
                norm(0)
                for u in range(U_E):
                    low(u + RING)
                    for name, arg in ORDER[u]:
                        if name in steps:
                            steps[name](arg)

                made = [0]

                def after(n):
                    dve.wait_ge(sg_tk.sem, sg_tk.at(l, n))
                    dve.sem_inc(s_apart)

                def step(ins):
                    made[0] += 1
                    ins.then_inc(sg_tk.sem, 1)
                    return made[0]

                def top16(values, scratch, val, idx):
                    a = step(dve.max(val[:, 0:8], values))
                    after(a)
                    step(dve.max_index(idx[:, 0:8], val[:, 0:8], values))
                    b = step(dve.match_replace(scratch, val[:, 0:8], values, NEG))
                    after(b)
                    c = step(dve.max(val[:, 8:16], scratch))
                    after(c)
                    step(dve.max_index(idx[:, 8:16], val[:, 8:16], scratch))

                wait(sg_kv, 4)
                dve.sem_inc(s_apart)
                for t in range(TT):
                    for h in range(RH):
                        for c in range(2):
                            top16(sc[:, t, 2 * h + c, :], tkt[:, c, 0:KEYS], t_val[:, t, h, c], t_idx[:, t, h, c])
                after(made[0])
                step(dve.tensor_copy(t_idf[:], t_idx[:]))
                for t in range(TT):
                    grid = [P, RH, TOPK, TOPK]
                    n = step(dve.tensor_tensor(cand[:], t_val[:, t, :, 0, :].unsqueeze(3).broadcast_to(grid),
                                               t_val[:, t, :, 1, :].unsqueeze(2).broadcast_to(grid), ALU.add))
                    after(n)
                    for h in range(RH):
                        top16(cand[:, h].rearrange("p a b -> p (a b)"), tkt[:, h % 2, :], b_val[:, t, h], b_pos[:, t, h])
                after(made[0])
                step(dve.tensor_scalar(b_row[:, 0], b_pos[:], 4, None, ALU.logical_shift_right))
                step(dve.tensor_scalar(b_row[:, 1], b_pos[:], 15, None, ALU.bitwise_and))
                flat = [P, TT * RH, TOPK]
                bv = b_val[:].rearrange("p t h k -> p (t h) k")
                pg = pick[:, 2].rearrange("p t h k -> p (t h) k")
                n = step(dve.tensor_tensor(pg, bv, bv[:, :, 0:1].broadcast_to(flat), ALU.subtract))
                assert n == n_tk - 12 - 4
                after(n)
                n = step(dve.tensor_copy(b_rof[:], b_row[:]))
                after(n)
                for c in range(2):
                    for t in range(TT):
                        grid = [P, RH, TOPK, TOPK]
                        n = step(dve.tensor_tensor(eq[:], b_rof[:, c, t].unsqueeze(3).broadcast_to(grid),
                                                   iota[:, 0:TOPK].unsqueeze(1).unsqueeze(1).broadcast_to(grid), ALU.is_equal))
                        after(n)
                        n = step(dve.tensor_tensor(eq[:], eq[:], t_idf[:, t, :, c, :].unsqueeze(2).broadcast_to(grid), ALU.mult))
                        after(n)
                        n = step(dve.tensor_reduce(pick[:, c, t], eq[:], AX.X, ALU.add))
                        after(n)
                wait(sg_gx, 1)
                n = step(dve.tensor_reduce(stat[:, 20:36], pg, AX.X, ALU.add))
                after(n)
                n = step(dve.reciprocal(stat[:, 36:52], stat[:, 20:36]))
                after(n)
                n = step(dve.tensor_tensor(pg, pg, stat[:, 36:52].unsqueeze(2).broadcast_to(flat), ALU.mult))
                assert n == n_tk, (n, n_tk)
                wait(sg_ix, 1)
                for i in range(3):
                    dve.tensor_copy(pick_t[:, i, :], pm[:, i, 0:SEQ]).then_inc(sg_ixe.sem, 1)
                wait(sg_ixe, 3)
                dve.sem_inc(s_apart)
                with dve.Fori(0, SEQ // 16) as i:
                    for r in range(16):
                        dve.wait_ge(sg_rt.sem, sg_rt.at(l, 16 * i + max(r - 1, 0)))
                        col = bass.ds(16 * i + r, 1)
                        dve.tensor_scalar(hot[:, r % 2, 0, :], iota[:], pick_t[:, 0, col], None, ALU.is_equal)
                        dve.tensor_scalar(hot[:, r % 2, 1, :], iota[:], pick_t[:, 1, col], pick_t[:, 2, col], ALU.is_equal, ALU.mult).then_inc(sg_hot.sem, 1)

                def weigh(j, buf):
                    dve.wait_ge(sg_ge.sem, sg_ge.at(l, j + 1))
                    g = g_act[:, buf, :]
                    dve.tensor_tensor(g, g, route[:, bass.ds(j, 1), :].rearrange("p o t -> p (o t)"), ALU.mult).then_inc(sg_gl.sem, 1)
                    dve.wait_ge(sg_gl.sem, sg_gl.at(l, 3 * j + 1))
                    dve.tensor_copy(g_hi[:, buf, :], g).then_inc(sg_gl.sem, 1)
                    dve.wait_ge(sg_gl.sem, sg_gl.at(l, 3 * j + 2))
                    dve.tensor_tensor(g_lo[:, buf, :], g, g_hi[:, buf, :].bitcast(F32), ALU.subtract).then_inc(sg_gl.sem, 1)

                def expert_low(slot, vpos):
                    dve.wait_ge(sg_hi.sem, sg_hi.at(l, vpos + (U_E + 1)))
                    dve.tensor_tensor(w_lo[:, slot, :], raw[:, slot, :], w_hi[:, slot, :].bitcast(F32), ALU.subtract).then_inc(sg_lo.sem, 1)

                dve.wait_ge(sg_free.sem, sg_free.at(l, SEQ // 4))
                weigh(0, 0)
                expert_low((U_E + 4) % RING, 4)
                weigh(1, 1)
                expert_low((U_E + 5) % RING, 5)
                expert_low((U_E + 6) % RING, 6)
                with dve.Fori(1, KEYS // 2 - 1) as i:
                    for r in range(2):
                        weigh(2 * i + r, r)
                        for e in (3, 4):
                            expert_low((U_E + 2 * r + e) % RING, 4 * i + (2 * r + e))
                weigh(KEYS - 2, 0)
                expert_low((U_E + 2 * KEYS - 1) % RING, 2 * KEYS - 1)
                weigh(KEYS - 1, 1)
                add_x(1)
            dve.wait_ge(s_fina, 2)
            dve.reciprocal(stat[:, 12:14], stat[:, 2:4]).then_inc(s_fin, 1)
            dve.wait_ge(s_fin, 1)
            dve.wait_ge(s_fg, 16)
            for t in range(TT):
                dve.scalar_tensor_tensor(xn[:, t, :], x[:, t, :], stat[:, 12 + t:13 + t], fing[:], ALU.mult, ALU.mult).then_inc(s_fin, 1)
            dve.drain().then_inc(s_fin, 1)


def lay_out_chunks(w):
    layers, _, cols = w.shape
    n = cols // CW
    w = w.reshape(layers, 4, 2, P, n, CW).transpose(0, 4, 1, 3, 2, 5)
    return w.reshape(layers, 4 * n, P, 1024)


def lay_out_slabs(w):
    return w.reshape(w.shape[0], -1, P, D)


def lay_out_stream(w_in, w_a, w_b, w_c, w_out, w_query, sub_keys, down, up):
    widths = (A_W, A_W, A_W, C_W, C_W, C_W, SSD_IN, CONV, SSD_H, 3 * D)
    edges = np.concatenate([[0], np.cumsum(widths)])
    qa, ka, va, qc, kc, vc, zz, xbc, dtw, gl = (w_in[:, :, a:b] for a, b in zip(edges[:-1], edges[1:]))
    pad = np.zeros((LAYERS, D, V_CH * CW - V_COLS), w_in.dtype)
    w = np.concatenate([va, vc, dtw, pad, qa, ka, qc, kc, xbc, zz, gl], axis=2)
    stream = np.empty((LAYERS, UNITS, P, 1024), w_in.dtype)
    stream[:, 0:U_C] = lay_out_chunks(w)
    stream[:, U_C:U_A] = lay_out_slabs(w_c)
    stream[:, U_A:U_B] = lay_out_slabs(w_a)
    stream[:, U_B:U_O] = lay_out_slabs(w_b)
    stream[:, U_O:U_Q] = lay_out_slabs(w_out)
    stream[:, U_Q:U_K] = lay_out_chunks(w_query)
    stream[:, U_K:U_E] = sub_keys.reshape(LAYERS, 2, 8, KEYS, P).transpose(0, 1, 4, 2, 3).reshape(LAYERS, 2, P, 1024)
    downs = down.reshape(LAYERS, KEYS, KEYS, KD, P).transpose(0, 2, 4, 3, 1).reshape(LAYERS, KEYS, P, 1024)
    ups = up.reshape(LAYERS, KEYS, KEYS, D).transpose(0, 2, 1, 3)
    experts = stream[:, U_E:]
    experts[:, 0] = downs[:, 0]
    experts[:, 1:2 * KEYS - 2:2] = downs[:, 1:]
    experts[:, 2:2 * KEYS - 1:2] = ups[:, :KEYS - 1]
    experts[:, 2 * KEYS - 1] = ups[:, KEYS - 1]
    return stream.reshape(LAYERS * UNITS, P, 1024)


def mixer_constants():
    a, b = np.arange(P)[:, None], np.arange(P)[None, :]
    upper = (a > b).astype(np.float32)
    lower = (a <= b).astype(np.float32)
    neg_ge = -(a >= b).astype(np.float32)
    neg_one = -np.ones((P, P), np.float32)
    dists = []
    for d in DILATION:
        for t0, s0 in ((0, 0), (P, 0), (P, P)):
            diff = (t0 + a) - (s0 + b)
            ok = (diff >= 0) & (diff % d == 0) & (diff <= P * d)
            dists.append(np.where(ok, -diff, -1e30).astype(np.float32))
    f32 = np.concatenate([upper, lower, neg_ge, neg_one, *dists], axis=1)
    mask = np.where(a >= b, -1e30, 0.0).astype(np.float32)
    bf = np.concatenate([mask, np.eye(P, dtype=np.float32)], axis=1)
    return np.ascontiguousarray(f32), bf


def kernel(x, norm_mix_g, w_in, conv_w, conv_b, dt_bias, a_log, d_skip, ssd_norm_g, w_branch_a, w_branch_b,
           w_branch_c, w_out, norm_ffn_g, peer_w_query, peer_sub_keys, peer_down, peer_up, final_norm_g):
    import ml_dtypes
    import concourse.bacc as bacc
    from concourse.bass_utils import run_bass_kernel_spmd as run

    def fm(a, tiles):
        return np.asarray(a).reshape(LAYERS, tiles, P).transpose(0, 2, 1)

    x, final_norm_g = np.asarray(x), np.asarray(final_norm_g)
    stream = lay_out_stream(*(np.asarray(a) for a in (w_in, w_branch_a, w_branch_b, w_branch_c, w_out, peer_w_query,
                                                      peer_sub_keys, peer_down, peer_up)))
    taps = np.asarray(conv_w).reshape(LAYERS, 4, 32, P).transpose(0, 3, 2, 1).reshape(LAYERS, P, 128)
    fm_params = np.concatenate([fm(norm_mix_g, 8), fm(norm_ffn_g, 8), taps, fm(conv_b, 32), fm(ssd_norm_g, 16)], axis=2)
    row = np.concatenate([np.asarray(a) for a in (dt_bias, a_log, d_skip)], axis=1)
    row_params = np.broadcast_to(row[:, None, :], (LAYERS, P, 96))
    mix_f32, mix_bf16 = mixer_constants()
    arrays = {
        "x_in": x.reshape(SEQ, D),
        "stream": stream,
        "fm_params": fm_params,
        "row_params": row_params,
        "mix_f32": mix_f32,
        "mix_bf16": mix_bf16.astype(ml_dtypes.bfloat16),
        "ident_in": np.eye(P, dtype=np.float32),
        "iota_in": np.broadcast_to(np.arange(P, dtype=np.float32), (P, P)),
        "final_g": np.broadcast_to(final_norm_g, (P, D)),
    }
    arrays = {k: np.ascontiguousarray(a) for k, a in arrays.items()}
    nc = bacc.Bacc("TRN2", target_bir_lowering=False, num_devices=1)
    args = [nc.dram_tensor(n, a.shape, mybir.dt.from_np(a.dtype), kind="ExternalInput").ap() for n, a in arrays.items()]
    args.append(nc.dram_tensor("trunk_out", (SEQ, D), F32, kind="ExternalOutput").ap())
    build_trunk(nc, *args)
    result = run(nc, [arrays], core_ids=[0])
    return result.results[0]["trunk_out"].reshape(1, SEQ, D)
```

```python
from contextlib import ExitStack

import numpy as np
import concourse.bass as bass
from concourse import mybir

F32 = mybir.dt.float32
F32R = mybir.dt.float32r
BF16 = mybir.dt.bfloat16
U32 = mybir.dt.uint32
ALU = mybir.AluOpType
ACT = mybir.ActivationFunctionType
AX = mybir.AxisListType

P = 128
LAYERS, SEQ, D = 2, 256, 1024
TT = SEQ // P
KD = D // P
HD = 64
A_HEADS, A_SLOTS, A_GROUPS = 18, 6, 3
DILATION = (1, 4, 16)
A_W, C_W, A_OUT = A_HEADS * HD, 18 * HD, A_SLOTS * HD
C_HEADS = 18
SSD_IN, GROUPS, HPG, NSTATE = 2048, 8, 4, 128
SSD_H = GROUPS * HPG
CONV = SSD_IN + 2 * GROUPS * NSTATE
KEYS, TOPK, RH = 128, 16, 8
EPS = 1e-6
NEG = -3.0e38

RING = 4
CW = 512
V_CH, QK_CH, X_CH, Z_CH, G_CH = 5, 9, 8, 4, 6
C_V, C_QK = 0, V_CH
C_X = C_QK + QK_CH
C_Z = C_X + X_CH
C_G = C_Z + Z_CH
CHUNKS = C_G + G_CH
U_C = 4 * CHUNKS
U_A = U_C + C_W // P
U_B = U_A + A_OUT // P
U_O = U_B + SSD_IN // P
U_Q = U_O + KD
U_K = (U_Q + 8, U_Q + 17)
FIRST = KEYS // 2
U_E = U_K[1] + 1
U_U = U_E + FIRST
U_S = U_U + FIRST
UNITS = U_E + 2 * KEYS
LOW_POOL = U_K[0]
LOW_MIXED = (U_U + FIRST // 2 + RING) // RING * RING
AHEAD, GATE_EXP = 32, 28
HOT = 4
BANK_TOKENS = CW // FIRST
BATCHES, GROUPS_OF_ROUTES = SEQ // HOT, SEQ // BANK_TOKENS
assert GROUPS_OF_ROUTES == FIRST - AHEAD == FIRST // 2 and BANK_TOKENS == 2 * HOT
V_COLS = 2 * A_W + SSD_H


def chunk_of_stream(c):
    return 4 * c if c < CHUNKS else U_Q + 4 * (c - CHUNKS) + (c >= CHUNKS + 2)


def slot_units(slot):
    return len(range(slot, UNITS, RING))


def make_order():
    order = {u: [] for u in range(UNITS)}
    for c in range(CHUNKS + 4):
        order[chunk_of_stream(c) + 3].append(("evacuate", c))
    order[23].append(("dt", 0))
    a0 = 4 * (C_QK + 5) + 1
    for j in range(A_SLOTS):
        order[a0 + 2 + 4 * j].append(("a_turn", j))
        order[a0 + 4 + 4 * j].append(("a_mix", j))
    for j in range(A_SLOTS):
        order[a0 + 4 * j].append(("a_score", j))
    c0 = a0 + 4 * A_SLOTS + 1
    for p in range(C_HEADS // 2):
        order[c0 + 2 + 4 * p].append(("c_sum", p))
        order[c0 + 4 + 4 * p].append(("c_mix", p))
    for p in range(C_HEADS // 2):
        order[c0 + 4 * p].append(("c_score", p))
    s0 = 4 * C_G
    assert c0 + 4 * (C_HEADS // 2) < s0
    for n in range(2 * GROUPS):
        order[s0 + 2 * n].append(("ssd", n))
    order[s0 + 4 * GROUPS].append(("ssd", 2 * GROUPS))
    for i in range(3):
        order[s0 + 1 + 2 * i].append(("split_y", i))
    order[U_A - 1].append(("merge", 0))
    order[U_B - 1].append(("merge", 1))
    order[U_A].append(("ssd_norm", 0))
    for k in range(16):
        order[U_A + 1 + k].append(("turn_b", k))
    order[U_O - 1].append(("merge", 2))
    order[U_O - 1].append(("turn_merged", 0))
    order[U_Q - 1].append(("add_x", 0))
    order[U_Q - 1].append(("norm", 1))
    order[U_K[0]].append(("key_scores", 0))
    for i in range(4):
        order[U_K[0] + 2 + 2 * i].append(("top_keys", i))
    order[U_K[1]].append(("key_scores", 1))
    return order


ORDER = make_order()


def build_trunk(nc, x_in, stream, fm_params, row_params, mix_f32, mix_bf16, ident_in, iota_in, final_g, out):
    with ExitStack() as ctx:
        base = 16512

        def at(name, shape, offset, dtype=F32):
            return nc.alloc_sbuf_tensor_at(name, [P, *shape], dtype, offset=base + 4 * offset)

        fence = ctx.enter_context(nc.sbuf_tensor("fence", [P, 53200], F32))
        x = at("x", [TT, D], 0)
        h_hi = at("h_hi", [KD, SEQ], 2048, F32R)
        h_lo = at("h_lo", [KD, SEQ], 4096, F32R)
        raw = at("raw", [RING, 1024], 6144)
        w_hi = at("w_hi", [RING, 1024], 10240, F32R)
        w_lo = at("w_lo", [RING, 1024], 14336, F32R)
        ident = at("ident", [P], 18432)
        iota = at("iota", [P], 18560)
        fmp = at("fmp", [LAYERS, 192], 18688)
        stat = at("stat", [64], 19072)
        ar = 19136
        qk = at("qk", [36, SEQ], ar)
        gates = at("gates", [TT, 3 * D], ar)
        yt_hi = at("yt_hi", [12, SEQ], ar + 6144, F32R)
        v = at("v", [TT, V_COLS], ar + 9216)
        xt = at("xt", [32, SEQ], ar + 13888)
        z = at("z", [TT, SSD_IN], ar + 22080)
        yt = at("yt", [12, SEQ], ar + 26176)
        yt_lo = at("yt_lo", [12, SEQ], ar + 26176, F32R)
        ws = ar + 29248
        a_p = at("a_p", [A_GROUPS, 384], ws)
        a_pt = at("a_pt", [A_GROUPS, 384], ws + 1152)
        c_sp = at("c_sp", [2, 384], ws)
        c_w = at("c_w", [2, 384], ws + 768)
        merged = at("merged", [TT, D], ws)
        dts = ar + 31552
        dt = at("dt", [TT, SSD_H], dts)
        da = at("da", [TT, SSD_H], dts + 64)
        ed = at("ed", [2, SSD_H], dts + 128)
        dtd = at("dtd", [SSD_H], dts + 192)
        dtt = at("dtt", [TT, SSD_H], dts + 224)
        ea = at("ea", [SSD_H], dts + 288)
        mixc = ar + 31872
        mixf = at("mixf", [1664], mixc)
        upper = mixf[:, 0:128]
        lower = mixf[:, 128:256]
        neg_ge = mixf[:, 256:384]
        neg_one = mixf[:, 384:512]
        dist = mixf[:, 512:1664].rearrange("p (g n) -> p g n", g=A_GROUPS)
        mixb = at("mixb", [2, P], mixc + 1664, BF16)
        rows = at("rows", [96], mixc + 1792)
        sv = ar + 9216
        s_r = at("s_r", [HPG, P], sv)
        s_e = at("s_e", [2, HPG, P], sv + 512)
        s_cb = at("s_cb", [P], sv + 1536)
        s_xdt = at("s_xdt", [2, HPG, HD], sv + 1664)
        s_xdd = at("s_xdd", [HPG, HD], sv + 2176)
        s_state = at("s_state", [HPG, HD], sv + 2432)
        s_bt = at("s_bt", [P], sv + 2688)
        s_y = at("s_y", [2, HPG, HD], sv + 2816)
        mtmp = at("mtmp", [2, CW], sv + 3392)
        junk = at("junk", [SSD_IN], sv)
        m_hi = at("m_hi", [KD, SEQ], sv, F32R)
        m_lo = at("m_lo", [KD, SEQ], sv + 2048, F32R)
        yb_hi = at("yb_hi", [16, SEQ], ar + 13888, F32R)
        yb_lo = at("yb_lo", [16, SEQ], ar + 13888 + 4096, F32R)
        xn = at("xn", [TT, D], ar + 22080)
        njunk = at("njunk", [TT, D], ar + 22080 + 2048)
        q_hi = at("q_hi", [16, SEQ], ar + 16384, F32R)
        q_lo = at("q_lo", [16, SEQ], ar + 16384 + 4096, F32R)
        sc = at("sc", [TT, 16, KEYS], ar)
        tk = ar + 4096
        t_val = at("t_val", [TT, RH, 2, TOPK], tk)
        t_idx = at("t_idx", [TT, RH, 2, TOPK], tk + 512, U32)
        t_idf = at("t_idf", [TT, RH, 2, TOPK], tk + 1024)
        b_val = at("b_val", [TT, RH, TOPK], tk + 1536)
        b_pos = at("b_pos", [TT, RH, TOPK], tk + 1792, U32)
        b_row = at("b_row", [2, TT, RH, TOPK], tk + 2048, U32)
        b_rof = at("b_rof", [2, TT, RH, TOPK], tk + 2560)
        pick = at("pick", [3, TT, RH, TOPK], tk + 3072)
        gate_t = at("gate_t", [3, SEQ], tk + 7936)
        cand = at("cand", [TT, RH, TOPK, TOPK], tk + 3840)
        tkt = at("tkt", [4, 256], tk + 7936)
        route = at("route", [FIRST, SEQ], ar)
        hid = at("hid", [FIRST, SEQ], ar + 16384)
        hot_r = at("hot_r", [2, HOT, KEYS], 0, BF16)
        hot_e = at("hot_e", [2, HOT, FIRST], 512, BF16)
        hot_c = at("hot_c", [2, 3, HOT, FIRST], 768, BF16)
        g_act = at("g_act", [2, SEQ], 1536)
        g_lo = at("g_lo", [2, SEQ], 1536, F32R)
        tail = ar + 32768
        place_t = at("place_t", [2, SEQ], tail, BF16)
        gate_p = at("gate_p", [3, SEQ], tail + 256, BF16)
        iota_b = at("iota_b", [P], tail + 640, BF16)
        g_hi = at("g_hi", [2, SEQ], tail + 768, F32R)
        fing = at("fing", [D], ar + 9216)

        pp = ctx.enter_context(nc.psum_tensor("pp", [P, 4, 512], F32))
        pm = ctx.enter_context(nc.psum_tensor("pm", [P, 4, 512], F32))

        class Signal:

            def __init__(self, name, per_layer, start=0):
                self.sem = ctx.enter_context(nc.semaphore(name))
                self.per, self.start = per_layer, start

            def at(self, l, n):
                return l * self.per + (n + self.start)

        sg_raw = [Signal(f"raw_landed{s}", 16 * slot_units(s)) for s in range(RING)]
        sg_hi = Signal("high_ready", UNITS, 1)
        sg_lo = [Signal(f"low_ready{s}", slot_units(s), 1) for s in range(RING)]
        sg_used = Signal("unit_used", UNITS, 1)
        sg_sq, sg_root, sg_rstd, sg_xn = (Signal(n, 2) for n in ("squares", "roots", "rstd_ready", "xn_ready"))
        sg_turn, sg_hh, sg_hl = Signal("xn_turned", 8), Signal("h_high", 16), Signal("h_low", 16)
        sg_ev, sg_cv, sg_xs, sg_ql = Signal("chunk_out", 28), Signal("conv_step", 128), Signal("conv_silu", 4), Signal("query_low", 4)
        sg_dt, sg_dta, sg_dtp = Signal("dt_vector", 4), Signal("dt_scalar", 5), Signal("dt_sums", 1)
        sg_as, sg_ab, sg_am, sg_ae, sg_ar = Signal("a_scores", 18), Signal("a_biased", 18), Signal("a_max", 6), Signal("a_exp", 6), Signal("a_scaled", 12)
        sg_at, sg_ap, sg_apv, sg_ay = Signal("a_turned", 18), Signal("a_turned_out", 18), Signal("a_mixed", 6), Signal("a_out", 6)
        sg_cz, sg_cl, sg_csp, sg_cc = Signal("c_scores", 18), Signal("c_log", 54), Signal("c_softplus", 18), Signal("c_summed", 18)
        sg_cw, sg_cpv, sg_cy = Signal("c_weights", 18), Signal("c_mixed", 9), Signal("c_out", 9)
        sg_sr, sg_s1, sg_sgm, sg_se, sg_sb = Signal("s_steps", 16), Signal("s_turned", 16), Signal("s_segments", 16), Signal("s_decay", 16), Signal("s_bt_out", 8)
        sg_sc, sg_sx, sg_sm, sg_s2, sg_st, sg_sd = Signal("s_cb_out", 16), Signal("s_inputs", 16), Signal("s_masked", 16), Signal("s_products", 16), Signal("s_state_out", 8), Signal("s_sum", 48)
        sg_yh, sg_yl = Signal("y_high", 3), Signal("y_low", 3)
        sg_bq, sg_br, sg_bt, sg_bh, sg_bl = Signal("b_squares", 3), Signal("b_rstd", 1), Signal("b_turned", 16), Signal("b_high", 16), Signal("b_low", 16)
        sg_mg, sg_mt = Signal("merged_c", 4), Signal("merge_step", 16)
        sg_mtt, sg_mh, sg_ml, sg_xa = Signal("merged_turned", 8), Signal("merged_high", 8), Signal("merged_low", 8), Signal("x_added", 2, 1)
        sg_kv = Signal("key_scores_out", 4)
        n_tk = 5 * 32 + 1 + 2 * (1 + 5 * 8) + 3 + 12 + 4
        sg_tk, sg_gx, sg_ix, sg_ixe = Signal("retrieval_step", n_tk), Signal("gate_exp", 1), Signal("picks_turned", 1), Signal("picks_out", 8)
        sg_xj, sg_hc = Signal("x_joined", 1), Signal("hot_columns", 2 * BATCHES)
        sg_hot, sg_rt, sg_free = Signal("one_hots", 2 * BATCHES), Signal("routes", 2 * BATCHES, 2), Signal("route_banks_free", 2 * GROUPS_OF_ROUTES, 2)
        sg_ge, sg_gl = Signal("gelu", KEYS), Signal("weighted", 3 * FIRST)
        sg_wm, sg_gh, sg_gw = Signal("hidden_weighted", FIRST // 4), Signal("hidden_high", FIRST), Signal("hidden_low", FIRST)
        s_init = ctx.enter_context(nc.semaphore("init_landed"))
        s_apart = ctx.enter_context(nc.semaphore("apart"))
        INIT = 5 * 16
        sg_mix = Signal("mix_constants", 48)
        s_fin = ctx.enter_context(nc.semaphore("final_step"))
        s_fina = ctx.enter_context(nc.semaphore("final_scalar"))
        s_out = ctx.enter_context(nc.semaphore("out_stored"))
        s_fg = ctx.enter_context(nc.semaphore("final_g_landed"))

        def final_of(n):
            return 6 * (n // 2) + (2 if n % 2 == 0 else 6)

        def a_head(j, g):
            h = g * A_SLOTS + j
            return h // 2, HD * (h % 2), HD * h

        def down_v(j):
            return 0 if j == 0 else 2 * j - 1

        def up_v(j):
            return 2 * j + 2 if j < FIRST - 1 else 2 * FIRST - 1

        block = ctx.enter_context(nc.Block())

        @block.sync
        def _(sp):
            sp.dma_start(x[:], x_in.rearrange("(a p) d -> p a d", p=P)).then_inc(s_init, 16)
            sp.dma_start(ident[:], ident_in).then_inc(s_init, 16)
            sp.dma_start(iota[:], iota_in).then_inc(s_init, 16)
            sp.dma_start(fmp[:], fm_params.rearrange("l p n -> p l n")).then_inc(s_init, 16)
            with sp.Fori(0, LAYERS) as l:
                for s in range(RING):
                    sp.wait_ge(sg_lo[s].sem, sg_lo[s].at(l, 0))
                    sp.dma_start(raw[:, s, :], stream[bass.ds(l * UNITS + s, 1)].rearrange("o p n -> p (o n)")).then_inc(sg_raw[s].sem, 16)
                with sp.Fori(1, UNITS // RING) as i:
                    for s in range(RING):
                        sp.wait_ge(sg_lo[s].sem, sg_lo[s].at(l, i))
                        sp.dma_start(raw[:, s, :], stream[bass.ds(l * UNITS + RING * i + s, 1)].rearrange("o p n -> p (o n)")).then_inc(sg_raw[s].sem, 16)
                for u in range(UNITS // RING * RING, UNITS):
                    sp.wait_ge(sg_lo[u % RING].sem, sg_lo[u % RING].at(l, u // RING))
                    sp.dma_start(raw[:, u % RING, :], stream[bass.ds(l * UNITS + u, 1)].rearrange("o p n -> p (o n)")).then_inc(sg_raw[u % RING].sem, 16)
            sp.wait_ge(s_fin, 4)
            sp.dma_start(out.rearrange("(a p) d -> p a d", p=P), xn[:]).then_inc(s_out, 16)
            sp.wait_ge(s_out, 16)

        @block.gpsimd
        def _(pool):
            with pool.Fori(0, LAYERS) as l:
                pool.wait_ge(sg_xa.sem, sg_xa.at(l, 0))
                pool.sem_inc(s_apart)
                pool.dma_start(mixf[:], mix_f32).then_inc(sg_mix.sem, 16)
                pool.dma_start(mixb[:], mix_bf16.rearrange("p (a n) -> p a n", a=2)).then_inc(sg_mix.sem, 16)
                pool.dma_start(rows[:], row_params[bass.ds(l, 1)].rearrange("o p n -> p (o n)")).then_inc(sg_mix.sem, 16)

                def low(s, hi_count):
                    pool.wait_ge(sg_hi.sem, sg_hi.at(l, hi_count))
                    pool.tensor_tensor(w_lo[:, s, :], raw[:, s, :], w_hi[:, s, :].bitcast(F32), ALU.subtract).then_inc(sg_lo[s].sem, 1)

                with pool.Fori(LOW_POOL // RING, LOW_MIXED // RING) as i:
                    for s in range(RING):
                        low(s, RING * i + (s + 1))
                wait_first = sg_gw.at(l, FIRST // 2)
                pool.wait_ge(sg_gw.sem, wait_first)
                pool.sem_inc(s_apart)
                with pool.Fori(0, FIRST // 2 // RING) as i:
                    for r in range(RING):
                        j = RING * i + (r + FIRST // 2)
                        pool.wait_ge(sg_gh.sem, sg_gh.at(l, j + 1))
                        pool.tensor_tensor(g_lo[:, r % 2, :], hid[:, bass.ds(j, 1), :].rearrange("p o t -> p (o t)"),
                                           g_hi[:, r % 2, :].bitcast(F32), ALU.subtract).then_inc(sg_gw.sem, 1)
                        low((LOW_MIXED + r) % RING, RING * i + (LOW_MIXED + r + 1))
                for u in range(LOW_MIXED + FIRST // 2, U_S + RING):
                    low(u % RING, u + 1)
            pool.wait_ge(sg_xa.sem, sg_xa.at(LAYERS, 0))
            pool.dma_start(fing[:], final_g).then_inc(s_fg, 16)

        @block.tensor
        def _(pe):
            pe.sem_inc(sg_used.sem, sg_used.start)
            pe.sem_inc(sg_rt.sem, sg_rt.start)
            pe.wait_ge(s_init, INIT)
            with pe.Fori(0, LAYERS) as l:

                def wait(sig, n):
                    pe.wait_ge(sig.sem, sig.at(l, n))

                def transpose(dst, src):
                    return pe.transpose(dst, src, ident[0:src.shape[0], 0:src.shape[0]])

                def unit_ready(u):
                    wait(sg_lo[u % RING], u // RING + 1)

                def chunk_unit_fm(c, q, rhs_hi, rhs_lo):
                    u = chunk_of_stream(c) + q
                    unit_ready(u)
                    pair = c % 2
                    for s in range(2):
                        for m in range(4):
                            dst = pp[:, 2 * pair + m // 2, SEQ * (m % 2):SEQ * (m % 2 + 1)]
                            col = slice(CW * s + P * m, CW * s + P * (m + 1))
                            wh, wl = w_hi[:, u % RING, col], w_lo[:, u % RING, col]
                            k = 2 * q + s
                            pe.matmul(dst, wh, rhs_hi[:, k, :], start=(k == 0 and m % 2 == 0), stop=False, skip_group_check=True)
                            pe.matmul(dst, wh, rhs_lo[:, k, :], start=False, stop=False, skip_group_check=True)
                            last = pe.matmul(dst, wl, rhs_hi[:, k, :], start=False, stop=(k == KD - 1), skip_group_check=True)
                    last.then_inc(sg_used.sem, 1)

                def chunk_unit_tm(c, q):
                    u = chunk_of_stream(c) + q
                    unit_ready(u)
                    pair = c % 2
                    for s in range(2):
                        k = 2 * q + s
                        col = slice(CW * s, CW * (s + 1))
                        for t in range(TT):
                            tok = slice(P * t, P * (t + 1))
                            dst = pp[:, 2 * pair + t, :]
                            pe.matmul(dst, h_hi[:, k, tok], w_hi[:, u % RING, col], start=(k == 0), stop=False)
                            pe.matmul(dst, h_hi[:, k, tok], w_lo[:, u % RING, col], start=False, stop=False)
                            last = pe.matmul(dst, h_lo[:, k, tok], w_hi[:, u % RING, col], start=False, stop=(k == KD - 1))
                    last.then_inc(sg_used.sem, 1)

                def pair_free(c):
                    if c in (0, 1):
                        return
                    if c in (CHUNKS, CHUNKS + 1):
                        return
                    b = c - 2
                    if C_X <= b < C_Z:
                        wait(sg_cv, 16 * (b - C_X + 1))
                    elif b < C_X:
                        wait(sg_ev, b + 1)
                    elif b < CHUNKS:
                        wait(sg_ev, b + 1 - X_CH)
                    else:
                        wait(sg_ql, b - CHUNKS + 1)

                def slab_unit(u, k, lhs_hi, lhs_lo, start, stop):
                    unit_ready(u)
                    for t in range(TT):
                        tok = slice(P * t, P * (t + 1))
                        for half in range(2):
                            col = slice(CW * half, CW * (half + 1))
                            dst = pp[:, 2 * t + half, :]
                            pe.matmul(dst, lhs_hi[:, k, tok], w_hi[:, u % RING, col], start=start, stop=False)
                            pe.matmul(dst, lhs_hi[:, k, tok], w_lo[:, u % RING, col], start=False, stop=False)
                            last = pe.matmul(dst, lhs_lo[:, k, tok], w_hi[:, u % RING, col], start=False, stop=stop)
                    last.then_inc(sg_used.sem, 1)

                def norm(n):
                    wait(sg_xn, n + 1)
                    for b in range(4):
                        for k in (2 * b, 2 * b + 1):
                            for t in range(TT):
                                last = transpose(pm[:, b, SEQ * (k % 2) + P * t:SEQ * (k % 2) + P * (t + 1)], xn[:, t, P * k:P * (k + 1)])
                        last.then_inc(sg_turn.sem, 1)

                def dt_sums(_n):
                    wait(sg_mix, 48)
                    wait(sg_dt, 3)
                    pe.matmul(pm[:, 3, 0:SSD_H], lower, da[:, 1, :], start=True, stop=True)
                    pe.matmul(pm[:, 3, SSD_H:2 * SSD_H], upper, da[:, 0, :], start=True, stop=True).then_inc(sg_dtp.sem, 1)

                def a_score(j):
                    wait(sg_ev, C_QK + 5)
                    for g in range(A_GROUPS):
                        if j == 0:
                            wait(sg_hl, 8)
                        else:
                            wait(sg_ap, 3 * (j - 1) + g + 1)
                        tile, part, _ = a_head(j, g)
                        row = slice(part, part + HD)
                        q, k = qk[row, tile, :], qk[row, 9 + tile, :]
                        pe.matmul(pm[:, g, 0:P], q[:, 0:P], k[:, 0:P], start=True, stop=True)
                        pe.matmul(pm[:, g, P:3 * P], q[:, P:SEQ], k[:, 0:SEQ], start=True, stop=True).then_inc(sg_as.sem, 1)

                def a_turn(j):
                    wait(sg_ar, 2 * j + 2)
                    for g in range(A_GROUPS):
                        for b in range(3):
                            last = transpose(pm[:, g, P * b:P * (b + 1)], a_p[:, g, P * b:P * (b + 1)])
                        last.then_inc(sg_at.sem, 1)

                def a_mix(j):
                    wait(sg_ap, 3 * j + 3)
                    if j == 0:
                        wait(sg_dta, 5)
                    else:
                        wait(sg_ay, j)
                    part = HD * (j % 2)
                    dst = pm[part:part + HD, 3, :]
                    for g in range(A_GROUPS):
                        _, _, col = a_head(j, g)
                        pe.matmul(dst[:, 0:SEQ], v[:, 0, col:col + HD], a_pt[:, g, 0:SEQ], start=(g == 0), stop=False)
                        last = pe.matmul(dst[:, P:SEQ], v[:, 1, col:col + HD], a_pt[:, g, SEQ:3 * P], start=False, stop=(g == A_GROUPS - 1))
                    last.then_inc(sg_apv.sem, 1)

                def c_score(p):
                    wait(sg_ev, C_X)
                    for i in range(2):
                        h = 2 * p + i
                        if p == 0:
                            wait(sg_ap, 18)
                        else:
                            wait(sg_cw, h - 1)
                        row = slice(HD * i, HD * i + HD)
                        q, k = qk[row, 18 + p, :], qk[row, 27 + p, :]
                        pe.matmul(pm[:, i, 0:SEQ], k[:, 0:P], q, start=True, stop=False, skip_group_check=True)
                        pe.matmul(pm[:, i, SEQ:3 * P], k[:, P:SEQ], q[:, P:SEQ], start=False, stop=False, skip_group_check=True)
                        pe.matmul(pm[:, i, 0:P], mixb[:, 1, :], mixb[:, 0, :], start=False, stop=False, skip_group_check=True)
                        pe.matmul(pm[:, i, SEQ:3 * P], mixb[:, 1, :], mixb[:, 0, :], start=False, stop=False, skip_group_check=True).then_inc(sg_cz.sem, 1)

                def c_sum(p):
                    for i in range(2):
                        wait(sg_csp, 2 * p + i + 1)
                        pe.matmul(pm[:, i, 0:3 * P], neg_ge, c_sp[:, i, :], start=False, stop=False, skip_group_check=True)
                        pe.matmul(pm[:, i, P:SEQ], neg_one, c_sp[:, i, SEQ:3 * P], start=False, stop=True, skip_group_check=True).then_inc(sg_cc.sem, 1)

                def c_mix(p):
                    wait(sg_cw, 2 * p + 2)
                    if p >= 1:
                        wait(sg_cy, p)
                    for i in range(2):
                        dst = pm[HD * i:HD * (i + 1), 2, :]
                        col = A_W + HD * (2 * p + i)
                        pe.matmul(dst[:, 0:SEQ], v[:, 0, col:col + HD], c_w[:, i, 0:SEQ], start=True, stop=False)
                        last = pe.matmul(dst[:, P:SEQ], v[:, 1, col:col + HD], c_w[:, i, SEQ:3 * P], start=False, stop=True)
                    last.then_inc(sg_cpv.sem, 1)

                def ssd(n):
                    if n < 2 * GROUPS:
                        g, t = n // 2, n % 2
                        tok = slice(P * t, P * (t + 1))
                        wait(sg_xs, 4)
                        if n < 2:
                            wait(sg_cw, 18)
                        else:
                            wait(sg_sx, n - 1)
                        if n >= 2 and t == 0:
                            wait(sg_sb, g)
                        b = pm[:, t, :]
                        transpose(b[:, 0:P], xt[:, 2 * g, tok])
                        transpose(b[:, P:2 * P], xt[:, 2 * g + 1, tok])
                        bm, cm = xt[:, 16 + g, tok], xt[:, 24 + g, tok]
                        last = pe.matmul(b[:, 2 * P:3 * P], bm, cm, start=True, stop=True)
                        if t == 0:
                            last = transpose(b[:, 3 * P:4 * P], bm)
                        last.then_inc(sg_s1.sem, 1)
                        wait(sg_sr, n + 1)
                        if n == 0:
                            wait(sg_cy, 9)
                        else:
                            wait(sg_se, n)
                        pe.matmul(pm[:, 2, :], upper, s_r[:].rearrange("p h t -> p (h t)"), start=True, stop=True).then_inc(sg_sgm.sem, 1)
                    if n >= 1:
                        m = n - 1
                        g, t = m // 2, m % 2
                        wait(sg_sm, m + 1)
                        wait(sg_sx, m + 1)
                        if m == 0:
                            wait(sg_ay, 6)
                        else:
                            wait(sg_sd, final_of(m - 1))
                        if g + t:
                            wait(sg_st, g + t)
                        if t == 0:
                            wait(sg_sb, g + 1)
                        for h in range(HPG):
                            pe.matmul(pm[:, 3, HD * h:HD * (h + 1)], s_e[:, t, h, :], s_xdt[:, t, h, :], start=True, stop=True)
                        if t == 0:
                            last = pe.matmul(pm[:, 3, 256:512], s_bt[:], s_xdd[:].rearrange("p h d -> p (h d)"), start=True, stop=True)
                        else:
                            last = pe.matmul(pm[:, 3, 256:512], xt[:, 24 + g, P:SEQ], s_state[:].rearrange("p h d -> p (h d)"), start=True, stop=True)
                        last.then_inc(sg_s2.sem, 1)

                def turn_b(k):
                    wait(sg_sd, 48)
                    if k >= 4:
                        wait(sg_bl, k - 3)
                    for t in range(TT):
                        last = transpose(pm[:, k % 4, P * t:P * (t + 1)], z[:, t, P * k:P * (k + 1)])
                    last.then_inc(sg_bt.sem, 1)

                def turn_merged(_n):
                    wait(sg_mt, 16)
                    wait(sg_bl, 16)
                    for k in range(KD):
                        for t in range(TT):
                            last = transpose(pm[:, k // 2, SEQ * (k % 2) + P * t:SEQ * (k % 2) + P * (t + 1)], merged[:, t, P * k:P * (k + 1)])
                        last.then_inc(sg_mtt.sem, 1)

                steps = {"norm": norm, "dt": dt_sums, "a_score": a_score, "a_turn": a_turn, "a_mix": a_mix,
                         "c_score": c_score, "c_sum": c_sum, "c_mix": c_mix, "ssd": ssd, "turn_b": turn_b,
                         "turn_merged": turn_merged}

                def between(u):
                    for name, arg in ORDER[u]:
                        if name in steps:
                            steps[name](arg)

                norm(0)
                wait(sg_hl, 8)
                for c in range(CHUNKS):
                    pair_free(c)
                    for q in range(4):
                        if C_QK <= c < C_Z:
                            chunk_unit_fm(c, q, h_hi, h_lo)
                        else:
                            chunk_unit_tm(c, q)
                        between(4 * c + q)
                wait(sg_ev, 24)
                wait(sg_yl, 3)
                for u in range(U_C, U_A):
                    k = u - U_C
                    slab_unit(u, 3 + k, yt_hi, yt_lo, k == 0, u == U_A - 1)
                    between(u)
                wait(sg_mg, 4)
                for u in range(U_A, U_B):
                    k = u - U_A
                    slab_unit(u, k, yt_hi, yt_lo, k == 0, u == U_B - 1)
                    between(u)
                wait(sg_mt, 8)
                for u in range(U_B, U_O):
                    k = u - U_B
                    wait(sg_bl, k + 1)
                    slab_unit(u, k, yb_hi, yb_lo, k == 0, u == U_O - 1)
                    between(u)
                for u in range(U_O, U_Q):
                    k = u - U_O
                    wait(sg_ml, k + 1)
                    slab_unit(u, k, m_hi, m_lo, k == 0, u == U_Q - 1)
                    between(u)
                def key_scores(b, banks):
                    u = U_K[b]
                    unit_ready(u)
                    wait(sg_ql, 2 * b + 2)
                    for t in range(TT):
                        tok = slice(P * t, P * (t + 1))
                        for i in range(8):
                            hc = 8 * b + i
                            col = slice(P * i, P * (i + 1))
                            dst = banks[:, 2 * t + i // 4, P * (i % 4):P * (i % 4 + 1)]
                            pe.matmul(dst, q_hi[:, hc, tok], w_hi[:, u % RING, col], start=True, stop=False)
                            pe.matmul(dst, q_hi[:, hc, tok], w_lo[:, u % RING, col], start=False, stop=False)
                            last = pe.matmul(dst, q_lo[:, hc, tok], w_hi[:, u % RING, col], start=False, stop=True)
                    last.then_inc(sg_used.sem, 1)

                wait(sg_hl, 16)
                for c in range(CHUNKS, CHUNKS + 4):
                    pair_free(c)
                    for q in range(4):
                        chunk_unit_fm(c, q, h_hi, h_lo)
                        between(chunk_of_stream(c) + q)
                    if c % 2 == 1:
                        key_scores((c - CHUNKS) // 2, pm if c == CHUNKS + 1 else pp)

                def down(slot, turn, bank, midway=None):
                    pe.wait_ge(sg_lo[slot].sem, sg_lo[slot].at(l, turn))
                    for k in range(KD):
                        if midway and k == KD // 2:
                            midway()
                        col = slice(P * k, P * (k + 1))
                        wh, wl = w_hi[:, slot, col], w_lo[:, slot, col]
                        dst = pm[:, bank, 0:SEQ]
                        pe.matmul(dst, wh, h_hi[:, k, :], start=(k == 0), stop=False)
                        pe.matmul(dst, wh, h_lo[:, k, :], start=False, stop=False)
                        last = pe.matmul(dst, wl, h_hi[:, k, :], start=False, stop=(k == KD - 1))
                    last.then_inc(sg_used.sem, 1)

                def up(slot, turn, lhs_hi, lhs_lo, stop=False, midway=None):
                    pe.wait_ge(sg_lo[slot].sem, sg_lo[slot].at(l, turn))
                    for t in range(TT):
                        if midway and t == 1:
                            midway()
                        tok = slice(P * t, P * (t + 1))
                        for half in range(2):
                            col = slice(CW * half, CW * (half + 1))
                            dst = pp[:, 2 * t + half, :]
                            pe.matmul(dst, lhs_hi[:, tok], w_hi[:, slot, col], start=False, stop=False, skip_group_check=True)
                            pe.matmul(dst, lhs_hi[:, tok], w_lo[:, slot, col], start=False, stop=False, skip_group_check=True)
                            last = pe.matmul(dst, lhs_lo[:, tok], w_hi[:, slot, col], start=False, stop=stop, skip_group_check=True)
                    last.then_inc(sg_used.sem, 1)

                def routes(half, n, bank, b):
                    if b == 0:
                        pe.wait_ge(sg_free.sem, sg_free.at(l, n + (GROUPS_OF_ROUTES * half - 1)))
                    pe.wait_ge(sg_hot.sem, sg_hot.at(l, 2 * n + (BATCHES * half + b + 1)))
                    for r in range(HOT):
                        c = FIRST * (HOT * b + r)
                        for part in range(3):
                            last = pe.matmul(pm[:, 2 + bank, c:c + FIRST], hot_r[:, b, r, :], hot_c[:, b, part, r, :], start=(part == 0), stop=(part == 2))
                    last.then_inc(sg_rt.sem, 1)

                wait(sg_kv, 2)
                for j in range(RING):
                    if j >= 2:
                        wait(sg_ge, j - 1)
                    down((U_E + j) % RING, (U_E + j) // RING + 1, j % 2)
                wait(sg_kv, 4)
                for t in range(TT):
                    for half in range(2):
                        last = pe.matmul(pp[:, 2 * t + half, :], ident[:], x[:, t, CW * half:CW * (half + 1)], start=True, stop=False, skip_group_check=True)
                last.then_inc(sg_xj.sem, 1)

                def first_down(i, r, midway=None):
                    pe.wait_ge(sg_ge.sem, sg_ge.at(l, RING * i + (r - 1)))
                    down((U_E + r) % RING, i + ((U_E + r) // RING + 1), r % 2, midway)

                with pe.Fori(1, AHEAD // RING) as i:
                    for r in range(RING):
                        first_down(i, r)
                wait(sg_tk, n_tk)
                for i in range(3):
                    for t in range(TT):
                        last = transpose(pm[:, 2 + i // 2, SEQ * (i % 2) + P * t:SEQ * (i % 2) + P * (t + 1)], pick[:, i, t].rearrange("p h k -> p (h k)"))
                last.then_inc(sg_ix.sem, 1)
                wait(sg_ixe, 2)
                pe.sem_inc(s_apart)
                with pe.Fori(AHEAD // RING, FIRST // RING) as i:
                    for r in range(RING):
                        n = RING * i + (r - AHEAD)
                        routes(0, n, r % 2, 0)
                        first_down(i, r, midway=lambda: routes(0, n, r % 2, 1))

                def first_up(i, r, midway=None):
                    pe.wait_ge(sg_gw.sem, sg_gw.at(l, RING * i + (r + 1)))
                    up((U_U + r) % RING, i + ((U_U + r) // RING + 1), g_hi[:, r % 2, :], g_lo[:, r % 2, :], midway=midway)

                with pe.Fori(0, FIRST // RING // 2) as i:
                    for r in range(RING):
                        first_up(i, r)
                with pe.Fori(FIRST // RING // 2, FIRST // RING) as i:
                    for r in range(RING):
                        n = RING * i + (r - FIRST // 2)
                        routes(1, n, r % 2, 0)
                        first_up(i, r, midway=lambda: routes(1, n, r % 2, 1))

                def other_down(i, v, j, bank):
                    pe.wait_ge(sg_ge.sem, sg_ge.at(l, j + (FIRST - 1)))
                    down((U_S + v) % RING, i + ((U_S + v) // RING + 1), bank)

                def other_up(i, v, j, buf, stop=False):
                    pe.wait_ge(sg_gl.sem, sg_gl.at(l, 3 * j + 3))
                    up((U_S + v) % RING, i + ((U_S + v) // RING + 1), g_hi[:, buf, :], g_lo[:, buf, :], stop)

                other_down(0, 0, 0, 0)
                with pe.Fori(0, FIRST // 2 - 1) as i:
                    for r in range(2):
                        other_down(i, 2 * r + 1, 2 * i + (r + 1), (r + 1) % 2)
                        other_up(i, 2 * r + 2, 2 * i + r, r)
                i = FIRST // 2 - 1
                other_down(i, 1, FIRST - 1, 1)
                other_up(i, 2, FIRST - 2, 0)
                other_up(i, 3, FIRST - 1, 1, stop=True)

        @block.scalar
        def _(act):
            act.sem_inc(sg_free.sem, sg_free.start)
            act.sem_inc(sg_hi.sem, sg_hi.start)
            act.wait_ge(s_init, INIT)
            with act.Fori(0, LAYERS) as l:

                def wait(sig, n):
                    act.wait_ge(sig.sem, sig.at(l, n))

                def high(u):
                    act.wait_ge(sg_raw[u % RING].sem, sg_raw[u % RING].at(l, 16 * (u // RING + 1)))
                    wait(sg_used, max(u - RING + 1, 0))
                    act.activation(w_hi[:, u % RING, :], raw[:, u % RING, :], ACT.Copy).then_inc(sg_hi.sem, 1)

                def norm(n):
                    for t in range(TT):
                        last = act.activation(njunk[:, t, :], x[:, t, :], ACT.Square, accum_out=stat[:, t:t + 1])
                    last.then_inc(sg_sq.sem, 1)
                    wait(sg_sq, n + 1)
                    act.activation(stat[:, 2:4], stat[:, 0:2], ACT.Sqrt, scale=1.0 / D, bias=stat[:, 60:61]).then_inc(sg_root.sem, 1)
                    for k in range(KD):
                        if k % 2 == 0:
                            wait(sg_turn, 4 * n + k // 2 + 1)
                        act.activation(h_hi[:, k, :], pm[:, k // 2, SEQ * (k % 2):SEQ * (k % 2 + 1)], ACT.Copy,
                                       scale=fmp[:, bass.ds(l, 1), 8 * n + k]).then_inc(sg_hh.sem, 1)

                def evacuate(c):
                    if C_X <= c < C_Z:
                        return
                    wait(sg_used, chunk_of_stream(c) + 4)
                    pair = 2 * (c % 2)
                    for b in range(2):
                        src = pp[:, pair + b, :]
                        if c < C_QK:
                            w = min(CW, V_COLS - CW * c)
                            last = act.activation(v[:, b, CW * c:CW * c + w], src[:, 0:w], ACT.Copy)
                        elif c < C_X:
                            first = 4 * (c - C_QK) + 2 * b
                            for m in (0, 1):
                                is_q = (first + m) // 9 % 2 == 0
                                last = act.activation(qk[:, first + m, :], src[:, SEQ * m:SEQ * (m + 1)], ACT.Copy,
                                                      scale=HD ** -0.5 if is_q else 1.0)
                        elif c < C_G:
                            last = act.activation(z[:, b, CW * (c - C_Z):CW * (c - C_Z + 1)], src, ACT.Silu)
                        elif c < CHUNKS:
                            last = act.activation(gates[:, b, CW * (c - C_G):CW * (c - C_G + 1)], src, ACT.Sigmoid)
                        else:
                            tile = 4 * (c - CHUNKS) + 2 * b
                            last = act.activation(q_hi[:, tile:tile + 2, :].rearrange("p a t -> p (a t)"), src, ACT.Copy)
                    last.then_inc(sg_ev.sem, 1)
                    if C_Z <= c < C_G:
                        i = c - C_Z
                        wait(sg_cv, 128)
                        q = xt[:, 8 * i:8 * i + 8, :]
                        act.activation(q, q, ACT.Silu).then_inc(sg_xs.sem, 1)

                def dt_scalar(_n):
                    wait(sg_mix, 48)
                    act.activation(ea[:], rows[:, 32:64], ACT.Exp).then_inc(sg_dta.sem, 1)
                    wait(sg_dt, 1)
                    act.activation(dtt[:], dt[:], ACT.Abs).then_inc(sg_dta.sem, 1)
                    wait(sg_dta, 2)
                    act.activation(dtt[:], dtt[:], ACT.Exp, scale=-1.0).then_inc(sg_dta.sem, 1)
                    wait(sg_dta, 3)
                    act.activation(dtt[:], dtt[:], ACT.Ln, bias=1.0).then_inc(sg_dta.sem, 1)
                    wait(sg_dtp, 1)
                    act.activation(ed[:].rearrange("p a h -> p (a h)"), pm[:, 3, 0:64], ACT.Exp).then_inc(sg_dta.sem, 1)

                def a_score(j):
                    wait(sg_am, j + 1)
                    act.activation(a_p[:, :, 0:P], a_p[:, :, 0:P], ACT.Exp, bias=stat[:, 4:5], accum_out=stat[:, 6:7])
                    act.activation(a_p[:, :, P:3 * P], a_p[:, :, P:3 * P], ACT.Exp, bias=stat[:, 5:6], accum_out=stat[:, 7:8]).then_inc(sg_ae.sem, 1)

                def a_turn(j):
                    if j >= 1:
                        wait(sg_apv, j)
                    for g in range(A_GROUPS):
                        wait(sg_at, 3 * j + g + 1)
                        act.activation(a_pt[:, g, :], pm[:, g, 0:384], ACT.Copy).then_inc(sg_ap.sem, 1)

                def a_mix(j):
                    wait(sg_apv, j + 1)
                    row = slice(HD * (j % 2), HD * (j % 2) + HD)
                    act.activation(yt[row, j // 2, :], pm[row, 3, 0:SEQ], ACT.Copy).then_inc(sg_ay.sem, 1)

                def c_score(p):
                    for i in range(2):
                        h = 2 * p + i
                        wait(sg_cz, h + 1)
                        if p == 0:
                            wait(sg_apv, 6)
                        else:
                            wait(sg_cc, h - 1)
                        act.activation(c_sp[:, i, :], pm[:, i, 0:384], ACT.Abs).then_inc(sg_cl.sem, 1)
                    for i in range(2):
                        wait(sg_cl, 6 * p + i + 1)
                        act.activation(c_sp[:, i, :], c_sp[:, i, :], ACT.Exp, scale=-1.0).then_inc(sg_cl.sem, 1)
                    for i in range(2):
                        wait(sg_cl, 6 * p + i + 3)
                        act.activation(c_sp[:, i, :], c_sp[:, i, :], ACT.Ln, bias=1.0).then_inc(sg_cl.sem, 1)

                def c_sum(p):
                    if p >= 1:
                        wait(sg_cpv, p)
                    for i in range(2):
                        wait(sg_cc, 2 * p + i + 1)
                        act.activation(c_w[:, i, :], pm[:, i, 0:384], ACT.Exp).then_inc(sg_cw.sem, 1)

                def ssd(n):
                    if n < 2 * GROUPS:
                        t = n % 2
                        if t == 0:
                            wait(sg_s1, n + 1)
                            if n >= 2:
                                wait(sg_s2, n - 1)
                            act.activation(s_bt[:], pm[:, 0, 384:512], ACT.Copy).then_inc(sg_sb.sem, 1)
                        wait(sg_sgm, n + 1)
                        if n >= 2:
                            wait(sg_s2, n - 1)
                        act.activation(s_e[:, t].rearrange("p h t -> p (h t)"), pm[:, 2, :], ACT.Exp).then_inc(sg_se.sem, 1)
                    if n >= 1 and (n - 1) % 2 == 0:
                        wait(sg_s2, n)
                        act.activation(s_state[:].rearrange("p h d -> p (h d)"), pm[:, 3, 256:512], ACT.Copy).then_inc(sg_st.sem, 1)

                def split_y(i):
                    if i == 0:
                        wait(sg_cy, 9)
                        wait(sg_ay, 6)
                        wait(sg_cz, 18)
                    act.activation(yt_hi[:, 4 * i:4 * i + 4, :], yt[:, 4 * i:4 * i + 4, :], ACT.Copy).then_inc(sg_yh.sem, 1)

                def ssd_norm(_n):
                    wait(sg_sd, 48)
                    for t in range(TT):
                        act.activation(junk[:], z[:, t, :], ACT.Square, accum_out=stat[:, 8 + t:9 + t]).then_inc(sg_bq.sem, 1)
                        wait(sg_bq, t + 1)
                    act.activation(stat[:, 10:12], stat[:, 8:10], ACT.Sqrt, scale=1.0 / SSD_IN, bias=stat[:, 60:61]).then_inc(sg_bq.sem, 1)

                def turn_b(k):
                    wait(sg_bt, k + 1)
                    act.activation(yb_hi[:, k, :], pm[:, k % 4, 0:SEQ], ACT.Copy,
                                   scale=fmp[:, bass.ds(l, 1), 176 + k]).then_inc(sg_bh.sem, 1)

                def turn_merged(_n):
                    for k in range(KD):
                        wait(sg_mtt, k // 2 * 2 + 2)
                        act.activation(m_hi[:, k, :], pm[:, k // 2, SEQ * (k % 2):SEQ * (k % 2 + 1)], ACT.Copy).then_inc(sg_mh.sem, 1)

                def norm1(n):
                    wait(sg_xa, 1)
                    norm(n)

                def key_scores(b):
                    banks = pm if b == 0 else pp
                    wait(sg_used, U_K[b] + 1)
                    for t in range(TT):
                        act.activation(sc[:, t, 8 * b:8 * b + 8, :].rearrange("p a n -> p (a n)"),
                                       banks[:, 2 * t:2 * t + 2, :].rearrange("p a n -> p (a n)"), ACT.Copy).then_inc(sg_kv.sem, 1)

                steps = {"evacuate": evacuate, "dt": dt_scalar, "a_score": a_score, "a_turn": a_turn, "a_mix": a_mix,
                         "c_score": c_score, "c_sum": c_sum, "ssd": ssd, "split_y": split_y, "ssd_norm": ssd_norm,
                         "turn_b": turn_b, "turn_merged": turn_merged, "norm": norm1, "key_scores": key_scores}

                wait(sg_xa, 0)
                for u in range(RING):
                    high(u)
                norm(0)
                for u in range(U_E):
                    if u + RING < U_E + RING:
                        high(u + RING)
                    for name, arg in ORDER[u]:
                        if name in steps:
                            steps[name](arg)
                def expert_high(v, i=0):
                    slot = v % RING
                    act.wait_ge(sg_raw[slot].sem, sg_raw[slot].at(l, i * 16 + 16 * (v // RING + 1)))
                    act.wait_ge(sg_used.sem, sg_used.at(l, RING * i + (v - RING + 1)))
                    act.activation(w_hi[:, slot, :], raw[:, slot, :], ACT.Copy).then_inc(sg_hi.sem, 1)

                def first_down(i, r):
                    act.wait_ge(sg_used.sem, sg_used.at(l, RING * i + (U_E + r + 1)))
                    act.activation(hid[:, bass.ds(RING * i + r, 1), :].rearrange("p o t -> p (o t)"), pm[:, r % 2, 0:SEQ], ACT.Gelu).then_inc(sg_ge.sem, 1)
                    expert_high(U_E + r + RING, i)

                def routes(half, n, bank):
                    act.wait_ge(sg_rt.sem, sg_rt.at(l, 2 * n + (BATCHES * half + 2)))
                    act.activation(route[:, :, bass.ds(BANK_TOKENS * n, BANK_TOKENS)], pm[:, 2 + bank, :].rearrange("p (t j) -> p j t", j=FIRST), ACT.Copy).then_inc(sg_free.sem, 1)

                with act.Fori(0, GATE_EXP // RING) as i:
                    for r in range(RING):
                        first_down(i, r)
                wait(sg_tk, n_tk - 12 - 4)
                act.activation(pick[:, 2], pick[:, 2], ACT.Exp).then_inc(sg_gx.sem, 1)
                with act.Fori(GATE_EXP // RING, AHEAD // RING) as i:
                    for r in range(RING):
                        first_down(i, r)
                with act.Fori(AHEAD // RING, FIRST // RING) as i:
                    for r in range(RING):
                        routes(0, RING * i + (r - AHEAD), r % 2)
                        first_down(i, r)

                def hidden_high(i, r):
                    act.wait_ge(sg_wm.sem, sg_wm.at(l, i + (r // RING + 1)))
                    act.wait_ge(sg_used.sem, sg_used.at(l, RING * i + (U_U + r - 1)))
                    act.activation(g_hi[:, r % 2, :], hid[:, bass.ds(RING * i + r, 1), :].rearrange("p o t -> p (o t)"), ACT.Copy).then_inc(sg_gh.sem, 1)

                def first_up(i, r, last=False):
                    if not last:
                        hidden_high(i, r + 1)
                    expert_high(U_U + r + RING, i)

                hidden_high(0, 0)
                with act.Fori(0, FIRST // RING // 2) as i:
                    for r in range(RING):
                        first_up(i, r)

                def ups_with_routes(i, last):
                    for r in range(RING):
                        routes(1, RING * i + (r - FIRST // 2), r % 2)
                        first_up(i, r, last and r == RING - 1)

                with act.Fori(FIRST // RING // 2, FIRST // RING - 1) as i:
                    ups_with_routes(i, False)
                ups_with_routes(FIRST // RING - 1, True)

                def gelu(i, v, buf):
                    act.wait_ge(sg_used.sem, sg_used.at(l, RING * i + (U_S + v + 1)))
                    act.activation(g_act[:, buf, :], pm[:, buf, 0:SEQ], ACT.Gelu).then_inc(sg_ge.sem, 1)

                gelu(0, 0, 0)
                expert_high(U_S + 4)
                gelu(0, 1, 1)
                expert_high(U_S + 5)
                expert_high(U_S + 6)
                with act.Fori(1, FIRST // 2 - 1) as i:
                    for r in range(2):
                        gelu(i, 2 * r - 1, r)
                        expert_high(U_S + 2 * r + 3, i)
                        expert_high(U_S + 2 * r + 4, i)
                gelu(0, down_v(FIRST - 2), 0)
                expert_high(U_S + 2 * FIRST - 1)
                gelu(0, down_v(FIRST - 1), 1)
            act.wait_ge(sg_xa.sem, sg_xa.at(LAYERS, 0))
            for t in range(TT):
                last = act.activation(njunk[:, t, :], x[:, t, :], ACT.Square, accum_out=stat[:, t:t + 1])
            last.then_inc(s_fina, 1)
            act.wait_ge(s_fina, 1)
            act.activation(stat[:, 2:4], stat[:, 0:2], ACT.Sqrt, scale=1.0 / D, bias=stat[:, 60:61]).then_inc(s_fina, 1)

        @block.vector
        def _(dve):
            for s in range(RING):
                dve.sem_inc(sg_lo[s].sem, sg_lo[s].start)
            dve.sem_inc(sg_xa.sem, sg_xa.start)
            dve.memset(stat[:], EPS).then_inc(s_init, 16)
            slopes = [2.0 ** (-8.0 * (h + 1) / A_HEADS) for h in range(A_HEADS)]
            dve.wait_ge(s_init, INIT)
            with dve.Fori(0, LAYERS) as l:

                def wait(sig, n):
                    dve.wait_ge(sig.sem, sig.at(l, n))

                def low(u):
                    wait(sg_hi, u + 1)
                    dve.tensor_tensor(w_lo[:, u % RING, :], raw[:, u % RING, :], w_hi[:, u % RING, :].bitcast(F32), ALU.subtract).then_inc(sg_lo[u % RING].sem, 1)

                def norm(n):
                    wait(sg_root, n + 1)
                    dve.reciprocal(stat[:, 12:14], stat[:, 2:4]).then_inc(sg_rstd.sem, 1)
                    wait(sg_rstd, n + 1)
                    for t in range(TT):
                        last = dve.tensor_scalar(xn[:, t, :], x[:, t, :], stat[:, 12 + t:13 + t], None, ALU.mult)
                    last.then_inc(sg_xn.sem, 1)
                    for k in range(KD):
                        wait(sg_hh, 8 * n + k // 2 * 2 + 2)
                        dve.scalar_tensor_tensor(h_lo[:, k, :], pm[:, k // 2, SEQ * (k % 2):SEQ * (k % 2 + 1)],
                                                 fmp[:, bass.ds(l, 1), 8 * n + k], h_hi[:, k, :].bitcast(F32), ALU.mult, ALU.subtract).then_inc(sg_hl.sem, 1)

                def evacuate(c):
                    if c >= CHUNKS:
                        wait(sg_ev, c - X_CH + 1)
                        for b in range(2):
                            tile = 4 * (c - CHUNKS) + 2 * b
                            last = dve.tensor_tensor(q_lo[:, tile:tile + 2, :].rearrange("p a t -> p (a t)"), pp[:, 2 * (c % 2) + b, :],
                                                     q_hi[:, tile:tile + 2, :].rearrange("p a t -> p (a t)").bitcast(F32), ALU.subtract)
                        last.then_inc(sg_ql.sem, 1)
                    if not C_X <= c < C_Z:
                        return
                    wait(sg_used, 4 * c + 4)
                    for tap in range(4):
                        for m in range(4):
                            ch = 4 * (c - C_X) + m
                            src = pp[:, 2 * (c % 2) + m // 2, SEQ * (m % 2):SEQ * (m % 2 + 1)]
                            wk = fmp[:, bass.ds(l, 1), 16 + 4 * ch + 3 - tap]
                            if tap == 0:
                                ins = dve.tensor_scalar(xt[:, ch, :], src, wk, fmp[:, bass.ds(l, 1), 144 + ch], ALU.mult, ALU.add)
                            else:
                                wait(sg_cv, 16 * (c - C_X) + 4 * (tap - 1) + m + 1)
                                ins = dve.scalar_tensor_tensor(xt[:, ch, tap:SEQ], src[:, 0:SEQ - tap], wk, xt[:, ch, tap:SEQ], ALU.mult, ALU.add)
                            ins.then_inc(sg_cv.sem, 1)

                def dt_vector(_n):
                    wait(sg_ev, V_CH)
                    wait(sg_mix, 48)
                    dve.tensor_tensor(dt[:], v[:, :, 2 * A_W:V_COLS], rows[:, 0:32].unsqueeze(1).broadcast_to([P, TT, SSD_H]), ALU.add).then_inc(sg_dt.sem, 1)
                    wait(sg_dta, 4)
                    dve.scalar_tensor_tensor(dt[:], dt[:], 0.0, dtt[:], ALU.max, ALU.add).then_inc(sg_dt.sem, 1)
                    wait(sg_dt, 2)
                    dve.scalar_tensor_tensor(da[:], dt[:], -1.0, ea[:].unsqueeze(1).broadcast_to([P, TT, SSD_H]), ALU.mult, ALU.mult).then_inc(sg_dt.sem, 1)
                    wait(sg_dta, 5)
                    dve.tensor_tensor(dtd[:], dt[:, 0, :], ed[:, 1, :], ALU.mult).then_inc(sg_dt.sem, 1)

                def a_score(j):
                    for g in range(A_GROUPS):
                        wait(sg_as, 3 * j + g + 1)
                        if j >= 1 and g == 0:
                            wait(sg_at, 3 * j)
                        dve.scalar_tensor_tensor(a_p[:, g, :], dist[:, g, :], slopes[g * A_SLOTS + j], pm[:, g, 0:384], ALU.mult, ALU.add).then_inc(sg_ab.sem, 1)
                    wait(sg_ab, 3 * j + 3)
                    dve.tensor_reduce(stat[:, 4:5], a_p[:, :, 0:P], AX.XY, ALU.max, negate=True)
                    dve.tensor_reduce(stat[:, 5:6], a_p[:, :, P:3 * P], AX.XY, ALU.max, negate=True).then_inc(sg_am.sem, 1)
                    wait(sg_ae, j + 1)
                    dve.reciprocal(stat[:, 14:16], stat[:, 6:8]).then_inc(sg_ar.sem, 1)
                    wait(sg_ar, 2 * j + 1)
                    dve.tensor_scalar(a_p[:, :, 0:P], a_p[:, :, 0:P], stat[:, 14:15], None, ALU.mult)
                    dve.tensor_scalar(a_p[:, :, P:3 * P], a_p[:, :, P:3 * P], stat[:, 15:16], None, ALU.mult).then_inc(sg_ar.sem, 1)

                def c_score(p):
                    for i in range(2):
                        wait(sg_cl, 6 * p + i + 5)
                        dve.scalar_tensor_tensor(c_sp[:, i, :], pm[:, i, 0:384], 0.0, c_sp[:, i, :], ALU.max, ALU.add).then_inc(sg_csp.sem, 1)

                def c_mix(p):
                    wait(sg_cpv, p + 1)
                    dve.tensor_copy(yt[:, 3 + p, :], pm[:, 2, 0:SEQ]).then_inc(sg_cy.sem, 1)

                def scan_steps(n):
                    g, t = n // 2, n % 2
                    if n == 0:
                        wait(sg_cy, 9)
                    else:
                        wait(sg_sgm, n)
                    dve.tensor_tensor(s_r[:], da[:, t, HPG * g:HPG * (g + 1)].unsqueeze(2).broadcast_to([P, HPG, P]),
                                      lower.unsqueeze(1).broadcast_to([P, HPG, P]), ALU.mult).then_inc(sg_sr.sem, 1)

                def per_head(row):
                    return row.unsqueeze(2).broadcast_to([P, HPG, HD])

                def ssd(n):
                    if n == 0:
                        scan_steps(0)
                    if n < 2 * GROUPS:
                        g, t = n // 2, n % 2
                        hs = slice(HPG * g, HPG * (g + 1))
                        xs = pm[:, t, 0:256].rearrange("p (h d) -> p h d", h=HPG)
                        wait(sg_s1, n + 1)
                        if t == 0:
                            wait(sg_sb, g + 1)
                        if n:
                            wait(sg_sm, n)
                        dve.tensor_tensor(s_cb[:], pm[:, t, 256:384], lower, ALU.mult).then_inc(sg_sc.sem, 1)
                        if n >= 2:
                            wait(sg_s2, n - 1)
                            wait(sg_sd, final_of(n - 2))
                        dve.tensor_tensor(s_xdt[:, t], xs, per_head(dt[:, t, hs]), ALU.mult)
                        if t == 0:
                            dve.tensor_tensor(s_xdd[:], xs, per_head(dtd[:, hs]), ALU.mult)
                        dve.tensor_tensor(s_y[:, t], xs, per_head(rows[:, 64 + HPG * g:64 + HPG * (g + 1)]), ALU.mult).then_inc(sg_sx.sem, 1)
                        wait(sg_sc, n + 1)
                        wait(sg_se, n + 1)
                        dve.tensor_tensor(s_e[:, t], s_e[:, t], s_cb[:].unsqueeze(1).broadcast_to([P, HPG, P]), ALU.mult).then_inc(sg_sm.sem, 1)
                    if n >= 1:
                        m = n - 1
                        g, t = m // 2, m % 2
                        done = final_of(m - 1) if m else 0
                        heads = slice(HPG * HD * g, HPG * HD * (g + 1))
                        wait(sg_s2, m + 1)
                        wait(sg_st, g + 1)
                        y = s_y[:, t]
                        dve.tensor_tensor(y, y, pm[:, 3, 0:256].rearrange("p (h d) -> p h d", h=HPG), ALU.add).then_inc(sg_sd.sem, 1)
                        if t == 1:
                            off = s_xdt[:, 1]
                            dve.tensor_tensor(off, pm[:, 3, 256:512].rearrange("p (h d) -> p h d", h=HPG),
                                              per_head(ed[:, 0, HPG * g:HPG * (g + 1)]), ALU.mult).then_inc(sg_sd.sem, 1)
                            wait(sg_sd, done + 2)
                            dve.tensor_tensor(y, y, off, ALU.add).then_inc(sg_sd.sem, 1)
                        wait(sg_sd, final_of(m) - 1)
                        zg = z[:, t, heads]
                        dve.tensor_tensor(zg, zg, y.rearrange("p h d -> p (h d)"), ALU.mult).then_inc(sg_sd.sem, 1)
                    if n + 1 < 2 * GROUPS:
                        scan_steps(n + 1)

                def split_y(i):
                    wait(sg_yh, i + 1)
                    dve.tensor_tensor(yt_lo[:, 4 * i:4 * i + 4, :], yt[:, 4 * i:4 * i + 4, :], yt_hi[:, 4 * i:4 * i + 4, :].bitcast(F32), ALU.subtract).then_inc(sg_yl.sem, 1)

                def gate(branch, i):
                    t, half = i // 2, i % 2
                    return gates[:, t, D * branch + CW * half:D * branch + CW * (half + 1)]

                def merged_part(i):
                    return merged[:, i // 2, CW * (i % 2):CW * (i % 2 + 1)]

                def merge(n):
                    if n == 0:
                        wait(sg_used, U_A)
                        for i in range(4):
                            dve.tensor_tensor(merged_part(i), pp[:, i, :], gate(2, i), ALU.mult).then_inc(sg_mg.sem, 1)
                        return
                    wait(sg_used, U_B if n == 1 else U_O)
                    if n == 1:
                        wait(sg_mg, 4)
                    else:
                        wait(sg_br, 1)
                    done = 8 * (n - 1)
                    for i in range(6):
                        if i >= 2:
                            wait(sg_mt, done + (i - 1 if i < 4 else 2 * i - 4 + (i == 4)))
                            dve.tensor_tensor(merged_part(i - 2), merged_part(i - 2), mtmp[:, i % 2, :], ALU.add).then_inc(sg_mt.sem, 1)
                        if i < 4:
                            if i >= 2:
                                wait(sg_mt, done + (3 if i == 2 else 5))
                            if n == 1:
                                dve.tensor_tensor(mtmp[:, i % 2, :], pp[:, i, :], gate(0, i), ALU.mult).then_inc(sg_mt.sem, 1)
                            else:
                                dve.scalar_tensor_tensor(mtmp[:, i % 2, :], pp[:, i, :], stat[:, 16 + i // 2:17 + i // 2], gate(1, i), ALU.mult, ALU.mult).then_inc(sg_mt.sem, 1)

                def ssd_norm(_n):
                    wait(sg_bq, 3)
                    dve.reciprocal(stat[:, 16:18], stat[:, 10:12]).then_inc(sg_br.sem, 1)

                def turn_b(k):
                    wait(sg_bh, k + 1)
                    dve.scalar_tensor_tensor(yb_lo[:, k, :], pm[:, k % 4, 0:SEQ],
                                             fmp[:, bass.ds(l, 1), 176 + k], yb_hi[:, k, :].bitcast(F32), ALU.mult, ALU.subtract).then_inc(sg_bl.sem, 1)

                def turn_merged(_n):
                    for k in range(KD):
                        wait(sg_mh, k // 2 * 2 + 2)
                        dve.tensor_tensor(m_lo[:, k, :], pm[:, k // 2, SEQ * (k % 2):SEQ * (k % 2 + 1)], m_hi[:, k, :].bitcast(F32), ALU.subtract).then_inc(sg_ml.sem, 1)

                def add_x(n):
                    wait(sg_used, U_Q if n == 0 else UNITS)
                    for t in range(TT):
                        y = pp[:, 2 * t:2 * t + 2, :].rearrange("p a n -> p (a n)")
                        last = dve.tensor_tensor(x[:, t, :], x[:, t, :], y, ALU.add) if n == 0 else dve.tensor_copy(x[:, t, :], y)
                    last.then_inc(sg_xa.sem, 1)

                made = [0]

                def after(n):
                    dve.wait_ge(sg_tk.sem, sg_tk.at(l, n))
                    dve.sem_inc(s_apart)

                def step(ins):
                    made[0] += 1
                    ins.then_inc(sg_tk.sem, 1)
                    return made[0]

                def top16(rows_of_four):
                    firsts = [step(dve.max(val[:, 0:8], values)) for values, _, val, _ in rows_of_four]
                    seconds = []
                    for i, (values, scratch, val, _) in enumerate(rows_of_four):
                        if i % 2 == 0:
                            after(firsts[i + 1])
                        seconds.append(step(dve.match_replace(scratch, val[:, 0:8], values, NEG)))
                    thirds = []
                    for i, (_, scratch, val, _) in enumerate(rows_of_four):
                        if i % 2 == 0:
                            after(seconds[i + 1])
                        thirds.append(step(dve.max(val[:, 8:16], scratch)))
                    for values, _, val, idx in rows_of_four:
                        step(dve.max_index(idx[:, 0:8], val[:, 0:8], values))
                    after(thirds[-1])
                    for _, scratch, val, idx in rows_of_four:
                        step(dve.max_index(idx[:, 8:16], val[:, 8:16], scratch))

                def top_keys(n):
                    b, t = n // 4, n // 2 % 2
                    wait(sg_kv, 2 * b + t + 1)
                    dve.sem_inc(s_apart)
                    sets = range(8 * b + 4 * (n % 2), 8 * b + 4 * (n % 2) + 4)
                    top16([(sc[:, t, hc, :], tkt[:, hc % 4, 0:KEYS], t_val[:, t, hc // 2, hc % 2], t_idx[:, t, hc // 2, hc % 2]) for hc in sets])

                steps = {"evacuate": evacuate, "dt": dt_vector, "a_score": a_score, "c_score": c_score, "c_mix": c_mix,
                         "ssd": ssd, "split_y": split_y, "merge": merge, "ssd_norm": ssd_norm, "turn_b": turn_b,
                         "turn_merged": turn_merged, "add_x": add_x, "norm": norm, "top_keys": top_keys}

                for u in range(RING):
                    low(u)
                norm(0)
                for u in range(U_E):
                    if u + RING < LOW_POOL:
                        low(u + RING)
                    for name, arg in ORDER[u]:
                        if name in steps:
                            steps[name](arg)

                for i in range(4, 8):
                    top_keys(i)
                after(made[0])
                step(dve.tensor_copy(t_idf[:], t_idx[:]))
                grid = [P, RH, TOPK, TOPK]
                for t in range(TT):
                    n = step(dve.tensor_tensor(cand[:, t], t_val[:, t, :, 0, :].unsqueeze(3).broadcast_to(grid),
                                               t_val[:, t, :, 1, :].unsqueeze(2).broadcast_to(grid), ALU.add))
                for t in range(TT):
                    if t == 0:
                        after(n)
                    for h in range(0, RH, 4):
                        top16([(cand[:, t, h + i].rearrange("p a b -> p (a b)"), tkt[:, i, :], b_val[:, t, h + i], b_pos[:, t, h + i]) for i in range(4)])
                after(made[0])
                step(dve.tensor_scalar(b_row[:, 0], b_pos[:], 4, None, ALU.logical_shift_right))
                step(dve.tensor_scalar(b_row[:, 1], b_pos[:], 15, None, ALU.bitwise_and))
                flat = [P, TT * RH, TOPK]
                bv = b_val[:].rearrange("p t h k -> p (t h) k")
                pg = pick[:, 2].rearrange("p t h k -> p (t h) k")
                n = step(dve.tensor_tensor(pg, bv, bv[:, :, 0:1].broadcast_to(flat), ALU.subtract))
                assert n == n_tk - 12 - 4
                after(n - 1)
                n = step(dve.tensor_copy(b_rof[:], b_row[:]))
                after(n)
                for c in range(2):
                    for t in range(TT):
                        if c:
                            after(made[0] - 1)
                        step(dve.tensor_tensor(cand[:, t], b_rof[:, c, t].unsqueeze(3).broadcast_to(grid),
                                               iota[:, 0:TOPK].unsqueeze(1).unsqueeze(1).broadcast_to(grid), ALU.is_equal))
                    for t in range(TT):
                        after(made[0] - 1)
                        step(dve.tensor_tensor(cand[:, t], cand[:, t], t_idf[:, t, :, c, :].unsqueeze(2).broadcast_to(grid), ALU.mult))
                    for t in range(TT):
                        after(made[0] - 1)
                        step(dve.tensor_reduce(pick[:, c, t], cand[:, t], AX.X, ALU.add))
                wait(sg_gx, 1)
                n = step(dve.tensor_reduce(stat[:, 20:36], pg, AX.X, ALU.add))
                after(n)
                n = step(dve.reciprocal(stat[:, 36:52], stat[:, 20:36]))
                after(n)
                n = step(dve.tensor_tensor(pg, pg, stat[:, 36:52].unsqueeze(2).broadcast_to(flat), ALU.mult))
                assert n == n_tk, (n, n_tk)
                wait(sg_ix, 1)
                dve.tensor_copy(gate_t[:, 0, :], pm[:, 3, 0:SEQ]).then_inc(sg_ixe.sem, 1)
                dve.tensor_copy(place_t[:].rearrange("p a t -> p (a t)"), pm[:, 2, :]).then_inc(sg_ixe.sem, 1)
                dve.tensor_copy(iota_b[:], iota[:]).then_inc(sg_ixe.sem, 1)
                for part in range(3):
                    wait(sg_ixe, 1 if part == 0 else 3 + 2 * part)
                    dve.tensor_copy(gate_p[:, part, :], gate_t[:, part, :]).then_inc(sg_ixe.sem, 1)
                    if part < 2:
                        wait(sg_ixe, 4 + 2 * part)
                        dve.tensor_tensor(gate_t[:, part + 1, :], gate_t[:, part, :], gate_p[:, part, :], ALU.subtract).then_inc(sg_ixe.sem, 1)
                wait(sg_ixe, 8)
                wait(sg_xj, 1)
                dve.sem_inc(s_apart)

                def one_hots(half, n, buf):
                    dve.wait_ge(sg_rt.sem, sg_rt.at(l, n + (BATCHES * half - 1)))
                    tok = bass.ds(HOT * n, HOT)
                    ks = iota_b[:, FIRST * half:FIRST * (half + 1)]
                    cols = [P, 3, HOT, FIRST]

                    def each(row, width):
                        return row.unsqueeze(2).broadcast_to([P, HOT, width])

                    dve.tensor_tensor(hot_e[:, buf], ks.unsqueeze(1).broadcast_to([P, HOT, FIRST]), each(place_t[:, 1, tok], FIRST), ALU.is_equal).then_inc(sg_hc.sem, 1)
                    dve.tensor_tensor(hot_r[:, buf], iota_b[:].unsqueeze(1).broadcast_to([P, HOT, KEYS]), each(place_t[:, 0, tok], KEYS), ALU.is_equal)
                    dve.wait_ge(sg_hc.sem, sg_hc.at(l, n + (BATCHES * half + 1)))
                    dve.tensor_tensor(hot_c[:, buf], hot_e[:, buf].unsqueeze(1).broadcast_to(cols), gate_p[:, :, tok].unsqueeze(3).broadcast_to(cols), ALU.mult).then_inc(sg_hot.sem, 1)

                with dve.Fori(0, BATCHES // 4) as i:
                    for r in range(4):
                        one_hots(0, 4 * i + r, r % 2)

                def weigh_four(n):
                    cols = bass.ds(4 * n, 4)
                    dve.tensor_tensor(hid[:, cols, :].rearrange("p a t -> p (a t)"), hid[:, cols, :].rearrange("p a t -> p (a t)"),
                                      route[:, cols, :].rearrange("p a t -> p (a t)"), ALU.mult).then_inc(sg_wm.sem, 1)

                def hidden_low(i, r):
                    dve.wait_ge(sg_gh.sem, sg_gh.at(l, RING * i + (r + 1)))
                    dve.tensor_tensor(g_lo[:, r % 2, :], hid[:, bass.ds(RING * i + r, 1), :].rearrange("p o t -> p (o t)"),
                                      g_hi[:, r % 2, :].bitcast(F32), ALU.subtract).then_inc(sg_gw.sem, 1)

                wait(sg_free, GROUPS_OF_ROUTES)
                wait(sg_ge, FIRST)
                dve.sem_inc(s_apart)
                with dve.Fori(0, FIRST // RING // 2) as i:
                    for r in range(RING):
                        if r % 2 == 0:
                            weigh_four(2 * i + r // 2)
                        hidden_low(i, r)
                with dve.Fori(FIRST // RING // 2, FIRST // RING) as i:
                    for r in range(RING):
                        for b in range(2):
                            one_hots(1, 2 * RING * i + (2 * r + b - FIRST), b)

                def weigh(j, buf):
                    dve.wait_ge(sg_ge.sem, sg_ge.at(l, j + (FIRST + 1)))
                    g = g_act[:, buf, :]
                    dve.tensor_tensor(g, g, route[:, bass.ds(j, 1), :].rearrange("p o t -> p (o t)"), ALU.mult).then_inc(sg_gl.sem, 1)
                    dve.wait_ge(sg_gl.sem, sg_gl.at(l, 3 * j + 1))
                    dve.tensor_copy(g_hi[:, buf, :], g).then_inc(sg_gl.sem, 1)
                    dve.wait_ge(sg_gl.sem, sg_gl.at(l, 3 * j + 2))
                    dve.tensor_tensor(g_lo[:, buf, :], g, g_hi[:, buf, :].bitcast(F32), ALU.subtract).then_inc(sg_gl.sem, 1)

                def expert_low(v, i=0):
                    s = v % RING
                    dve.wait_ge(sg_hi.sem, sg_hi.at(l, RING * i + (v + 1)))
                    dve.tensor_tensor(w_lo[:, s, :], raw[:, s, :], w_hi[:, s, :].bitcast(F32), ALU.subtract).then_inc(sg_lo[s].sem, 1)

                wait(sg_free, 2 * GROUPS_OF_ROUTES)
                weigh(0, 0)
                expert_low(U_S + 4)
                weigh(1, 1)
                expert_low(U_S + 5)
                expert_low(U_S + 6)
                with dve.Fori(1, FIRST // 2 - 1) as i:
                    for r in range(2):
                        weigh(2 * i + r, r)
                        expert_low(U_S + 2 * r + 3, i)
                        expert_low(U_S + 2 * r + 4, i)
                weigh(FIRST - 2, 0)
                expert_low(U_S + 2 * FIRST - 1)
                weigh(FIRST - 1, 1)
                add_x(1)
            dve.wait_ge(s_fina, 2)
            dve.reciprocal(stat[:, 12:14], stat[:, 2:4]).then_inc(s_fin, 1)
            dve.wait_ge(s_fin, 1)
            dve.wait_ge(s_fg, 16)
            for t in range(TT):
                dve.scalar_tensor_tensor(xn[:, t, :], x[:, t, :], stat[:, 12 + t:13 + t], fing[:], ALU.mult, ALU.mult).then_inc(s_fin, 1)
            dve.drain().then_inc(s_fin, 1)


def lay_out_chunks(w):
    layers, _, cols = w.shape
    n = cols // CW
    w = w.reshape(layers, 4, 2, P, n, CW).transpose(0, 4, 1, 3, 2, 5)
    return w.reshape(layers, 4 * n, P, 1024)


def lay_out_slabs(w):
    return w.reshape(w.shape[0], -1, P, D)


def lay_out_stream(w_in, w_a, w_b, w_c, w_out, w_query, sub_keys, down, up):
    widths = (A_W, A_W, A_W, C_W, C_W, C_W, SSD_IN, CONV, SSD_H, 3 * D)
    edges = np.concatenate([[0], np.cumsum(widths)])
    qa, ka, va, qc, kc, vc, zz, xbc, dtw, gl = (w_in[:, :, a:b] for a, b in zip(edges[:-1], edges[1:]))
    pad = np.zeros((LAYERS, D, V_CH * CW - V_COLS), w_in.dtype)
    w = np.concatenate([va, vc, dtw, pad, qa, ka, qc, kc, xbc, zz, gl], axis=2)
    stream = np.empty((LAYERS, UNITS, P, 1024), w_in.dtype)
    stream[:, 0:U_C] = lay_out_chunks(w)
    stream[:, U_C:U_A] = lay_out_slabs(w_c)
    stream[:, U_A:U_B] = lay_out_slabs(w_a)
    stream[:, U_B:U_O] = lay_out_slabs(w_b)
    stream[:, U_O:U_Q] = lay_out_slabs(w_out)
    queries = lay_out_chunks(w_query)
    stream[:, U_Q:U_K[0]] = queries[:, :8]
    stream[:, U_K[0] + 1:U_K[1]] = queries[:, 8:]
    stream[:, U_K] = sub_keys.reshape(LAYERS, 2, 8, KEYS, P).transpose(0, 1, 4, 2, 3).reshape(LAYERS, 2, P, 1024)
    downs = down.reshape(LAYERS, KEYS, KEYS, KD, P).transpose(0, 2, 4, 3, 1).reshape(LAYERS, KEYS, P, 1024)
    ups = up.reshape(LAYERS, KEYS, KEYS, D).transpose(0, 2, 1, 3)
    stream[:, U_E:U_U] = downs[:, :FIRST]
    stream[:, U_U:U_S] = ups[:, :FIRST]
    others = stream[:, U_S:]
    others[:, 0] = downs[:, FIRST]
    others[:, 1:2 * FIRST - 2:2] = downs[:, FIRST + 1:]
    others[:, 2:2 * FIRST - 1:2] = ups[:, FIRST:KEYS - 1]
    others[:, 2 * FIRST - 1] = ups[:, KEYS - 1]
    return stream.reshape(LAYERS * UNITS, P, 1024)


def mixer_constants():
    a, b = np.arange(P)[:, None], np.arange(P)[None, :]
    upper = (a > b).astype(np.float32)
    lower = (a <= b).astype(np.float32)
    neg_ge = -(a >= b).astype(np.float32)
    neg_one = -np.ones((P, P), np.float32)
    dists = []
    for d in DILATION:
        for t0, s0 in ((0, 0), (P, 0), (P, P)):
            diff = (t0 + a) - (s0 + b)
            ok = (diff >= 0) & (diff % d == 0) & (diff <= P * d)
            dists.append(np.where(ok, -diff, -1e30).astype(np.float32))
    f32 = np.concatenate([upper, lower, neg_ge, neg_one, *dists], axis=1)
    mask = np.where(a >= b, -1e30, 0.0).astype(np.float32)
    bf = np.concatenate([mask, np.eye(P, dtype=np.float32)], axis=1)
    return np.ascontiguousarray(f32), bf


def kernel(x, norm_mix_g, w_in, conv_w, conv_b, dt_bias, a_log, d_skip, ssd_norm_g, w_branch_a, w_branch_b,
           w_branch_c, w_out, norm_ffn_g, peer_w_query, peer_sub_keys, peer_down, peer_up, final_norm_g):
    import ml_dtypes
    import concourse.bacc as bacc
    from concourse.bass_utils import run_bass_kernel_spmd as run

    def fm(a, tiles):
        return np.asarray(a).reshape(LAYERS, tiles, P).transpose(0, 2, 1)

    x, final_norm_g = np.asarray(x), np.asarray(final_norm_g)
    stream = lay_out_stream(*(np.asarray(a) for a in (w_in, w_branch_a, w_branch_b, w_branch_c, w_out, peer_w_query,
                                                      peer_sub_keys, peer_down, peer_up)))
    taps = np.asarray(conv_w).reshape(LAYERS, 4, 32, P).transpose(0, 3, 2, 1).reshape(LAYERS, P, 128)
    fm_params = np.concatenate([fm(norm_mix_g, 8), fm(norm_ffn_g, 8), taps, fm(conv_b, 32), fm(ssd_norm_g, 16)], axis=2)
    row = np.concatenate([np.asarray(a) for a in (dt_bias, a_log, d_skip)], axis=1)
    row_params = np.broadcast_to(row[:, None, :], (LAYERS, P, 96))
    mix_f32, mix_bf16 = mixer_constants()
    arrays = {
        "x_in": x.reshape(SEQ, D),
        "stream": stream,
        "fm_params": fm_params,
        "row_params": row_params,
        "mix_f32": mix_f32,
        "mix_bf16": mix_bf16.astype(ml_dtypes.bfloat16),
        "ident_in": np.eye(P, dtype=np.float32),
        "iota_in": np.broadcast_to(np.arange(P, dtype=np.float32), (P, P)),
        "final_g": np.broadcast_to(final_norm_g, (P, D)),
    }
    arrays = {k: np.ascontiguousarray(a) for k, a in arrays.items()}
    nc = bacc.Bacc("TRN2", target_bir_lowering=False, num_devices=1)
    args = [nc.dram_tensor(n, a.shape, mybir.dt.from_np(a.dtype), kind="ExternalInput").ap() for n, a in arrays.items()]
    args.append(nc.dram_tensor("trunk_out", (SEQ, D), F32, kind="ExternalOutput").ap())
    build_trunk(nc, *args)
    result = run(nc, [arrays], core_ids=[0])
    return result.results[0]["trunk_out"].reshape(1, SEQ, D)
```

```python
from contextlib import ExitStack

import numpy as np
import concourse.bass as bass
from concourse import mybir

F32 = mybir.dt.float32
F32R = mybir.dt.float32r
BF16 = mybir.dt.bfloat16
U32 = mybir.dt.uint32
ALU = mybir.AluOpType
ACT = mybir.ActivationFunctionType
AX = mybir.AxisListType

P = 128
LAYERS, SEQ, D = 2, 256, 1024
TT = SEQ // P
KD = D // P
HD = 64
A_HEADS, A_SLOTS, A_GROUPS = 18, 6, 3
DILATION = (1, 4, 16)
A_W, C_W, A_OUT = A_HEADS * HD, 18 * HD, A_SLOTS * HD
C_HEADS = 18
SSD_IN, GROUPS, HPG, NSTATE = 2048, 8, 4, 128
SSD_H = GROUPS * HPG
CONV = SSD_IN + 2 * GROUPS * NSTATE
KEYS, TOPK, RH = 128, 16, 8
EPS = 1e-6
NEG = -3.0e38

RING = 4
CW = 512
V_CH, QK_CH, X_CH, Z_CH, G_CH = 5, 9, 8, 4, 6
C_V, C_QK = 0, V_CH
C_X = C_QK + QK_CH
C_Z = C_X + X_CH
C_G = C_Z + Z_CH
CHUNKS = C_G + G_CH
U_C = 4 * CHUNKS
U_B = U_C + 2 * (C_W + A_OUT) // (2 * P)
U_O = U_B + 2 * SSD_IN // (2 * P)
U_Q = U_O + KD
FIRST = KEYS // 2
U_E = U_Q + 16
U_U = U_E + FIRST
U_S = U_U + FIRST
UNITS = U_E + 2 * KEYS
LOW_POOL = U_Q + 8
POOL_SLOTS = (1, 3)
AHEAD, GATE_EXP = 32, 24
HOT = 4
BANK_TOKENS = CW // FIRST
BATCHES, GROUPS_OF_ROUTES = SEQ // HOT, SEQ // BANK_TOKENS
assert GROUPS_OF_ROUTES == FIRST - AHEAD == 32 and BANK_TOKENS == 2 * HOT
V_COLS = 2 * A_W + SSD_H


def chunk_of_stream(c):
    return 4 * c if c < CHUNKS else U_Q + 4 * (c - CHUNKS)


def slot_units(slot):
    return len(range(slot, UNITS, RING))


def make_order():
    order = {u: [] for u in range(UNITS)}
    for c in range(CHUNKS + 4):
        order[chunk_of_stream(c) + 3].append(("evacuate" if c < CHUNKS else "query_out", c))
    order[23].append(("dt", 0))
    order[26].append(("dt_sums", 0))
    a0 = 4 * (C_QK + 5) + 1
    for j in range(A_SLOTS):
        order[a0 + 2 + 4 * j].append(("a_turn", j))
        order[a0 + 4 + 4 * j].append(("a_mix", j))
    for j in range(A_SLOTS):
        order[a0 + 4 * j].append(("a_score", j))
    c0 = a0 + 4 * A_SLOTS + 1
    for p in range(C_HEADS // 2):
        order[c0 + 2 + 4 * p].append(("c_sum", p))
        order[c0 + 4 + 4 * p].append(("c_mix", p))
    for p in range(C_HEADS // 2):
        order[c0 + 4 * p].append(("c_score", p))
    s0 = 4 * C_G
    assert c0 + 4 * (C_HEADS // 2) < s0
    for n in range(2 * GROUPS):
        order[s0 + 1 + 2 * n].append(("ssd", n))
    order[s0 + 1 + 4 * GROUPS].append(("ssd", 2 * GROUPS))
    for i in range(3):
        order[s0 + 1 + 2 * i].append(("split_y", i))
    order[U_C + 4].append(("merge", 0))
    order[U_C + 5].append(("merge", 1))
    order[U_C + 10].append(("merge", 2))
    order[U_C + 11].append(("merge", 3))
    for k in range(16):
        order[U_C + 10 + k // 2].append(("turn_b", k))
    order[U_B + 5].append(("ssd_norm", 0))
    order[U_B + 7].append(("merge", 4))
    order[U_B + 9].append(("turn_merged", 0))
    order[U_B + 15].append(("merge", 5))
    order[U_O + 1].append(("turn_merged", 1))
    for n in range(3):
        order[U_Q + 4 * (n + 1)].append(("key_scores", n))
        order[U_Q + 4 * (n + 1) + 1].append(("top_keys", 2 * n))
        order[U_Q + 4 * (n + 1) + 3].append(("top_keys", 2 * n + 1))
    return order


ORDER = make_order()
URGENT = ("merge", "query_out")


def build_trunk(nc, x_in, stream, sub_keys, fm_params, row_params, mix_f32, mix_bf16, ident_in, iota_in, final_g, out):
    with ExitStack() as ctx:
        base = 16512

        def at(name, shape, offset, dtype=F32):
            return nc.alloc_sbuf_tensor_at(name, [P, *shape], dtype, offset=base + 4 * offset)

        fence = ctx.enter_context(nc.sbuf_tensor("fence", [P, 53200], F32))
        x = at("x", [TT, D], 0)
        h_hi = at("h_hi", [KD, SEQ], 2048, F32R)
        h_lo = at("h_lo", [KD, SEQ], 4096, F32R)
        raw = at("raw", [RING, 1024], 6144)
        w_hi = at("w_hi", [RING, 1024], 10240, F32R)
        w_lo = at("w_lo", [RING, 1024], 14336, F32R)
        ident = at("ident", [P], 18432)
        iota = at("iota", [P], 18560)
        fmp = at("fmp", [LAYERS, 192], 18688)
        stat = at("stat", [64], 19072)
        ar = 19136
        qk = at("qk", [36, SEQ], ar)
        gates = at("gates", [TT, 3 * D], ar)
        yt_hi = at("yt_hi", [12, SEQ], ar + 6144, F32R)
        v = at("v", [TT, V_COLS], ar + 9216)
        xt = at("xt", [32, SEQ], ar + 13888)
        z = at("z", [TT, SSD_IN], ar + 22080)
        yt = at("yt", [12, SEQ], ar + 26176)
        yt_lo = at("yt_lo", [12, SEQ], ar + 26176, F32R)
        ws = ar + 29248
        a_p = at("a_p", [A_GROUPS, 384], ws)
        a_pt = at("a_pt", [A_GROUPS, 384], ws + 1152)
        c_sp = at("c_sp", [2, 384], ws)
        c_w = at("c_w", [2, 384], ws + 768)
        merged = at("merged", [TT, D], ws)
        dts = ar + 31552
        dt = at("dt", [TT, SSD_H], dts)
        da = at("da", [TT, SSD_H], dts + 64)
        ed = at("ed", [2, SSD_H], dts + 128)
        dtd = at("dtd", [SSD_H], dts + 192)
        dtt = at("dtt", [TT, SSD_H], dts + 224)
        ea = at("ea", [SSD_H], dts + 288)
        mixc = ar + 31872
        mixf = at("mixf", [1664], mixc)
        upper = mixf[:, 0:128]
        lower = mixf[:, 128:256]
        neg_ge = mixf[:, 256:384]
        neg_one = mixf[:, 384:512]
        dist = mixf[:, 512:1664].rearrange("p (g n) -> p g n", g=A_GROUPS)
        mixb = at("mixb", [2, P], mixc + 1664, BF16)
        rows = at("rows", [96], mixc + 1792)
        sv = ar + 9216
        s_rh = at("s_rh", [HPG, P], sv, F32R)
        s_rl = at("s_rl", [HPG, P], sv + 3392, F32R)
        upper_r = at("upper_r", [P], ws + 2048, F32R)
        da_hi = at("da_hi", [TT, SSD_H], ws + 2176, F32R)
        da_lo = at("da_lo", [TT, SSD_H], ws + 2240, F32R)
        s_e = at("s_e", [2, HPG, P], sv + 512)
        s_cb = at("s_cb", [P], sv + 1536)
        s_xdt = at("s_xdt", [2, HPG, HD], sv + 1664)
        s_xdd = at("s_xdd", [HPG, HD], sv + 2176)
        s_state = at("s_state", [HPG, HD], sv + 2432)
        s_bt = at("s_bt", [P], sv + 2688)
        s_y = at("s_y", [2, HPG, HD], sv + 2816)
        mtmp = at("mtmp", [2, CW], mixc + 512)
        junk = at("junk", [SSD_IN], sv)
        m_hi = at("m_hi", [KD, SEQ], sv, F32R)
        m_lo = at("m_lo", [KD, SEQ], sv + 2048, F32R)
        yb_hi = at("yb_hi", [16, SEQ], ar + 13888, F32R)
        yb_lo = at("yb_lo", [16, SEQ], ar + 13888 + 4096, F32R)
        xn = at("xn", [TT, D], ar + 22080)
        njunk = at("njunk", [TT, D], ar + 22080 + 2048)
        query = at("query", [16, SEQ], ar + 16384)
        keys = at("keys", [16, KEYS], ar + 13312)
        sc = at("sc", [TT, 16, KEYS], ar)
        tk = ar + 4096
        t_val = at("t_val", [TT, RH, 2, TOPK], tk)
        t_idx = at("t_idx", [TT, RH, 2, TOPK], tk + 512, U32)
        t_idf = at("t_idf", [TT, RH, 2, TOPK], tk + 1024)
        b_val = at("b_val", [TT, RH, TOPK], tk + 1536)
        b_pos = at("b_pos", [TT, RH, TOPK], tk + 1792, U32)
        b_row = at("b_row", [2, TT, RH, TOPK], tk + 2048, U32)
        b_rof = at("b_rof", [2, TT, RH, TOPK], tk + 2560)
        pick = at("pick", [3, TT, RH, TOPK], tk + 3072)
        gate_t = at("gate_t", [3, SEQ], tk + 7936)
        cand = at("cand", [TT, RH, TOPK, TOPK], tk + 3840)
        tkt = at("tkt", [4, 256], tk + 7936)
        route = at("route", [FIRST, SEQ], ar)
        hid = at("hid", [FIRST, SEQ], ar + 16384)
        hot_r = at("hot_r", [2, HOT, KEYS], 0, BF16)
        hot_e = at("hot_e", [2, HOT, FIRST], 512, BF16)
        hot_c = at("hot_c", [2, 3, HOT, FIRST], 768, BF16)
        g_act = at("g_act", [2, SEQ], 1536)
        g_lo = at("g_lo", [2, SEQ], 1536, F32R)
        tail = ar + 32768
        place_t = at("place_t", [2, SEQ], tail, BF16)
        gate_p = at("gate_p", [3, SEQ], tail + 256, BF16)
        iota_b = at("iota_b", [P], tail + 640, BF16)
        g_hi = at("g_hi", [2, SEQ], tail + 768, F32R)
        fing = at("fing", [D], ar + 9216)

        pp = ctx.enter_context(nc.psum_tensor("pp", [P, 4, 512], F32))
        pm = ctx.enter_context(nc.psum_tensor("pm", [P, 4, 512], F32))

        ROUTES_FROM = 16
        assert (FIRST - ROUTES_FROM) * 16 == BATCHES * 12

        def batches_of_up(r):
            first = r + r // 3
            return ([first], first + 1) if r % 3 == 2 else ([], first)

        def ring_turn(i, r):
            return 3 * i + (ROUTES_FROM + r) // RING, r % RING

        class Signal:

            def __init__(self, name, per_layer, start=0):
                self.sem = ctx.enter_context(nc.semaphore(name))
                self.per, self.start = per_layer, start

            def at(self, l, n):
                return l * self.per + (n + self.start)

        sg_raw = [Signal(f"raw_landed{s}", 16 * slot_units(s)) for s in range(RING)]
        sg_hi = Signal("high_ready", UNITS, 1)
        sg_lo = [Signal(f"low_ready{s}", slot_units(s), 1) for s in range(RING)]
        sg_used = Signal("unit_used", UNITS, 1)
        sg_sq, sg_root, sg_rstd, sg_xn = (Signal(n, 4) for n in ("squares", "roots", "rstd_ready", "xn_ready"))
        sg_turn, sg_hh, sg_hl = Signal("xn_turned", 16), Signal("h_high", 32), Signal("h_low", 32)
        sg_ev, sg_cv, sg_xs = Signal("chunk_out", 28), Signal("conv_step", 128), Signal("conv_silu", 4)
        sg_dt, sg_dta, sg_dtp = Signal("dt_vector", 4), Signal("dt_scalar", 5), Signal("dt_sums", 1)
        sg_as, sg_ab, sg_am, sg_ae, sg_ar = Signal("a_scores", 18), Signal("a_biased", 18), Signal("a_max", 6), Signal("a_exp", 6), Signal("a_scaled", 12)
        sg_at, sg_ap, sg_apv, sg_ay = Signal("a_turned", 18), Signal("a_turned_out", 18), Signal("a_mixed", 6), Signal("a_out", 6)
        sg_cz, sg_cl, sg_csp, sg_cc = Signal("c_scores", 18), Signal("c_log", 54), Signal("c_softplus", 18), Signal("c_summed", 18)
        sg_cw, sg_cpv, sg_cy = Signal("c_weights", 18), Signal("c_mixed", 9), Signal("c_out", 9)
        sg_da, sg_srl = Signal("da_split", 3), Signal("s_steps_low", 16)
        sg_sr, sg_s1, sg_sgm, sg_se, sg_sb = Signal("s_steps", 16), Signal("s_turned", 16), Signal("s_segments", 16, 1), Signal("s_decay", 16), Signal("s_bt_out", 8)
        sg_sc, sg_sx, sg_sm, sg_s2, sg_st, sg_sd = Signal("s_cb_out", 16), Signal("s_inputs", 16), Signal("s_masked", 16), Signal("s_products", 16), Signal("s_state_out", 8), Signal("s_sum", 48)
        sg_yh, sg_yl = Signal("y_high", 3), Signal("y_low", 3)
        sg_bq, sg_br, sg_bt, sg_bh, sg_bl = Signal("b_squares", 3), Signal("b_rstd", 1), Signal("b_turned", 16), Signal("b_high", 16), Signal("b_low", 16)
        sg_cd, sg_mt = Signal("c_half_done", 2), Signal("merge_step", 20)
        sg_mtt, sg_mh, sg_ml, sg_xa = Signal("merged_turned", 4), Signal("merged_high", 8), Signal("merged_low", 8), Signal("x_added", 4, 2)
        sg_t0 = Signal("first_tile_summed", 2)
        sg_keys, sg_ks, sg_kv = Signal("sub_keys_landed", 16), Signal("key_scores", 4), Signal("key_scores_out", 8)
        n_tk = 5 * 32 + 1 + 2 * (1 + 5 * 8) + 3 + 12 + 4
        sg_tk, sg_gx, sg_ix, sg_ixe = Signal("retrieval_step", n_tk), Signal("gate_exp", 1), Signal("picks_turned", 1), Signal("picks_out", 8)
        sg_xj, sg_hc = Signal("x_joined", 1), Signal("hot_columns", 2 * BATCHES)
        sg_hot, sg_rt, sg_free = Signal("one_hots", 2 * BATCHES), Signal("routes", 2 * BATCHES, 2), Signal("route_banks_free", 2 * GROUPS_OF_ROUTES, 2)
        sg_ge, sg_gl = Signal("gelu", KEYS), Signal("weighted", 3 * FIRST)
        sg_wm, sg_gh, sg_gw = Signal("hidden_weighted", FIRST // 4), Signal("hidden_high", FIRST), Signal("hidden_low", FIRST)
        s_init = ctx.enter_context(nc.semaphore("init_landed"))
        s_apart = ctx.enter_context(nc.semaphore("apart"))
        INIT = 4 * 16
        s_x = ctx.enter_context(nc.semaphore("x_landed"))
        sg_mix = Signal("mix_constants", 48)
        s_fin = ctx.enter_context(nc.semaphore("final_step"))
        s_fina = ctx.enter_context(nc.semaphore("final_scalar"))
        s_out = ctx.enter_context(nc.semaphore("out_stored"))
        s_fg = ctx.enter_context(nc.semaphore("final_g_landed"))

        def merges(n):
            return (2, 6, 8, 12, 16, 20)[n]

        def final_of(n):
            return 6 * (n // 2) + (2 if n % 2 == 0 else 6)

        def score_bank(n, t):
            return pm[:, 2 * (n % 2) + t, :]

        def a_head(j, g):
            h = g * A_SLOTS + j
            return h // 2, HD * (h % 2), HD * h

        def down_v(j):
            return 0 if j == 0 else 2 * j - 1

        def up_v(j):
            return 2 * j + 2 if j < FIRST - 1 else 2 * FIRST - 1

        block = ctx.enter_context(nc.Block())

        @block.sync
        def _(sp):
            sp.dma_start(x[:], x_in.rearrange("(a p) d -> p a d", p=P)).then_inc(s_x, 16)
            sp.dma_start(ident[:], ident_in).then_inc(s_init, 16)
            sp.dma_start(iota[:], iota_in).then_inc(s_init, 16)
            sp.dma_start(fmp[:], fm_params.rearrange("l p n -> p l n")).then_inc(s_init, 16)
            with sp.Fori(0, LAYERS) as l:
                for s in range(RING):
                    sp.wait_ge(sg_lo[s].sem, sg_lo[s].at(l, 0))
                    sp.dma_start(raw[:, s, :], stream[bass.ds(l * UNITS + s, 1)].rearrange("o p n -> p (o n)")).then_inc(sg_raw[s].sem, 16)
                with sp.Fori(1, UNITS // RING) as i:
                    for s in range(RING):
                        sp.wait_ge(sg_lo[s].sem, sg_lo[s].at(l, i))
                        sp.dma_start(raw[:, s, :], stream[bass.ds(l * UNITS + RING * i + s, 1)].rearrange("o p n -> p (o n)")).then_inc(sg_raw[s].sem, 16)
                for u in range(UNITS // RING * RING, UNITS):
                    sp.wait_ge(sg_lo[u % RING].sem, sg_lo[u % RING].at(l, u // RING))
                    sp.dma_start(raw[:, u % RING, :], stream[bass.ds(l * UNITS + u, 1)].rearrange("o p n -> p (o n)")).then_inc(sg_raw[u % RING].sem, 16)
            for t in range(TT):
                sp.wait_ge(s_fin, 2 * t + 2)
                sp.dma_start(out[P * t:P * (t + 1), :], xn[:, t, :]).then_inc(s_out, 16)
            sp.wait_ge(s_out, 16 * TT)

        @block.gpsimd
        def _(pool):
            pool.wait_ge(s_x, 16)
            with pool.Fori(0, LAYERS) as l:
                pool.wait_ge(sg_xa.sem, sg_xa.at(l, 0))
                pool.sem_inc(s_apart)
                pool.dma_start(mixf[:], mix_f32).then_inc(sg_mix.sem, 16)
                pool.dma_start(mixb[:], mix_bf16.rearrange("p (a n) -> p a n", a=2)).then_inc(sg_mix.sem, 16)
                pool.dma_start(rows[:], row_params[bass.ds(l, 1)].rearrange("o p n -> p (o n)")).then_inc(sg_mix.sem, 16)

                def low(s, hi_count):
                    pool.wait_ge(sg_hi.sem, sg_hi.at(l, hi_count))
                    pool.tensor_tensor(w_lo[:, s, :], raw[:, s, :], w_hi[:, s, :].bitcast(F32), ALU.subtract).then_inc(sg_lo[s].sem, 1)

                def lows(i):
                    for s in POOL_SLOTS:
                        low(s, RING * i + (s + 1))

                def scan_steps_low(i, t):
                    pool.wait_ge(sg_sgm.sem, sg_sgm.at(l, 2 * i + t))
                    pool.tensor_tensor(s_rl[:], da_lo[:, t, bass.ds(HPG * i, HPG)].bitcast(F32).unsqueeze(2).broadcast_to([P, HPG, P]),
                                       lower.unsqueeze(1).broadcast_to([P, HPG, P]), ALU.mult).then_inc(sg_srl.sem, 1)

                scan = C_G
                with pool.Fori(0, scan) as i:
                    lows(i)
                pool.wait_ge(sg_da.sem, sg_da.at(l, 3))
                pool.wait_ge(sg_cy.sem, sg_cy.at(l, 9))
                pool.sem_inc(s_apart)
                with pool.Fori(0, GROUPS) as i:
                    for t, s in enumerate(POOL_SLOTS):
                        low(s, RING * i + (RING * scan + s + 1))
                        scan_steps_low(i, t)
                with pool.Fori(scan + GROUPS, U_O // RING) as i:
                    lows(i)
                pool.wait_ge(sg_used.sem, sg_used.at(l, U_O))
                pool.sem_inc(s_apart)
                pool.dma_start(keys[:], sub_keys[bass.ds(l, 1)].rearrange("o p s n -> p (o s) n")).then_inc(sg_keys.sem, 16)
                for u in range(U_O, LOW_POOL):
                    if u % RING in POOL_SLOTS:
                        low(u % RING, u + 1)
                with pool.Fori(LOW_POOL // RING, U_S // RING + 1) as i:
                    for s in range(RING):
                        low(s, RING * i + (s + 1))
            pool.wait_ge(sg_xa.sem, sg_xa.at(LAYERS, 0))
            pool.dma_start(fing[:], final_g).then_inc(s_fg, 16)

        @block.tensor
        def _(pe):
            pe.sem_inc(sg_used.sem, sg_used.start)
            pe.sem_inc(sg_sgm.sem, sg_sgm.start)
            pe.sem_inc(sg_rt.sem, sg_rt.start)
            pe.wait_ge(s_init, INIT)
            with pe.Fori(0, LAYERS) as l:

                def wait(sig, n):
                    pe.wait_ge(sig.sem, sig.at(l, n))

                def transpose(dst, src):
                    return pe.transpose(dst, src, ident[0:src.shape[0], 0:src.shape[0]])

                def unit_ready(u):
                    wait(sg_lo[u % RING], u // RING + 1)

                def chunk_unit_fm(c, q, rhs_hi, rhs_lo):
                    u = chunk_of_stream(c) + q
                    unit_ready(u)
                    pair = c % 2
                    for s in range(2):
                        for m in range(4):
                            dst = pp[:, 2 * pair + m // 2, SEQ * (m % 2):SEQ * (m % 2 + 1)]
                            col = slice(CW * s + P * m, CW * s + P * (m + 1))
                            wh, wl = w_hi[:, u % RING, col], w_lo[:, u % RING, col]
                            k = 2 * q + s
                            pe.matmul(dst, wh, rhs_hi[:, k, :], start=(k == 0 and m % 2 == 0), stop=False, skip_group_check=True)
                            pe.matmul(dst, wh, rhs_lo[:, k, :], start=False, stop=False, skip_group_check=True)
                            last = pe.matmul(dst, wl, rhs_hi[:, k, :], start=False, stop=(k == KD - 1), skip_group_check=True)
                    last.then_inc(sg_used.sem, 1)

                def chunk_unit_tm(c, q):
                    u = chunk_of_stream(c) + q
                    unit_ready(u)
                    pair = c % 2
                    for s in range(2):
                        k = 2 * q + s
                        col = slice(CW * s, CW * (s + 1))
                        for t in range(TT):
                            tok = slice(P * t, P * (t + 1))
                            dst = pp[:, 2 * pair + t, :]
                            pe.matmul(dst, h_hi[:, k, tok], w_hi[:, u % RING, col], start=(k == 0), stop=False)
                            pe.matmul(dst, h_hi[:, k, tok], w_lo[:, u % RING, col], start=False, stop=False)
                            last = pe.matmul(dst, h_lo[:, k, tok], w_hi[:, u % RING, col], start=False, stop=(k == KD - 1))
                    last.then_inc(sg_used.sem, 1)

                def pair_free(c):
                    if c in (0, 1):
                        return
                    if c in (CHUNKS, CHUNKS + 1):
                        return
                    b = c - 2
                    if C_X <= b < C_Z:
                        wait(sg_cv, 16 * (b - C_X + 1))
                    elif b < C_X:
                        wait(sg_ev, b + 1)
                    else:
                        wait(sg_ev, b + 1 - X_CH)

                def half_slab(u, s, k, lhs_hi, lhs_lo, pair, tiles=range(TT), start=False, stop=False):
                    col = slice(CW * s, CW * (s + 1))
                    for t in tiles:
                        tok = slice(P * t, P * (t + 1))
                        dst = pp[:, 2 * pair + t, :]
                        pe.matmul(dst, lhs_hi[:, k, tok], w_hi[:, u % RING, col], start=start, stop=False)
                        pe.matmul(dst, lhs_hi[:, k, tok], w_lo[:, u % RING, col], start=False, stop=False)
                        last = pe.matmul(dst, lhs_lo[:, k, tok], w_hi[:, u % RING, col], start=False, stop=stop)
                    return last

                def turn_x(n, t):
                    wait(sg_xn, 2 * n + t + 1)
                    for b in range(4):
                        if t == 1:
                            wait(sg_hl, 16 * n + 2 * b + 2)
                        for k in (2 * b, 2 * b + 1):
                            last = transpose(pm[:, b, P * (k % 2):P * (k % 2 + 1)], xn[:, t, P * k:P * (k + 1)])
                        last.then_inc(sg_turn.sem, 1)

                def dt_sums(_n):
                    wait(sg_mix, 48)
                    wait(sg_dt, 3)
                    pe.matmul(pm[:, 3, 0:SSD_H], lower, da[:, 1, :], start=True, stop=True)
                    pe.matmul(pm[:, 3, SSD_H:2 * SSD_H], upper, da[:, 0, :], start=True, stop=True).then_inc(sg_dtp.sem, 1)

                def a_score(j):
                    wait(sg_ev, C_QK + 5)
                    for g in range(A_GROUPS):
                        if j == 0:
                            wait(sg_hl, 16)
                        else:
                            wait(sg_ap, 3 * (j - 1) + g + 1)
                        tile, part, _ = a_head(j, g)
                        row = slice(part, part + HD)
                        q, k = qk[row, tile, :], qk[row, 9 + tile, :]
                        pe.matmul(pm[:, g, 0:P], q[:, 0:P], k[:, 0:P], start=True, stop=True)
                        pe.matmul(pm[:, g, P:3 * P], q[:, P:SEQ], k[:, 0:SEQ], start=True, stop=True).then_inc(sg_as.sem, 1)

                def a_turn(j):
                    wait(sg_ar, 2 * j + 2)
                    for g in range(A_GROUPS):
                        for b in range(3):
                            last = transpose(pm[:, g, P * b:P * (b + 1)], a_p[:, g, P * b:P * (b + 1)])
                        last.then_inc(sg_at.sem, 1)

                def a_mix(j):
                    wait(sg_ap, 3 * j + 3)
                    if j == 0:
                        wait(sg_dta, 5)
                    else:
                        wait(sg_ay, j)
                    part = HD * (j % 2)
                    dst = pm[part:part + HD, 3, :]
                    for g in range(A_GROUPS):
                        _, _, col = a_head(j, g)
                        pe.matmul(dst[:, 0:SEQ], v[:, 0, col:col + HD], a_pt[:, g, 0:SEQ], start=(g == 0), stop=False)
                        last = pe.matmul(dst[:, P:SEQ], v[:, 1, col:col + HD], a_pt[:, g, SEQ:3 * P], start=False, stop=(g == A_GROUPS - 1))
                    last.then_inc(sg_apv.sem, 1)

                def c_score(p):
                    wait(sg_ev, C_X)
                    for i in range(2):
                        h = 2 * p + i
                        if p == 0:
                            wait(sg_ap, 18)
                        else:
                            wait(sg_cw, h - 1)
                        row = slice(HD * i, HD * i + HD)
                        q, k = qk[row, 18 + p, :], qk[row, 27 + p, :]
                        pe.matmul(pm[:, i, 0:SEQ], k[:, 0:P], q, start=True, stop=False, skip_group_check=True)
                        pe.matmul(pm[:, i, SEQ:3 * P], k[:, P:SEQ], q[:, P:SEQ], start=False, stop=False, skip_group_check=True)
                        pe.matmul(pm[:, i, 0:P], mixb[:, 1, :], mixb[:, 0, :], start=False, stop=False, skip_group_check=True)
                        pe.matmul(pm[:, i, SEQ:3 * P], mixb[:, 1, :], mixb[:, 0, :], start=False, stop=False, skip_group_check=True).then_inc(sg_cz.sem, 1)

                def c_sum(p):
                    for i in range(2):
                        wait(sg_csp, 2 * p + i + 1)
                        pe.matmul(pm[:, i, 0:3 * P], neg_ge, c_sp[:, i, :], start=False, stop=False, skip_group_check=True)
                        pe.matmul(pm[:, i, P:SEQ], neg_one, c_sp[:, i, SEQ:3 * P], start=False, stop=True, skip_group_check=True).then_inc(sg_cc.sem, 1)

                def c_mix(p):
                    wait(sg_cw, 2 * p + 2)
                    if p >= 1:
                        wait(sg_cy, p)
                    for i in range(2):
                        dst = pm[HD * i:HD * (i + 1), 2, :]
                        col = A_W + HD * (2 * p + i)
                        pe.matmul(dst[:, 0:SEQ], v[:, 0, col:col + HD], c_w[:, i, 0:SEQ], start=True, stop=False)
                        last = pe.matmul(dst[:, P:SEQ], v[:, 1, col:col + HD], c_w[:, i, SEQ:3 * P], start=False, stop=True)
                    last.then_inc(sg_cpv.sem, 1)

                def ssd(n):
                    if n < 2 * GROUPS:
                        g, t = n // 2, n % 2
                        tok = slice(P * t, P * (t + 1))
                        wait(sg_xs, 4)
                        if n < 2:
                            wait(sg_cw, 18)
                        else:
                            wait(sg_sx, n - 1)
                        if n >= 2 and t == 0:
                            wait(sg_sb, g)
                        b = pm[:, t, :]
                        transpose(b[:, 0:P], xt[:, 2 * g, tok])
                        transpose(b[:, P:2 * P], xt[:, 2 * g + 1, tok])
                        bm, cm = xt[:, 16 + g, tok], xt[:, 24 + g, tok]
                        last = pe.matmul(b[:, 2 * P:3 * P], bm, cm, start=True, stop=True)
                        if t == 0:
                            last = transpose(b[:, 3 * P:4 * P], bm)
                        last.then_inc(sg_s1.sem, 1)
                        wait(sg_sr, n + 1)
                        wait(sg_srl, n + 1)
                        if n == 0:
                            wait(sg_cy, 9)
                        else:
                            wait(sg_se, n)
                        pe.matmul(pm[:, 2, :], upper_r[:], s_rh[:].rearrange("p h t -> p (h t)"), start=True, stop=False)
                        pe.matmul(pm[:, 2, :], upper_r[:], s_rl[:].rearrange("p h t -> p (h t)"), start=False, stop=True).then_inc(sg_sgm.sem, 1)
                    if n >= 1:
                        m = n - 1
                        g, t = m // 2, m % 2
                        wait(sg_sm, m + 1)
                        wait(sg_sx, m + 1)
                        if m == 0:
                            wait(sg_ay, 6)
                        else:
                            wait(sg_sd, final_of(m - 1))
                        if g + t:
                            wait(sg_st, g + t)
                        if t == 0:
                            wait(sg_sb, g + 1)
                        for h in range(HPG):
                            pe.matmul(pm[:, 3, HD * h:HD * (h + 1)], s_e[:, t, h, :], s_xdt[:, t, h, :], start=True, stop=True)
                        if t == 0:
                            last = pe.matmul(pm[:, 3, 256:512], s_bt[:], s_xdd[:].rearrange("p h d -> p (h d)"), start=True, stop=True)
                        else:
                            last = pe.matmul(pm[:, 3, 256:512], xt[:, 24 + g, P:SEQ], s_state[:].rearrange("p h d -> p (h d)"), start=True, stop=True)
                        last.then_inc(sg_s2.sem, 1)

                def turn_b(k):
                    wait(sg_sd, 48)
                    if k >= 4:
                        wait(sg_bl, k - 3)
                    for t in range(TT):
                        last = transpose(pm[:, k % 4, P * t:P * (t + 1)], z[:, t, P * k:P * (k + 1)])
                    last.then_inc(sg_bt.sem, 1)

                def turn_merged(h):
                    wait(sg_mt, merges(4 + h))
                    wait(sg_bl, 16)
                    for b in (2 * h, 2 * h + 1):
                        for k in (2 * b, 2 * b + 1):
                            for t in range(TT):
                                last = transpose(pm[:, b, SEQ * (k % 2) + P * t:SEQ * (k % 2) + P * (t + 1)], merged[:, t, P * k:P * (k + 1)])
                        last.then_inc(sg_mtt.sem, 1)

                def key_scores(n):
                    wait(sg_ev, CHUNKS + n + 1 - X_CH)
                    if n == 0:
                        wait(sg_keys, 16)
                    if n >= 2:
                        wait(sg_kv, 2 * (n - 2) + 2)
                    for t in range(TT):
                        for i in range(4):
                            hc = 4 * n + i
                            last = pe.matmul(score_bank(n, t)[:, P * i:P * (i + 1)], query[:, hc, P * t:P * (t + 1)], keys[:, hc, :], start=True, stop=True)
                    last.then_inc(sg_ks.sem, 1)

                steps = {"key_scores": key_scores, "dt_sums": dt_sums, "a_score": a_score, "a_turn": a_turn, "a_mix": a_mix,
                         "c_score": c_score, "c_sum": c_sum, "c_mix": c_mix, "ssd": ssd, "turn_b": turn_b,
                         "turn_merged": turn_merged}

                def between(u):
                    for name, arg in ORDER[u]:
                        if name in steps:
                            steps[name](arg)

                turn_x(0, 0)
                turn_x(0, 1)
                for c in range(CHUNKS):
                    pair_free(c)
                    for q in range(4):
                        if c == 0:
                            wait(sg_hl, 8 + 2 * q + 2)
                        if C_QK <= c < C_Z:
                            chunk_unit_fm(c, q, h_hi, h_lo)
                        else:
                            chunk_unit_tm(c, q)
                        between(4 * c + q)
                wait(sg_ev, 23)
                wait(sg_yl, 3)
                slabs = C_W // P + A_OUT // P
                for u in range(U_C, U_B):
                    half, q = divmod(u - U_C, slabs // 2)
                    unit_ready(u)
                    for s in range(2):
                        n = 2 * q + s
                        if n < C_W // P:
                            if n == 0 and half == 1:
                                wait(sg_mt, merges(0))
                            last = half_slab(u, s, 3 + n, yt_hi, yt_lo, 0, start=(n == 0), stop=(n == C_W // P - 1))
                            if n == C_W // P - 1:
                                last.then_inc(sg_cd.sem, 1)
                        else:
                            k = n - C_W // P
                            if k == 0:
                                if half == 0:
                                    wait(sg_ev, 24)
                                else:
                                    wait(sg_mt, merges(1))
                            last = half_slab(u, s, k, yt_hi, yt_lo, 1, start=(k == 0), stop=(n == slabs - 1))
                    last.then_inc(sg_used.sem, 1)
                    between(u)
                for u in range(U_B, U_O):
                    half, q = divmod(u - U_B, 8)
                    unit_ready(u)
                    if q == 0:
                        wait(sg_mt, merges(2 + half))
                    wait(sg_bl, 2 * q + 2)
                    for s in range(2):
                        k = 2 * q + s
                        last = half_slab(u, s, k, yb_hi, yb_lo, half, start=(k == 0), stop=(k == 15))
                    last.then_inc(sg_used.sem, 1)
                    between(u)

                def out_unit(u, tiles):
                    block_of_4, half, q = (u - U_O) // 4, (u - U_O) % 4 // 2, (u - U_O) % 2
                    unit_ready(u)
                    wait(sg_ml, 4 * block_of_4 + 2 * q + 2)
                    for s in range(2):
                        k = 4 * block_of_4 + 2 * q + s
                        last = half_slab(u, s, k, m_hi, m_lo, half, tiles, start=(k == 0), stop=(k == KD - 1))
                    return last

                for u in range(U_O, U_O + 4):
                    if (u - U_O) % 2 == 0:
                        wait(sg_mt, merges(4 + (u - U_O) // 2))
                    out_unit(u, range(TT)).then_inc(sg_used.sem, 1)
                    between(u)
                for u in range(U_O + 4, U_Q):
                    last = out_unit(u, [0])
                last.then_inc(sg_t0.sem, 1)
                for u in range(U_O + 4, U_Q):
                    out_unit(u, [1]).then_inc(sg_used.sem, 1)
                    if u == U_Q - 2:
                        turn_x(1, 0)
                turn_x(1, 1)

                for c in range(CHUNKS, CHUNKS + 4):
                    pair_free(c)
                    for q in range(4):
                        if c == CHUNKS:
                            wait(sg_hl, 24 + 2 * q + 2)
                        chunk_unit_fm(c, q, h_hi, h_lo)
                        between(chunk_of_stream(c) + q)

                def down(slot, turn, bank, midway=None):
                    pe.wait_ge(sg_lo[slot].sem, sg_lo[slot].at(l, turn))
                    for k in range(KD):
                        if midway and k == KD // 2:
                            midway()
                        col = slice(P * k, P * (k + 1))
                        wh, wl = w_hi[:, slot, col], w_lo[:, slot, col]
                        dst = pm[:, bank, 0:SEQ]
                        pe.matmul(dst, wh, h_hi[:, k, :], start=(k == 0), stop=False)
                        pe.matmul(dst, wh, h_lo[:, k, :], start=False, stop=False)
                        last = pe.matmul(dst, wl, h_hi[:, k, :], start=False, stop=(k == KD - 1))
                    last.then_inc(sg_used.sem, 1)

                def up_tile(slot, t, lhs_hi, lhs_lo, stop=False):
                    tok = slice(P * t, P * (t + 1))
                    for half in range(2):
                        col = slice(CW * half, CW * (half + 1))
                        dst = pp[:, 2 * t + half, :]
                        pe.matmul(dst, lhs_hi[:, tok], w_hi[:, slot, col], start=False, stop=False, skip_group_check=True)
                        pe.matmul(dst, lhs_hi[:, tok], w_lo[:, slot, col], start=False, stop=False, skip_group_check=True)
                        last = pe.matmul(dst, lhs_lo[:, tok], w_hi[:, slot, col], start=False, stop=stop, skip_group_check=True)
                    return last

                def up(slot, turn, lhs_hi, lhs_lo, midway=None):
                    pe.wait_ge(sg_lo[slot].sem, sg_lo[slot].at(l, turn))
                    for t in range(TT):
                        if midway and t == 1:
                            midway()
                        last = up_tile(slot, t, lhs_hi, lhs_lo)
                    last.then_inc(sg_used.sem, 1)

                def routes(half, n, bank, b):
                    if b == 0:
                        pe.wait_ge(sg_free.sem, sg_free.at(l, n + (GROUPS_OF_ROUTES * half - 1)))
                    pe.wait_ge(sg_hot.sem, sg_hot.at(l, 2 * n + (BATCHES * half + b + 1)))
                    for r in range(HOT):
                        c = FIRST * (HOT * b + r)
                        for part in range(3):
                            last = pe.matmul(pm[:, 2 + bank, c:c + FIRST], hot_r[:, b, r, :], hot_c[:, b, part, r, :], start=(part == 0), stop=(part == 2))
                    last.then_inc(sg_rt.sem, 1)

                wait(sg_kv, 6)
                for j in range(RING):
                    if j >= 2:
                        wait(sg_ge, j - 1)
                    down((U_E + j) % RING, (U_E + j) // RING + 1, j % 2)
                    if j == 1:
                        key_scores(3)
                for t in range(TT):
                    for half in range(2):
                        last = pe.matmul(pp[:, 2 * t + half, :], ident[:], x[:, t, CW * half:CW * (half + 1)], start=True, stop=False, skip_group_check=True)
                last.then_inc(sg_xj.sem, 1)

                def first_down(i, r, midway=None):
                    pe.wait_ge(sg_ge.sem, sg_ge.at(l, RING * i + (r - 1)))
                    down((U_E + r) % RING, i + ((U_E + r) // RING + 1), r % 2, midway)

                with pe.Fori(1, AHEAD // RING - 1) as i:
                    for r in range(RING):
                        first_down(i, r)
                for r in range(RING):
                    if r == 1:
                        wait(sg_tk, n_tk)
                        for i in range(3):
                            for t in range(TT):
                                last = transpose(pm[:, 2 + i // 2, SEQ * (i % 2) + P * t:SEQ * (i % 2) + P * (t + 1)], pick[:, i, t].rearrange("p h k -> p (h k)"))
                        last.then_inc(sg_ix.sem, 1)
                    first_down(AHEAD // RING - 1, r)
                wait(sg_ixe, 2)
                pe.sem_inc(s_apart)
                with pe.Fori(AHEAD // RING, FIRST // RING) as i:
                    for r in range(RING):
                        n = RING * i + (r - AHEAD)
                        routes(0, n, r % 2, 0)
                        first_down(i, r, midway=lambda: routes(0, n, r % 2, 1))

                def first_up(i, r, midway=None):
                    pe.wait_ge(sg_gw.sem, sg_gw.at(l, RING * i + (r + 1)))
                    up((U_U + r) % RING, i + ((U_U + r) // RING + 1), g_hi[:, r % 2, :], g_lo[:, r % 2, :], midway=midway)

                with pe.Fori(0, ROUTES_FROM // RING) as i:
                    for r in range(RING):
                        first_up(i, r)

                def routes_between(i, b):
                    routes(1, 8 * i + b // 2, b // 2 % 2, b % 2)

                with pe.Fori(0, BATCHES // 16) as i:
                    for r in range(12):
                        ahead, midway = batches_of_up(r)
                        for b in ahead:
                            routes_between(i, b)
                        first_up(*ring_turn(i, r), midway=lambda: routes_between(i, midway))

                def other_down(i, v, j, bank):
                    pe.wait_ge(sg_ge.sem, sg_ge.at(l, j + (FIRST - 1)))
                    down((U_S + v) % RING, i + ((U_S + v) // RING + 1), bank)

                def other_up(i, v, j, buf):
                    pe.wait_ge(sg_gl.sem, sg_gl.at(l, 3 * j + 3))
                    up((U_S + v) % RING, i + ((U_S + v) // RING + 1), g_hi[:, buf, :], g_lo[:, buf, :])

                other_down(0, 0, 0, 0)
                with pe.Fori(0, FIRST // 2 - 1) as i:
                    for r in range(2):
                        other_down(i, 2 * r + 1, 2 * i + (r + 1), (r + 1) % 2)
                        other_up(i, 2 * r + 2, 2 * i + r, r)
                i = FIRST // 2 - 1
                other_down(i, 1, FIRST - 1, 1)
                for t in range(TT):
                    for j in (FIRST - 2, FIRST - 1):
                        u = U_S + up_v(j)
                        if t == 0:
                            wait(sg_lo[u % RING], u // RING + 1)
                            wait(sg_gl, 3 * j + 3)
                        last = up_tile(u % RING, t, g_hi[:, j % 2, :], g_lo[:, j % 2, :], stop=(j == FIRST - 1))
                        if t == 1:
                            last.then_inc(sg_used.sem, 1)
                    if t == 0:
                        last.then_inc(sg_t0.sem, 1)

        @block.scalar
        def _(act):
            act.sem_inc(sg_free.sem, sg_free.start)
            act.sem_inc(sg_hi.sem, sg_hi.start)
            act.wait_ge(s_init, INIT)
            act.wait_ge(s_x, 16)
            with act.Fori(0, LAYERS) as l:

                def wait(sig, n):
                    act.wait_ge(sig.sem, sig.at(l, n))

                def high(u):
                    act.wait_ge(sg_raw[u % RING].sem, sg_raw[u % RING].at(l, 16 * (u // RING + 1)))
                    wait(sg_used, max(u - RING + 1, 0))
                    act.activation(w_hi[:, u % RING, :], raw[:, u % RING, :], ACT.Copy).then_inc(sg_hi.sem, 1)

                def squares(n, t):
                    wait(sg_xa, 2 * n + t - 1)
                    act.activation(njunk[:, t, :], x[:, t, :], ACT.Square, scale=D ** -0.5, accum_out=stat[:, t:t + 1]).then_inc(sg_sq.sem, 1)
                    wait(sg_sq, 2 * n + t + 1)
                    act.activation(stat[:, 2 + t:3 + t], stat[:, t:t + 1], ACT.Sqrt, bias=stat[:, 60:61]).then_inc(sg_root.sem, 1)

                def h_high(n, t):
                    for k in range(KD):
                        if k % 2 == 0:
                            wait(sg_turn, 8 * n + 4 * t + k // 2 + 1)
                            act.sem_inc(s_apart)
                        act.activation(h_hi[:, k, P * t:P * (t + 1)], pm[:, k // 2, P * (k % 2):P * (k % 2 + 1)], ACT.Copy,
                                       scale=fmp[:, bass.ds(l, 1), 8 * n + k]).then_inc(sg_hh.sem, 1)

                def norm(n):
                    first = 0 if n == 0 else U_Q
                    act.activation(stat[:, 61:62], stat[:, 60:61], ACT.Sqrt)
                    squares(n, 0)
                    high(first)
                    if n == 1:
                        h_high(n, 0)
                    squares(n, 1)
                    high(first + 1)
                    if n == 0:
                        h_high(n, 0)
                    h_high(n, 1)
                    high(first + 2)
                    high(first + 3)

                def evacuate(c):
                    if C_X <= c < C_Z:
                        return
                    wait(sg_used, chunk_of_stream(c) + 4)
                    pair = 2 * (c % 2)
                    for b in range(2):
                        src = pp[:, pair + b, :]
                        if c < C_QK:
                            w = min(CW, V_COLS - CW * c)
                            last = act.activation(v[:, b, CW * c:CW * c + w], src[:, 0:w], ACT.Copy)
                        elif c < C_X:
                            first = 4 * (c - C_QK) + 2 * b
                            for m in (0, 1):
                                is_q = (first + m) // 9 % 2 == 0
                                last = act.activation(qk[:, first + m, :], src[:, SEQ * m:SEQ * (m + 1)], ACT.Copy,
                                                      scale=HD ** -0.5 if is_q else 1.0)
                        elif c < C_G:
                            last = act.activation(z[:, b, CW * (c - C_Z):CW * (c - C_Z + 1)], src, ACT.Silu)
                        elif c < CHUNKS:
                            last = act.activation(gates[:, b, CW * (c - C_G):CW * (c - C_G + 1)], src, ACT.Sigmoid)
                        else:
                            tile = 4 * (c - CHUNKS) + 2 * b
                            last = act.activation(query[:, tile:tile + 2, :].rearrange("p a t -> p (a t)"), src, ACT.Copy)
                    last.then_inc(sg_ev.sem, 1)
                    if C_Z <= c < C_G:
                        wait(sg_cv, 128)
                        for i in ((0,), (1,), (2, 3), ())[c - C_Z]:
                            q = xt[:, 8 * i:8 * i + 8, :]
                            act.activation(q, q, ACT.Silu).then_inc(sg_xs.sem, 1)

                def dt_scalar(_n):
                    wait(sg_mix, 48)
                    act.activation(ea[:], rows[:, 32:64], ACT.Exp).then_inc(sg_dta.sem, 1)
                    wait(sg_dt, 1)
                    act.activation(dtt[:], dt[:], ACT.Abs).then_inc(sg_dta.sem, 1)
                    wait(sg_dta, 2)
                    act.activation(dtt[:], dtt[:], ACT.Exp, scale=-1.0).then_inc(sg_dta.sem, 1)
                    wait(sg_dta, 3)
                    act.activation(dtt[:], dtt[:], ACT.Ln, bias=1.0).then_inc(sg_dta.sem, 1)

                def dt_sums(_n):
                    wait(sg_dtp, 1)
                    act.activation(ed[:].rearrange("p a h -> p (a h)"), pm[:, 3, 0:64], ACT.Exp).then_inc(sg_dta.sem, 1)

                def a_score(j):
                    wait(sg_am, j + 1)
                    act.activation(a_p[:, :, 0:P], a_p[:, :, 0:P], ACT.Exp, bias=stat[:, 4:5], accum_out=stat[:, 6:7])
                    act.activation(a_p[:, :, P:3 * P], a_p[:, :, P:3 * P], ACT.Exp, bias=stat[:, 5:6], accum_out=stat[:, 7:8]).then_inc(sg_ae.sem, 1)

                def a_turn(j):
                    if j >= 1:
                        wait(sg_apv, j)
                    for g in range(A_GROUPS):
                        wait(sg_at, 3 * j + g + 1)
                        act.activation(a_pt[:, g, :], pm[:, g, 0:384], ACT.Copy).then_inc(sg_ap.sem, 1)

                def a_mix(j):
                    wait(sg_apv, j + 1)
                    row = slice(HD * (j % 2), HD * (j % 2) + HD)
                    act.activation(yt[row, j // 2, :], pm[row, 3, 0:SEQ], ACT.Copy).then_inc(sg_ay.sem, 1)

                def c_score(p):
                    for i in range(2):
                        h = 2 * p + i
                        wait(sg_cz, h + 1)
                        if p == 0:
                            wait(sg_apv, 6)
                        else:
                            wait(sg_cc, h - 1)
                        act.activation(c_sp[:, i, :], pm[:, i, 0:384], ACT.Abs).then_inc(sg_cl.sem, 1)
                    for i in range(2):
                        wait(sg_cl, 6 * p + i + 1)
                        act.activation(c_sp[:, i, :], c_sp[:, i, :], ACT.Exp, scale=-1.0).then_inc(sg_cl.sem, 1)
                    for i in range(2):
                        wait(sg_cl, 6 * p + i + 3)
                        act.activation(c_sp[:, i, :], c_sp[:, i, :], ACT.Ln, bias=1.0).then_inc(sg_cl.sem, 1)

                def c_sum(p):
                    if p >= 1:
                        wait(sg_cpv, p)
                    for i in range(2):
                        wait(sg_cc, 2 * p + i + 1)
                        act.activation(c_w[:, i, :], pm[:, i, 0:384], ACT.Exp).then_inc(sg_cw.sem, 1)

                def ssd(n):
                    if n < 2 * GROUPS:
                        t = n % 2
                        if t == 0:
                            wait(sg_s1, n + 1)
                            if n >= 2:
                                wait(sg_s2, n - 1)
                            act.activation(s_bt[:], pm[:, 0, 384:512], ACT.Copy).then_inc(sg_sb.sem, 1)
                        wait(sg_sgm, n + 1)
                        if n >= 2:
                            wait(sg_s2, n - 1)
                        act.activation(s_e[:, t].rearrange("p h t -> p (h t)"), pm[:, 2, :], ACT.Exp).then_inc(sg_se.sem, 1)
                    if n >= 1 and (n - 1) % 2 == 0:
                        wait(sg_s2, n)
                        act.activation(s_state[:].rearrange("p h d -> p (h d)"), pm[:, 3, 256:512], ACT.Copy).then_inc(sg_st.sem, 1)

                def split_y(i):
                    if i == 0:
                        wait(sg_cy, 9)
                        wait(sg_ay, 6)
                        wait(sg_cz, 18)
                    act.activation(yt_hi[:, 4 * i:4 * i + 4, :], yt[:, 4 * i:4 * i + 4, :], ACT.Copy).then_inc(sg_yh.sem, 1)

                def ssd_norm(_n):
                    wait(sg_sd, 48)
                    for t in range(TT):
                        act.activation(junk[:], z[:, t, :], ACT.Square, accum_out=stat[:, 8 + t:9 + t]).then_inc(sg_bq.sem, 1)
                        wait(sg_bq, t + 1)
                    act.activation(stat[:, 10:12], stat[:, 8:10], ACT.Sqrt, scale=1.0 / SSD_IN, bias=stat[:, 60:61]).then_inc(sg_bq.sem, 1)

                def turn_b(k):
                    wait(sg_bt, k + 1)
                    act.activation(yb_hi[:, k, :], pm[:, k % 4, 0:SEQ], ACT.Copy,
                                   scale=fmp[:, bass.ds(l, 1), 176 + k]).then_inc(sg_bh.sem, 1)

                def turn_merged(h):
                    for k in range(4 * h, 4 * h + 4):
                        wait(sg_mtt, k // 2 + 1)
                        act.activation(m_hi[:, k, :], pm[:, k // 2, SEQ * (k % 2):SEQ * (k % 2 + 1)], ACT.Copy).then_inc(sg_mh.sem, 1)

                def key_scores(b):
                    wait(sg_ks, b + 1)
                    for t in range(TT):
                        act.activation(sc[:, t, 4 * b:4 * b + 4, :].rearrange("p a n -> p (a n)"), score_bank(b, t), ACT.Copy).then_inc(sg_kv.sem, 1)

                steps = {"evacuate": evacuate, "query_out": evacuate, "dt": dt_scalar, "dt_sums": dt_sums, "a_score": a_score, "a_turn": a_turn, "a_mix": a_mix,
                         "c_score": c_score, "c_sum": c_sum, "ssd": ssd, "split_y": split_y, "ssd_norm": ssd_norm,
                         "turn_b": turn_b, "turn_merged": turn_merged, "key_scores": key_scores}

                norm(0)
                for u in range(U_E):
                    for name, arg in ORDER[u]:
                        if name in steps and name in URGENT:
                            steps[name](arg)
                    if not U_O + 4 <= u < U_Q:
                        high(u + RING)
                    for name, arg in ORDER[u]:
                        if name in steps and name not in URGENT:
                            steps[name](arg)
                    if u == U_Q - 1:
                        norm(1)
                def expert_high(v, i=0):
                    slot = v % RING
                    act.wait_ge(sg_raw[slot].sem, sg_raw[slot].at(l, i * 16 + 16 * (v // RING + 1)))
                    act.wait_ge(sg_used.sem, sg_used.at(l, RING * i + (v - RING + 1)))
                    act.activation(w_hi[:, slot, :], raw[:, slot, :], ACT.Copy).then_inc(sg_hi.sem, 1)

                def first_down(i, r):
                    act.wait_ge(sg_used.sem, sg_used.at(l, RING * i + (U_E + r + 1)))
                    act.activation(hid[:, bass.ds(RING * i + r, 1), :].rearrange("p o t -> p (o t)"), pm[:, r % 2, 0:SEQ], ACT.Gelu).then_inc(sg_ge.sem, 1)
                    expert_high(U_E + r + RING, i)

                def routes(half, n, bank):
                    act.wait_ge(sg_rt.sem, sg_rt.at(l, 2 * n + (BATCHES * half + 2)))
                    act.activation(route[:, :, bass.ds(BANK_TOKENS * n, BANK_TOKENS)], pm[:, 2 + bank, :].rearrange("p (t j) -> p j t", j=FIRST), ACT.Copy).then_inc(sg_free.sem, 1)

                for r in range(RING):
                    first_down(0, r)
                    if r == 1:
                        key_scores(3)
                with act.Fori(1, GATE_EXP // RING) as i:
                    for r in range(RING):
                        first_down(i, r)
                wait(sg_tk, n_tk - 12 - 4)
                act.activation(pick[:, 2], pick[:, 2], ACT.Exp).then_inc(sg_gx.sem, 1)
                with act.Fori(GATE_EXP // RING, AHEAD // RING) as i:
                    for r in range(RING):
                        first_down(i, r)
                with act.Fori(AHEAD // RING, FIRST // RING) as i:
                    for r in range(RING):
                        routes(0, RING * i + (r - AHEAD), r % 2)
                        first_down(i, r)

                def hidden_high(i, r):
                    act.wait_ge(sg_wm.sem, sg_wm.at(l, i + (r // RING + 1)))
                    act.wait_ge(sg_used.sem, sg_used.at(l, RING * i + (U_U + r - 1)))
                    act.activation(g_hi[:, r % 2, :], hid[:, bass.ds(RING * i + r, 1), :].rearrange("p o t -> p (o t)"), ACT.Copy).then_inc(sg_gh.sem, 1)

                def first_up(i, r, last=False, groups=()):
                    if not last:
                        hidden_high(i, r + 1)
                    for n, bank in groups:
                        routes(1, n, bank)
                    expert_high(U_U + r + RING, i)

                hidden_high(0, 0)
                with act.Fori(0, ROUTES_FROM // RING) as i:
                    for r in range(RING):
                        first_up(i, r)

                def twelve_ups(i, last):
                    for r in range(12):
                        ahead, midway = batches_of_up(r)
                        groups = [(8 * i + b // 2, b // 2 % 2) for b in ahead + [midway] if b % 2 == 1]
                        first_up(*ring_turn(i, r), last=last and r == 11, groups=groups)

                with act.Fori(0, BATCHES // 16 - 1) as i:
                    twelve_ups(i, False)
                twelve_ups(BATCHES // 16 - 1, True)

                def gelu(i, v, buf):
                    act.wait_ge(sg_used.sem, sg_used.at(l, RING * i + (U_S + v + 1)))
                    act.activation(g_act[:, buf, :], pm[:, buf, 0:SEQ], ACT.Gelu).then_inc(sg_ge.sem, 1)

                gelu(0, 0, 0)
                expert_high(U_S + 4)
                gelu(0, 1, 1)
                expert_high(U_S + 5)
                expert_high(U_S + 6)
                with act.Fori(1, FIRST // 2 - 1) as i:
                    for r in range(2):
                        gelu(i, 2 * r - 1, r)
                        expert_high(U_S + 2 * r + 3, i)
                        expert_high(U_S + 2 * r + 4, i)
                gelu(0, down_v(FIRST - 2), 0)
                expert_high(U_S + 2 * FIRST - 1)
                gelu(0, down_v(FIRST - 1), 1)
            for t in range(TT):
                act.wait_ge(sg_xa.sem, sg_xa.at(LAYERS, t - 1))
                act.activation(njunk[:, t, :], x[:, t, :], ACT.Square, scale=D ** -0.5, accum_out=stat[:, t:t + 1]).then_inc(s_fina, 1)
                act.wait_ge(s_fina, 2 * t + 1)
                act.activation(stat[:, 2 + t:3 + t], stat[:, t:t + 1], ACT.Sqrt, bias=stat[:, 60:61]).then_inc(s_fina, 1)

        @block.vector
        def _(dve):
            for s in range(RING):
                dve.sem_inc(sg_lo[s].sem, sg_lo[s].start)
            dve.sem_inc(sg_xa.sem, sg_xa.start)
            dve.memset(stat[:], EPS).then_inc(s_init, 16)
            slopes = [2.0 ** (-8.0 * (h + 1) / A_HEADS) for h in range(A_HEADS)]
            dve.wait_ge(s_init, INIT)
            dve.wait_ge(s_x, 16)
            with dve.Fori(0, LAYERS) as l:

                def wait(sig, n):
                    dve.wait_ge(sig.sem, sig.at(l, n))

                def low(u):
                    if u % RING in POOL_SLOTS:
                        return
                    wait(sg_hi, u + 1)
                    dve.tensor_tensor(w_lo[:, u % RING, :], raw[:, u % RING, :], w_hi[:, u % RING, :].bitcast(F32), ALU.subtract).then_inc(sg_lo[u % RING].sem, 1)

                def x_rstd(n, t):
                    wait(sg_root, 2 * n + t + 1)
                    dve.reciprocal(stat[:, 12 + t:13 + t], stat[:, 2 + t:3 + t]).then_inc(sg_rstd.sem, 1)
                    wait(sg_rstd, 2 * n + t + 1)
                    dve.tensor_scalar(xn[:, t, :], x[:, t, :], stat[:, 12 + t:13 + t], None, ALU.mult).then_inc(sg_xn.sem, 1)

                def h_low(n, t, slabs):
                    for k in slabs:
                        wait(sg_hh, 16 * n + 8 * t + k // 2 * 2 + 2)
                        dve.scalar_tensor_tensor(h_lo[:, k, P * t:P * (t + 1)], pm[:, k // 2, P * (k % 2):P * (k % 2 + 1)],
                                                 fmp[:, bass.ds(l, 1), 8 * n + k], h_hi[:, k, P * t:P * (t + 1)].bitcast(F32), ALU.mult, ALU.subtract).then_inc(sg_hl.sem, 1)

                def add_x(n, t):
                    if t == 0:
                        wait(sg_t0, n + 1)
                    else:
                        wait(sg_used, U_Q if n == 0 else UNITS)
                    if n == 0:
                        for half in range(2):
                            part = x[:, t, CW * half:CW * (half + 1)]
                            last = dve.tensor_tensor(part, part, pp[:, 2 * half + t, :], ALU.add)
                        last.then_inc(sg_xa.sem, 1)
                    else:
                        dve.tensor_copy(x[:, t, :], pp[:, 2 * t:2 * t + 2, :].rearrange("p a n -> p (a n)")).then_inc(sg_xa.sem, 1)

                def norm(n):
                    first = 0 if n == 0 else U_Q
                    if n == 1:
                        add_x(0, 0)
                    x_rstd(n, 0)
                    low(first)
                    if n == 1:
                        add_x(0, 1)
                        h_low(n, 0, range(4))
                    x_rstd(n, 1)
                    h_low(n, 0, range(4 if n == 1 else 0, KD))
                    h_low(n, 1, range(4))
                    low(first + 1)
                    h_low(n, 1, range(4, KD))
                    low(first + 2)
                    low(first + 3)

                def evacuate(c):
                    if not C_X <= c < C_Z:
                        return
                    wait(sg_used, 4 * c + 4)
                    for tap in range(4):
                        for m in range(4):
                            ch = 4 * (c - C_X) + m
                            src = pp[:, 2 * (c % 2) + m // 2, SEQ * (m % 2):SEQ * (m % 2 + 1)]
                            wk = fmp[:, bass.ds(l, 1), 16 + 4 * ch + 3 - tap]
                            if tap == 0:
                                ins = dve.tensor_scalar(xt[:, ch, :], src, wk, fmp[:, bass.ds(l, 1), 144 + ch], ALU.mult, ALU.add)
                            else:
                                wait(sg_cv, 16 * (c - C_X) + 4 * (tap - 1) + m + 1)
                                ins = dve.scalar_tensor_tensor(xt[:, ch, tap:SEQ], src[:, 0:SEQ - tap], wk, xt[:, ch, tap:SEQ], ALU.mult, ALU.add)
                            ins.then_inc(sg_cv.sem, 1)

                def dt_vector(_n):
                    wait(sg_ev, V_CH)
                    wait(sg_mix, 48)
                    dve.tensor_tensor(dt[:], v[:, :, 2 * A_W:V_COLS], rows[:, 0:32].unsqueeze(1).broadcast_to([P, TT, SSD_H]), ALU.add).then_inc(sg_dt.sem, 1)
                    wait(sg_dta, 4)
                    dve.scalar_tensor_tensor(dt[:], dt[:], 0.0, dtt[:], ALU.max, ALU.add).then_inc(sg_dt.sem, 1)
                    wait(sg_dt, 2)
                    dve.scalar_tensor_tensor(da[:], dt[:], -1.0, ea[:].unsqueeze(1).broadcast_to([P, TT, SSD_H]), ALU.mult, ALU.mult).then_inc(sg_dt.sem, 1)

                def dt_sums(_n):
                    wait(sg_dta, 5)
                    dve.tensor_tensor(dtd[:], dt[:, 0, :], ed[:, 1, :], ALU.mult).then_inc(sg_dt.sem, 1)

                def a_score(j):
                    for g in range(A_GROUPS):
                        wait(sg_as, 3 * j + g + 1)
                        if j >= 1 and g == 0:
                            wait(sg_at, 3 * j)
                        dve.scalar_tensor_tensor(a_p[:, g, :], dist[:, g, :], slopes[g * A_SLOTS + j], pm[:, g, 0:384], ALU.mult, ALU.add).then_inc(sg_ab.sem, 1)
                    wait(sg_ab, 3 * j + 3)
                    dve.tensor_reduce(stat[:, 4:5], a_p[:, :, 0:P], AX.XY, ALU.max, negate=True)
                    dve.tensor_reduce(stat[:, 5:6], a_p[:, :, P:3 * P], AX.XY, ALU.max, negate=True).then_inc(sg_am.sem, 1)
                    wait(sg_ae, j + 1)
                    dve.reciprocal(stat[:, 14:16], stat[:, 6:8]).then_inc(sg_ar.sem, 1)
                    wait(sg_ar, 2 * j + 1)
                    dve.tensor_scalar(a_p[:, :, 0:P], a_p[:, :, 0:P], stat[:, 14:15], None, ALU.mult)
                    dve.tensor_scalar(a_p[:, :, P:3 * P], a_p[:, :, P:3 * P], stat[:, 15:16], None, ALU.mult).then_inc(sg_ar.sem, 1)

                def c_score(p):
                    for i in range(2):
                        wait(sg_cl, 6 * p + i + 5)
                        dve.scalar_tensor_tensor(c_sp[:, i, :], pm[:, i, 0:384], 0.0, c_sp[:, i, :], ALU.max, ALU.add).then_inc(sg_csp.sem, 1)

                def c_mix(p):
                    if p == 0:
                        wait(sg_apv, 6)
                        dve.tensor_copy(upper_r[:], upper).then_inc(sg_da.sem, 1)
                        dve.tensor_copy(da_hi[:], da[:]).then_inc(sg_da.sem, 1)
                        wait(sg_da, 2)
                        dve.tensor_tensor(da_lo[:], da[:], da_hi[:].bitcast(F32), ALU.subtract).then_inc(sg_da.sem, 1)
                    wait(sg_cpv, p + 1)
                    dve.tensor_copy(yt[:, 3 + p, :], pm[:, 2, 0:SEQ]).then_inc(sg_cy.sem, 1)

                def scan_steps(n):
                    g, t = n // 2, n % 2
                    if n == 0:
                        wait(sg_cy, 9)
                    else:
                        wait(sg_sgm, n)
                    dve.tensor_tensor(s_rh[:], da_hi[:, t, HPG * g:HPG * (g + 1)].bitcast(F32).unsqueeze(2).broadcast_to([P, HPG, P]),
                                      lower.unsqueeze(1).broadcast_to([P, HPG, P]), ALU.mult).then_inc(sg_sr.sem, 1)

                def per_head(row):
                    return row.unsqueeze(2).broadcast_to([P, HPG, HD])

                def ssd(n):
                    if n == 0:
                        scan_steps(0)
                    if n < 2 * GROUPS:
                        g, t = n // 2, n % 2
                        hs = slice(HPG * g, HPG * (g + 1))
                        xs = pm[:, t, 0:256].rearrange("p (h d) -> p h d", h=HPG)
                        wait(sg_s1, n + 1)
                        if t == 0:
                            wait(sg_sb, g + 1)
                        if n:
                            wait(sg_sm, n)
                        dve.tensor_tensor(s_cb[:], pm[:, t, 256:384], lower, ALU.mult).then_inc(sg_sc.sem, 1)
                        if n >= 2:
                            wait(sg_s2, n - 1)
                            wait(sg_sd, final_of(n - 2))
                        dve.tensor_tensor(s_xdt[:, t], xs, per_head(dt[:, t, hs]), ALU.mult)
                        if t == 0:
                            dve.tensor_tensor(s_xdd[:], xs, per_head(dtd[:, hs]), ALU.mult)
                        dve.tensor_tensor(s_y[:, t], xs, per_head(rows[:, 64 + HPG * g:64 + HPG * (g + 1)]), ALU.mult).then_inc(sg_sx.sem, 1)
                        wait(sg_sc, n + 1)
                        wait(sg_se, n + 1)
                        dve.tensor_tensor(s_e[:, t], s_e[:, t], s_cb[:].unsqueeze(1).broadcast_to([P, HPG, P]), ALU.mult).then_inc(sg_sm.sem, 1)
                    if n >= 1:
                        m = n - 1
                        g, t = m // 2, m % 2
                        done = final_of(m - 1) if m else 0
                        heads = slice(HPG * HD * g, HPG * HD * (g + 1))
                        wait(sg_s2, m + 1)
                        wait(sg_st, g + 1)
                        y = s_y[:, t]
                        dve.tensor_tensor(y, y, pm[:, 3, 0:256].rearrange("p (h d) -> p h d", h=HPG), ALU.add).then_inc(sg_sd.sem, 1)
                        if t == 1:
                            off = s_xdt[:, 1]
                            dve.tensor_tensor(off, pm[:, 3, 256:512].rearrange("p (h d) -> p h d", h=HPG),
                                              per_head(ed[:, 0, HPG * g:HPG * (g + 1)]), ALU.mult).then_inc(sg_sd.sem, 1)
                            wait(sg_sd, done + 2)
                            dve.tensor_tensor(y, y, off, ALU.add).then_inc(sg_sd.sem, 1)
                        wait(sg_sd, final_of(m) - 1)
                        zg = z[:, t, heads]
                        dve.tensor_tensor(zg, zg, y.rearrange("p h d -> p (h d)"), ALU.mult).then_inc(sg_sd.sem, 1)
                    if n + 1 < 2 * GROUPS:
                        scan_steps(n + 1)

                def split_y(i):
                    wait(sg_yh, i + 1)
                    dve.tensor_tensor(yt_lo[:, 4 * i:4 * i + 4, :], yt[:, 4 * i:4 * i + 4, :], yt_hi[:, 4 * i:4 * i + 4, :].bitcast(F32), ALU.subtract).then_inc(sg_yl.sem, 1)

                def merge(n):
                    branch = (2, 0, 2, 0, 1, 1)[n]
                    half = (0, 0, 1, 1, 0, 1)[n]
                    pair = (0, 1, 0, 1, 0, 1)[n]
                    if branch == 2:
                        wait(sg_cd, half + 1)
                    elif branch == 0:
                        wait(sg_used, U_C + (6, 12)[half])
                    else:
                        wait(sg_used, U_B + 8 * half + 8)
                        if half == 0:
                            wait(sg_br, 1)
                    if n:
                        wait(sg_mt, merges(n - 1))
                    part = slice(CW * half, CW * (half + 1))
                    for t in range(TT):
                        gate = gates[:, t, D * branch + CW * half:D * branch + CW * (half + 1)]
                        dst = merged[:, t, part] if branch == 2 else mtmp[:, t, :]
                        if branch == 1:
                            ins = dve.scalar_tensor_tensor(dst, pp[:, 2 * pair + t, :], stat[:, 16 + t:17 + t], gate, ALU.mult, ALU.mult)
                        else:
                            ins = dve.tensor_tensor(dst, pp[:, 2 * pair + t, :], gate, ALU.mult)
                        ins.then_inc(sg_mt.sem, 1)
                    if branch != 2:
                        for t in range(TT):
                            wait(sg_mt, merges(n - 1) + 1 + t)
                            dve.tensor_tensor(merged[:, t, part], merged[:, t, part], mtmp[:, t, :], ALU.add).then_inc(sg_mt.sem, 1)

                def ssd_norm(_n):
                    wait(sg_bq, 3)
                    dve.reciprocal(stat[:, 16:18], stat[:, 10:12]).then_inc(sg_br.sem, 1)

                def turn_b(k):
                    wait(sg_bh, k + 1)
                    dve.scalar_tensor_tensor(yb_lo[:, k, :], pm[:, k % 4, 0:SEQ],
                                             fmp[:, bass.ds(l, 1), 176 + k], yb_hi[:, k, :].bitcast(F32), ALU.mult, ALU.subtract).then_inc(sg_bl.sem, 1)

                def turn_merged(h):
                    for k in range(4 * h, 4 * h + 4):
                        wait(sg_mh, k // 2 * 2 + 2)
                        dve.tensor_tensor(m_lo[:, k, :], pm[:, k // 2, SEQ * (k % 2):SEQ * (k % 2 + 1)], m_hi[:, k, :].bitcast(F32), ALU.subtract).then_inc(sg_ml.sem, 1)

                made = [0]

                def after(n):
                    dve.wait_ge(sg_tk.sem, sg_tk.at(l, n))
                    dve.sem_inc(s_apart)

                def step(ins):
                    made[0] += 1
                    ins.then_inc(sg_tk.sem, 1)
                    return made[0]

                def top16(rows_of_four):
                    firsts = [step(dve.max(val[:, 0:8], values)) for values, _, val, _ in rows_of_four]
                    seconds = []
                    for i, (values, scratch, val, _) in enumerate(rows_of_four):
                        if i % 2 == 0:
                            after(firsts[i + 1])
                        seconds.append(step(dve.match_replace(scratch, val[:, 0:8], values, NEG)))
                    thirds = []
                    for i, (_, scratch, val, _) in enumerate(rows_of_four):
                        if i % 2 == 0:
                            after(seconds[i + 1])
                        thirds.append(step(dve.max(val[:, 8:16], scratch)))
                    for values, _, val, idx in rows_of_four:
                        step(dve.max_index(idx[:, 0:8], val[:, 0:8], values))
                    after(thirds[-1])
                    for _, scratch, val, idx in rows_of_four:
                        step(dve.max_index(idx[:, 8:16], val[:, 8:16], scratch))

                def top_keys(n):
                    t = n % 2
                    wait(sg_kv, n + 1)
                    dve.sem_inc(s_apart)
                    sets = range(4 * (n // 2), 4 * (n // 2) + 4)
                    top16([(sc[:, t, hc, :], tkt[:, hc % 4, 0:KEYS], t_val[:, t, hc // 2, hc % 2], t_idx[:, t, hc // 2, hc % 2]) for hc in sets])

                steps = {"evacuate": evacuate, "dt": dt_vector, "dt_sums": dt_sums, "a_score": a_score, "c_score": c_score, "c_mix": c_mix,
                         "ssd": ssd, "split_y": split_y, "merge": merge, "ssd_norm": ssd_norm, "turn_b": turn_b,
                         "turn_merged": turn_merged, "top_keys": top_keys}

                norm(0)
                for u in range(U_E):
                    for name, arg in ORDER[u]:
                        if name in steps and name in URGENT:
                            steps[name](arg)
                    if u + RING < LOW_POOL and not U_O + 4 <= u < U_Q:
                        low(u + RING)
                    for name, arg in ORDER[u]:
                        if name in steps and name not in URGENT:
                            steps[name](arg)
                    if u == U_Q - 1:
                        norm(1)

                for i in range(6, 8):
                    top_keys(i)
                after(made[0])
                step(dve.tensor_copy(t_idf[:], t_idx[:]))
                grid = [P, RH, TOPK, TOPK]
                for t in range(TT):
                    n = step(dve.tensor_tensor(cand[:, t], t_val[:, t, :, 0, :].unsqueeze(3).broadcast_to(grid),
                                               t_val[:, t, :, 1, :].unsqueeze(2).broadcast_to(grid), ALU.add))
                for t in range(TT):
                    if t == 0:
                        after(n)
                    for h in range(0, RH, 4):
                        top16([(cand[:, t, h + i].rearrange("p a b -> p (a b)"), tkt[:, i, :], b_val[:, t, h + i], b_pos[:, t, h + i]) for i in range(4)])
                after(made[0])
                step(dve.tensor_scalar(b_row[:, 0], b_pos[:], 4, None, ALU.logical_shift_right))
                step(dve.tensor_scalar(b_row[:, 1], b_pos[:], 15, None, ALU.bitwise_and))
                flat = [P, TT * RH, TOPK]
                bv = b_val[:].rearrange("p t h k -> p (t h) k")
                pg = pick[:, 2].rearrange("p t h k -> p (t h) k")
                n = step(dve.tensor_tensor(pg, bv, bv[:, :, 0:1].broadcast_to(flat), ALU.subtract))
                assert n == n_tk - 12 - 4
                after(n - 1)
                n = step(dve.tensor_copy(b_rof[:], b_row[:]))
                after(n)
                for c in range(2):
                    for t in range(TT):
                        if c:
                            after(made[0] - 1)
                        step(dve.tensor_tensor(cand[:, t], b_rof[:, c, t].unsqueeze(3).broadcast_to(grid),
                                               iota[:, 0:TOPK].unsqueeze(1).unsqueeze(1).broadcast_to(grid), ALU.is_equal))
                    for t in range(TT):
                        after(made[0] - 1)
                        step(dve.tensor_tensor(cand[:, t], cand[:, t], t_idf[:, t, :, c, :].unsqueeze(2).broadcast_to(grid), ALU.mult))
                    for t in range(TT):
                        after(made[0] - 1)
                        step(dve.tensor_reduce(pick[:, c, t], cand[:, t], AX.X, ALU.add))
                wait(sg_gx, 1)
                n = step(dve.tensor_reduce(stat[:, 20:36], pg, AX.X, ALU.add))
                after(n)
                n = step(dve.reciprocal(stat[:, 36:52], stat[:, 20:36]))
                after(n)
                n = step(dve.tensor_tensor(pg, pg, stat[:, 36:52].unsqueeze(2).broadcast_to(flat), ALU.mult))
                assert n == n_tk, (n, n_tk)
                wait(sg_ix, 1)
                dve.tensor_copy(gate_t[:, 0, :], pm[:, 3, 0:SEQ]).then_inc(sg_ixe.sem, 1)
                dve.tensor_copy(place_t[:].rearrange("p a t -> p (a t)"), pm[:, 2, :]).then_inc(sg_ixe.sem, 1)
                dve.tensor_copy(iota_b[:], iota[:]).then_inc(sg_ixe.sem, 1)
                for part in range(3):
                    wait(sg_ixe, 1 if part == 0 else 3 + 2 * part)
                    dve.tensor_copy(gate_p[:, part, :], gate_t[:, part, :]).then_inc(sg_ixe.sem, 1)
                    if part < 2:
                        wait(sg_ixe, 4 + 2 * part)
                        dve.tensor_tensor(gate_t[:, part + 1, :], gate_t[:, part, :], gate_p[:, part, :], ALU.subtract).then_inc(sg_ixe.sem, 1)
                wait(sg_ixe, 8)
                wait(sg_xj, 1)
                dve.sem_inc(s_apart)

                def one_hots(half, n, buf):
                    dve.wait_ge(sg_rt.sem, sg_rt.at(l, n + (BATCHES * half - 1)))
                    tok = bass.ds(HOT * n, HOT)
                    ks = iota_b[:, FIRST * half:FIRST * (half + 1)]
                    cols = [P, 3, HOT, FIRST]

                    def each(row, width):
                        return row.unsqueeze(2).broadcast_to([P, HOT, width])

                    dve.tensor_tensor(hot_e[:, buf], ks.unsqueeze(1).broadcast_to([P, HOT, FIRST]), each(place_t[:, 1, tok], FIRST), ALU.is_equal).then_inc(sg_hc.sem, 1)
                    dve.tensor_tensor(hot_r[:, buf], iota_b[:].unsqueeze(1).broadcast_to([P, HOT, KEYS]), each(place_t[:, 0, tok], KEYS), ALU.is_equal)
                    dve.wait_ge(sg_hc.sem, sg_hc.at(l, n + (BATCHES * half + 1)))
                    dve.tensor_tensor(hot_c[:, buf], hot_e[:, buf].unsqueeze(1).broadcast_to(cols), gate_p[:, :, tok].unsqueeze(3).broadcast_to(cols), ALU.mult).then_inc(sg_hot.sem, 1)

                with dve.Fori(0, BATCHES // 4) as i:
                    for r in range(4):
                        one_hots(0, 4 * i + r, r % 2)

                def weigh_four(n):
                    cols = bass.ds(4 * n, 4)
                    dve.wait_ge(sg_ge.sem, sg_ge.at(l, 4 * n + 4))
                    dve.tensor_tensor(hid[:, cols, :].rearrange("p a t -> p (a t)"), hid[:, cols, :].rearrange("p a t -> p (a t)"),
                                      route[:, cols, :].rearrange("p a t -> p (a t)"), ALU.mult).then_inc(sg_wm.sem, 1)

                def hidden_low(i, r):
                    dve.wait_ge(sg_gh.sem, sg_gh.at(l, RING * i + (r + 1)))
                    dve.tensor_tensor(g_lo[:, r % 2, :], hid[:, bass.ds(RING * i + r, 1), :].rearrange("p o t -> p (o t)"),
                                      g_hi[:, r % 2, :].bitcast(F32), ALU.subtract).then_inc(sg_gw.sem, 1)

                wait(sg_free, GROUPS_OF_ROUTES)
                dve.sem_inc(s_apart)
                with dve.Fori(0, ROUTES_FROM // RING) as i:
                    for r in range(RING):
                        weigh_four(RING * i + r)
                        hidden_low(i, r)
                with dve.Fori(0, BATCHES // 16) as i:
                    for r in range(12):
                        ahead, midway = batches_of_up(r)
                        for b in ahead:
                            one_hots(1, 16 * i + b, b % 2)
                        hidden_low(*ring_turn(i, r))
                        one_hots(1, 16 * i + midway, midway % 2)

                def weigh(j, buf):
                    dve.wait_ge(sg_ge.sem, sg_ge.at(l, j + (FIRST + 1)))
                    g = g_act[:, buf, :]
                    dve.tensor_tensor(g, g, route[:, bass.ds(j, 1), :].rearrange("p o t -> p (o t)"), ALU.mult).then_inc(sg_gl.sem, 1)
                    dve.wait_ge(sg_gl.sem, sg_gl.at(l, 3 * j + 1))
                    dve.tensor_copy(g_hi[:, buf, :], g).then_inc(sg_gl.sem, 1)
                    dve.wait_ge(sg_gl.sem, sg_gl.at(l, 3 * j + 2))
                    dve.tensor_tensor(g_lo[:, buf, :], g, g_hi[:, buf, :].bitcast(F32), ALU.subtract).then_inc(sg_gl.sem, 1)

                def expert_low(v, i=0):
                    s = v % RING
                    dve.wait_ge(sg_hi.sem, sg_hi.at(l, RING * i + (v + 1)))
                    dve.tensor_tensor(w_lo[:, s, :], raw[:, s, :], w_hi[:, s, :].bitcast(F32), ALU.subtract).then_inc(sg_lo[s].sem, 1)

                wait(sg_free, 2 * GROUPS_OF_ROUTES)
                weigh(0, 0)
                expert_low(U_S + 4)
                weigh(1, 1)
                expert_low(U_S + 5)
                expert_low(U_S + 6)
                with dve.Fori(1, FIRST // 2 - 1) as i:
                    for r in range(2):
                        weigh(2 * i + r, r)
                        expert_low(U_S + 2 * r + 3, i)
                        expert_low(U_S + 2 * r + 4, i)
                weigh(FIRST - 2, 0)
                expert_low(U_S + 2 * FIRST - 1)
                weigh(FIRST - 1, 1)
                add_x(1, 0)
                add_x(1, 1)
            dve.wait_ge(s_fg, 16)
            for t in range(TT):
                dve.wait_ge(s_fina, 2 * t + 2)
                dve.reciprocal(stat[:, 12 + t:13 + t], stat[:, 2 + t:3 + t]).then_inc(s_fin, 1)
                dve.wait_ge(s_fin, 2 * t + 1)
                dve.scalar_tensor_tensor(xn[:, t, :], x[:, t, :], stat[:, 12 + t:13 + t], fing[:], ALU.mult, ALU.mult).then_inc(s_fin, 1)


def lay_out_chunks(w):
    layers, rows, cols = w.shape
    m, n = rows // (2 * P), cols // CW
    w = w.reshape(layers, m, 2, P, n, CW).transpose(0, 4, 1, 3, 2, 5)
    return w.reshape(layers, m * n, P, 1024)


def lay_out_stream(w_in, w_a, w_b, w_c, w_out, w_query, down, up):
    widths = (A_W, A_W, A_W, C_W, C_W, C_W, SSD_IN, CONV, SSD_H, 3 * D)
    edges = np.concatenate([[0], np.cumsum(widths)])
    qa, ka, va, qc, kc, vc, zz, xbc, dtw, gl = (w_in[:, :, a:b] for a, b in zip(edges[:-1], edges[1:]))
    pad = np.zeros((LAYERS, D, V_CH * CW - V_COLS), w_in.dtype)
    w = np.concatenate([va, vc, dtw, pad, qa, ka, qc, kc, xbc, zz, gl], axis=2)
    stream = np.empty((LAYERS, UNITS, P, 1024), w_in.dtype)
    stream[:, 0:U_C] = lay_out_chunks(w)
    stream[:, U_C:U_B] = lay_out_chunks(np.concatenate([w_c, w_a], axis=1))
    stream[:, U_B:U_O] = lay_out_chunks(w_b)
    stream[:, U_O:U_O + 4] = lay_out_chunks(w_out[:, :CW])
    stream[:, U_O + 4:U_Q] = lay_out_chunks(w_out[:, CW:])
    stream[:, U_Q:U_E] = lay_out_chunks(w_query)
    downs = down.reshape(LAYERS, KEYS, KEYS, KD, P).transpose(0, 2, 4, 3, 1).reshape(LAYERS, KEYS, P, 1024)
    ups = up.reshape(LAYERS, KEYS, KEYS, D).transpose(0, 2, 1, 3)
    stream[:, U_E:U_U] = downs[:, :FIRST]
    stream[:, U_U:U_S] = ups[:, :FIRST]
    others = stream[:, U_S:]
    others[:, 0] = downs[:, FIRST]
    others[:, 1:2 * FIRST - 2:2] = downs[:, FIRST + 1:]
    others[:, 2:2 * FIRST - 1:2] = ups[:, FIRST:KEYS - 1]
    others[:, 2 * FIRST - 1] = ups[:, KEYS - 1]
    return stream.reshape(LAYERS * UNITS, P, 1024)


def mixer_constants():
    a, b = np.arange(P)[:, None], np.arange(P)[None, :]
    upper = (a > b).astype(np.float32)
    lower = (a <= b).astype(np.float32)
    neg_ge = -(a >= b).astype(np.float32)
    neg_one = -np.ones((P, P), np.float32)
    dists = []
    for d in DILATION:
        for t0, s0 in ((0, 0), (P, 0), (P, P)):
            diff = (t0 + a) - (s0 + b)
            ok = (diff >= 0) & (diff % d == 0) & (diff <= P * d)
            dists.append(np.where(ok, -diff, -1e30).astype(np.float32))
    f32 = np.concatenate([upper, lower, neg_ge, neg_one, *dists], axis=1)
    mask = np.where(a >= b, -1e30, 0.0).astype(np.float32)
    bf = np.concatenate([mask, np.eye(P, dtype=np.float32)], axis=1)
    return np.ascontiguousarray(f32), bf


def kernel(x, norm_mix_g, w_in, conv_w, conv_b, dt_bias, a_log, d_skip, ssd_norm_g, w_branch_a, w_branch_b,
           w_branch_c, w_out, norm_ffn_g, peer_w_query, peer_sub_keys, peer_down, peer_up, final_norm_g):
    import ml_dtypes
    import concourse.bacc as bacc
    from concourse.bass_utils import run_bass_kernel_spmd as run

    def fm(a, tiles):
        return np.asarray(a).reshape(LAYERS, tiles, P).transpose(0, 2, 1)

    x, final_norm_g = np.asarray(x), np.asarray(final_norm_g)
    stream = lay_out_stream(*(np.asarray(a) for a in (w_in, w_branch_a, w_branch_b, w_branch_c, w_out, peer_w_query,
                                                      peer_down, peer_up)))
    taps = np.asarray(conv_w).reshape(LAYERS, 4, 32, P).transpose(0, 3, 2, 1).reshape(LAYERS, P, 128)
    fm_params = np.concatenate([fm(norm_mix_g, 8), fm(norm_ffn_g, 8), taps, fm(conv_b, 32), fm(ssd_norm_g, 16)], axis=2)
    row = np.concatenate([np.asarray(a) for a in (dt_bias, a_log, d_skip)], axis=1)
    row_params = np.broadcast_to(row[:, None, :], (LAYERS, P, 96))
    mix_f32, mix_bf16 = mixer_constants()
    arrays = {
        "x_in": x.reshape(SEQ, D),
        "stream": stream,
        "sub_keys": np.asarray(peer_sub_keys).reshape(LAYERS, 16, KEYS, P).transpose(0, 3, 1, 2),
        "fm_params": fm_params,
        "row_params": row_params,
        "mix_f32": mix_f32,
        "mix_bf16": mix_bf16.astype(ml_dtypes.bfloat16),
        "ident_in": np.eye(P, dtype=np.float32),
        "iota_in": np.broadcast_to(np.arange(P, dtype=np.float32), (P, P)),
        "final_g": np.broadcast_to(final_norm_g, (P, D)),
    }
    arrays = {k: np.ascontiguousarray(a) for k, a in arrays.items()}
    nc = bacc.Bacc("TRN2", target_bir_lowering=False, num_devices=1)
    args = [nc.dram_tensor(n, a.shape, mybir.dt.from_np(a.dtype), kind="ExternalInput").ap() for n, a in arrays.items()]
    args.append(nc.dram_tensor("trunk_out", (SEQ, D), F32, kind="ExternalOutput").ap())
    build_trunk(nc, *args)
    result = run(nc, [arrays], core_ids=[0])
    return result.results[0]["trunk_out"].reshape(1, SEQ, D)
```
